# Optimizing a Trainium2 kernel written in Bass

```python
import math
import jax, jax.numpy as jnp
from jax import lax
import numpy as np

D_MODEL = 1024
BATCH = 1
SEQ = 512
DEPTH = 1
DEC_BATCH = 1
DEC_SEQ = 1024
PAST_LEN = 128

HEAD_DIM = 64
N_ATTN_HEADS = 8
ATTN_WIDTH = N_ATTN_HEADS * HEAD_DIM
ROT_DIM = HEAD_DIM // 4
ROPE_THETA = 500000.0
DILATED_PATTERNS = ((128, 1), (512, 4), (2048, 16))
N_SSM_HEADS = 8
SSM_HEAD_DIM = 64
SSM_WIDTH = N_SSM_HEADS * SSM_HEAD_DIM
SSM_GROUPS = 2
D_STATE = 128
CONV_K = 5
CHUNK = 128
CONV_CH = SSM_WIDTH + 2 * SSM_GROUPS * D_STATE
MIX_WIDTH = ATTN_WIDTH + SSM_WIDTH
IN_SIZES = (ATTN_WIDTH, ATTN_WIDTH, ATTN_WIDTH, SSM_WIDTH, SSM_WIDTH,
            SSM_GROUPS * D_STATE, SSM_GROUPS * D_STATE, N_SSM_HEADS, N_SSM_HEADS)
IN_WIDTH = 3 * ATTN_WIDTH + 2 * SSM_WIDTH + 2 * SSM_GROUPS * D_STATE + 2 * N_SSM_HEADS
N_EXPERTS = 16
CAPACITY_FACTOR = 2
D_FF_EXPERT = 2816
ALPHA = (2.0 * DEPTH) ** 0.25
BETA = (8.0 * DEPTH) ** -0.25
LN_EPS = 1e-5
RMS_EPS = 1e-5

kernel_name = 'hybrid_dilated_attn_ssd_ec_moe_encoder'

def layer_norm(x, g, b):
    xf = x.astype(jnp.float32)
    mu = jnp.mean(xf, axis=-1, keepdims=True)
    var = jnp.mean(jnp.square(xf - mu), axis=-1, keepdims=True)
    return ((xf - mu) * lax.rsqrt(var + LN_EPS) * g.astype(jnp.float32) + b.astype(jnp.float32)).astype(x.dtype)

def partial_rotary(t, pos):
    half = ROT_DIM // 2
    inv = ROPE_THETA ** (-jnp.arange(half, dtype=jnp.float32) * 2.0 / ROT_DIM)
    ang = pos.astype(jnp.float32)[:, None] * inv[None, :]
    cos = jnp.cos(ang)[None, :, None, :].astype(t.dtype)
    sin = jnp.sin(ang)[None, :, None, :].astype(t.dtype)
    t1 = t[..., :half]
    t2 = t[..., half:ROT_DIM]
    return jnp.concatenate([t1 * cos - t2 * sin, t2 * cos + t1 * sin, t[..., ROT_DIM:]], axis=-1)

def dilated_window_attention(q, k, v, window, dil):
    b, s, h, e = q.shape
    half = window // (2 * dil)
    L = s // dil
    nb = -(-L // half)
    Lp = nb * half

    def to_sub(t):
        t = t.reshape(b, L, dil, h, e).transpose(0, 2, 1, 3, 4)
        t = jnp.pad(t, ((0, 0), (0, 0), (0, Lp - L), (0, 0), (0, 0)))
        return t.reshape(b, dil, nb, half, h, e)

    def band(t):
        tp = jnp.pad(t, ((0, 0), (0, 0), (1, 1), (0, 0), (0, 0), (0, 0)))
        return jnp.concatenate([tp[:, :, :-2], tp[:, :, 1:-1], tp[:, :, 2:]], axis=3)

    qs = to_sub(q)
    kb = band(to_sub(k))
    vb = band(to_sub(v))
    qpos = jnp.arange(nb)[:, None] * half + jnp.arange(half)[None, :]
    kpos = (jnp.arange(nb)[:, None] - 1) * half + jnp.arange(3 * half)[None, :]
    mask = ((jnp.abs(qpos[:, :, None] - kpos[:, None, :]) <= half)
            & (kpos[:, None, :] >= 0) & (kpos[:, None, :] < L))
    scores = jnp.einsum('bdnqhe,bdnkhe->bdnhqk', qs, kb,
                        preferred_element_type=jnp.float32) * (e ** -0.5)
    scores = jnp.where(mask[None, None, :, None], scores, -jnp.inf)
    lse = jax.nn.logsumexp(scores, axis=-1)
    p = jnp.exp(scores - lse[..., None])
    o = jnp.einsum('bdnhqk,bdnkhe->bdnqhe', p, vb.astype(jnp.float32))
    o = o.reshape(b, dil, Lp, h, e)[:, :, :L].transpose(0, 2, 1, 3, 4).reshape(b, s, h, e)
    lse = lse.transpose(0, 1, 2, 4, 3).reshape(b, dil, Lp, h)[:, :, :L]
    lse = lse.transpose(0, 2, 1, 3).reshape(b, s, h)
    return o, lse

def centred_dwconv(u, w, bias):
    out = lax.conv_general_dilated(u, w[:, None, :].astype(u.dtype), window_strides=(1,),
                                   padding=[(CONV_K // 2, CONV_K // 2)],
                                   dimension_numbers=('NWC', 'WIO', 'NWC'),
                                   feature_group_count=u.shape[-1])
    return out + bias.astype(u.dtype)

def ssd_scan(x, dt, A, Bm, Cm):
    b, s, h, p = x.shape
    g = Bm.shape[2]
    r = h // g
    n = Bm.shape[3]
    nc = s // CHUNK
    xc = x.astype(jnp.float32).reshape(b, nc, CHUNK, g, r, p)
    dtc = dt.reshape(b, nc, CHUNK, g, r)
    Bc = Bm.astype(jnp.float32).reshape(b, nc, CHUNK, g, n)
    Cc = Cm.astype(jnp.float32).reshape(b, nc, CHUNK, g, n)
    a_cs = jnp.cumsum(dtc * A.reshape(g, r), axis=2)
    xdt = xc * dtc[..., None]
    diff = a_cs[:, :, :, None] - a_cs[:, :, None, :]
    tri = jnp.tril(jnp.ones((CHUNK, CHUNK), dtype=bool))[:, :, None, None]
    Lm = jnp.exp(jnp.where(tri, diff, -jnp.inf))
    cb = jnp.einsum('bclgn,bcsgn->bclsg', Cc, Bc)
    y_diag = jnp.einsum('bclsgr,bcsgrp->bclgrp', cb[..., None] * Lm, xdt)
    decay_to_end = jnp.exp(a_cs[:, :, -1:] - a_cs)
    states = jnp.einsum('bclgn,bclgr,bclgrp->bcgrpn', Bc, decay_to_end, xdt)
    chunk_decay = jnp.exp(a_cs[:, :, -1])

    def step(prev, inp):
        st, dec = inp
        return prev * dec[..., None, None] + st, prev

    init = jnp.zeros((b, g, r, p, n), jnp.float32)
    _, prev_states = lax.scan(step, init, (states.swapaxes(0, 1), chunk_decay.swapaxes(0, 1)))
    prev_states = prev_states.swapaxes(0, 1)
    y_off = jnp.einsum('bclgn,bcgrpn,bclgr->bclgrp', Cc, prev_states, jnp.exp(a_cs))
    return (y_diag + y_off).reshape(b, s, h, p)

def hybrid_mixer(x, w_in, conv_w, conv_b, dt_bias, a_log, d_skip, ssm_norm_w, w_out):
    b, s, _ = x.shape
    proj = x @ w_in
    cuts = []
    acc = 0
    for sz in IN_SIZES[:-1]:
        acc += sz
        cuts.append(acc)
    q, k, v, z, xs, Bs, Cs, dtf, dtb = jnp.split(proj, cuts, axis=-1)

    pos = jnp.arange(s)
    q = partial_rotary(q.reshape(b, s, N_ATTN_HEADS, HEAD_DIM), pos)
    k = partial_rotary(k.reshape(b, s, N_ATTN_HEADS, HEAD_DIM), pos)
    v = v.reshape(b, s, N_ATTN_HEADS, HEAD_DIM)
    outs = []
    lses = []
    for window, dil in DILATED_PATTERNS:
        o_i, l_i = dilated_window_attention(q, k, v, window, dil)
        outs.append(o_i)
        lses.append(l_i)
    wts = jax.nn.softmax(jnp.stack(lses, axis=0), axis=0)
    attn = jnp.sum(wts[..., None] * jnp.stack(outs, axis=0), axis=0)
    attn = attn.reshape(b, s, ATTN_WIDTH).astype(x.dtype)

    xBC = jax.nn.silu(centred_dwconv(jnp.concatenate([xs, Bs, Cs], axis=-1), conv_w, conv_b))
    xs, Bs, Cs = jnp.split(xBC, [SSM_WIDTH, SSM_WIDTH + SSM_GROUPS * D_STATE], axis=-1)
    xh = xs.reshape(b, s, N_SSM_HEADS, SSM_HEAD_DIM)
    Bg = Bs.reshape(b, s, SSM_GROUPS, D_STATE)
    Cg = Cs.reshape(b, s, SSM_GROUPS, D_STATE)
    dtb32 = dt_bias.astype(jnp.float32)
    dt_f = jax.nn.softplus(dtf.astype(jnp.float32) + dtb32[0])
    dt_b = jax.nn.softplus(dtb.astype(jnp.float32) + dtb32[1])
    A = -jnp.exp(a_log.astype(jnp.float32))
    rev = lambda t: jnp.flip(t, axis=1)
    y_f = ssd_scan(xh, dt_f, A[0], Bg, Cg)
    y_b = rev(ssd_scan(rev(xh), rev(dt_b), A[1], rev(Bg), rev(Cg)))
    y = y_f + y_b + d_skip.astype(jnp.float32)[:, None] * xh.astype(jnp.float32)
    y = y.reshape(b, s, SSM_WIDTH) * jax.nn.silu(z.astype(jnp.float32))
    y = y * lax.rsqrt(jnp.mean(jnp.square(y), axis=-1, keepdims=True) + RMS_EPS) * ssm_norm_w.astype(jnp.float32)

    return jnp.concatenate([attn, y.astype(x.dtype)], axis=-1) @ w_out

def expert_choice_ffn(x, w_router, w_gate, w_up, w_down):
    b, s, d = x.shape
    T = b * s
    cap = CAPACITY_FACTOR * T // N_EXPERTS
    h = x.reshape(T, d)
    aff = jax.nn.softmax((h @ w_router).astype(jnp.float32), axis=-1)
    gate_vals, tok_idx = lax.top_k(aff.T, cap)
    xg = h[tok_idx]
    hid = jax.nn.silu(jnp.einsum('ecd,edf->ecf', xg, w_gate)) * jnp.einsum('ecd,edf->ecf', xg, w_up)
    out = jnp.einsum('ecf,efd->ecd', hid, w_down) * gate_vals[..., None].astype(x.dtype)
    y = jnp.zeros_like(h).at[tok_idx.reshape(-1)].add(out.reshape(-1, d))
    return y.reshape(b, s, d)

def setup_inputs(seed: int = 0) -> dict:
    key = jax.random.key(seed)
    ks = jax.random.split(key, 20)
    f32 = jnp.float32
    x_prompt = jax.random.normal(ks[0], (BATCH, SEQ, D_MODEL), f32)
    x_sample = jax.random.normal(ks[1], (DEC_BATCH, DEC_SEQ, D_MODEL), f32)
    w_in = jax.random.normal(ks[2], (DEPTH, D_MODEL, IN_WIDTH), f32) * D_MODEL ** -0.5
    conv_w = jax.random.normal(ks[3], (DEPTH, CONV_K, CONV_CH), f32) * CONV_K ** -0.5
    conv_b = 0.02 * jax.random.normal(ks[4], (DEPTH, CONV_CH), f32)
    u = jax.random.uniform(ks[5], (DEPTH, 2, N_SSM_HEADS), f32)
    dt0 = jnp.exp(u * (math.log(0.1) - math.log(1e-3)) + math.log(1e-3))
    dt_bias = dt0 + jnp.log(-jnp.expm1(-dt0))
    a_log = jnp.log(jax.random.uniform(ks[6], (DEPTH, 2, N_SSM_HEADS), f32, minval=1.0, maxval=16.0))
    d_skip = 1.0 + 0.1 * jax.random.normal(ks[7], (DEPTH, N_SSM_HEADS), f32)
    ssm_norm_w = 1.0 + 0.1 * jax.random.normal(ks[8], (DEPTH, SSM_WIDTH), f32)
    w_out = jax.random.normal(ks[9], (DEPTH, MIX_WIDTH, D_MODEL), f32) * (MIX_WIDTH ** -0.5) * BETA
    ln1_g = 1.0 + 0.1 * jax.random.normal(ks[10], (DEPTH, D_MODEL), f32)
    ln1_b = 0.02 * jax.random.normal(ks[11], (DEPTH, D_MODEL), f32)
    w_router = jax.random.normal(ks[12], (DEPTH, D_MODEL, N_EXPERTS), f32) * D_MODEL ** -0.5
    w_gate = jax.random.normal(ks[13], (DEPTH, N_EXPERTS, D_MODEL, D_FF_EXPERT), f32) * D_MODEL ** -0.5
    w_up = jax.random.normal(ks[14], (DEPTH, N_EXPERTS, D_MODEL, D_FF_EXPERT), f32) * D_MODEL ** -0.5
    w_down = jax.random.normal(ks[15], (DEPTH, N_EXPERTS, D_FF_EXPERT, D_MODEL), f32) * (D_FF_EXPERT ** -0.5) * BETA
    ln2_g = 1.0 + 0.1 * jax.random.normal(ks[16], (DEPTH, D_MODEL), f32)
    ln2_b = 0.02 * jax.random.normal(ks[17], (DEPTH, D_MODEL), f32)
    return {'x_prompt': x_prompt, 'x_sample': x_sample, 'w_in': w_in, 'conv_w': conv_w,
            'conv_b': conv_b, 'dt_bias': dt_bias, 'a_log': a_log, 'd_skip': d_skip,
            'ssm_norm_w': ssm_norm_w, 'w_out': w_out, 'ln1_g': ln1_g, 'ln1_b': ln1_b,
            'w_router': w_router, 'w_gate': w_gate, 'w_up': w_up, 'w_down': w_down,
            'ln2_g': ln2_g, 'ln2_b': ln2_b}

def reference(x_prompt, x_sample, w_in, conv_w, conv_b, dt_bias, a_log, d_skip, ssm_norm_w,
              w_out, ln1_g, ln1_b, w_router, w_gate, w_up, w_down, ln2_g, ln2_b):
    def trunk(x):
        for l in range(DEPTH):
            mix = hybrid_mixer(x, w_in[l], conv_w[l], conv_b[l], dt_bias[l], a_log[l],
                               d_skip[l], ssm_norm_w[l], w_out[l])
            x = layer_norm(ALPHA * x + mix, ln1_g[l], ln1_b[l])
            ffn = expert_choice_ffn(x, w_router[l], w_gate[l], w_up[l], w_down[l])
            x = layer_norm(ALPHA * x + ffn, ln2_g[l], ln2_b[l])
        return x

    y_prompt = trunk(x_prompt)
    y_sample = trunk(x_sample)
    return (y_prompt, y_sample)


_drawn_inputs = setup_inputs


def setup_inputs(seed=0):
    import zlib

    import numpy as np

    out = dict(_drawn_inputs(seed))
    spreads = {}
    factors = {'conv_b': 4.724, 'd_skip': 3.142, 'ln1_b': 2.803, 'ln2_b': 2.899}
    for name, (base, spread) in spreads.items():
        noise = np.random.default_rng([zlib.crc32(name.encode()), seed]).standard_normal(out[name].shape)
        drawn = base * np.exp(spread * noise) if base else spread * noise
        out[name] = __import__('jax').numpy.asarray(drawn.astype(out[name].dtype))
    for name, factor in factors.items():
        out[name] = (out[name] * factor).astype(out[name].dtype)
    return out
```

```python
from contextlib import ExitStack

import numpy as np
import concourse.bass as bass
from concourse import mybir

F32 = mybir.dt.float32
U32 = mybir.dt.uint32
ALU = mybir.AluOpType
ACT = mybir.ActivationFunctionType

P = 128
SEQS = (512, 1024)
TOK = sum(SEQS)
NT = TOK // P
FIRST_TILE = (0, SEQS[0] // P)
D = 1024
KD = D // P
HEADS, HD = 8, 64
AW = HEADS * HD
ROT = HD // 4
HALF_ROT = ROT // 2
GROUPS, STATE = 2, 128
SSM_W = 512
CONV_CH = SSM_W + 2 * GROUPS * STATE
NCH = CONV_CH // P
CONV_K = 5
NDT = 16
TM_W = 4 * 512 + NDT
EXPERTS = 16
CAPS = tuple(2 * s // EXPERTS for s in SEQS)
CAP = sum(CAPS)
FF = 2816
FCH = FF // P
LN_EPS = 1e-5
RMS_EPS = 1e-5
ALPHA = 2.0 ** 0.25
PATTERNS = ((128, 1), (512, 4), (2048, 16))
MASK_W = 2 * SEQS[1] - P
MASK_0 = SEQS[1] - P
NEG = -1.0e30


class Mem:

    def __init__(self, nc, ctx, tag):
        self.nc, self.ctx, self.tag = nc, ctx, tag

    def sb(self, name, shape, dt=F32):
        return self.ctx.enter_context(self.nc.sbuf_tensor(f"{self.tag}_{name}", shape, dt))

    def ps(self, name, shape, dt=F32):
        return self.ctx.enter_context(self.nc.psum_tensor(f"{self.tag}_{name}", shape, dt))

    def sem(self, name):
        return self.ctx.enter_context(self.nc.semaphore(f"{self.tag}_{name}"))

    def sems(self, name, n=2):
        return [self.sem(f"{name}{i}") for i in range(n)]


def stage_project(nc, dram, res):
    with ExitStack() as ctx:
        m = Mem(nc, ctx, "prj")
        xT = m.sb("xT", [P, KD, TOK])
        wtm = m.sb("wtm", [P, KD, TM_W])
        wfm = [m.sb(f"wfm{s}", [P, KD, P]) for s in range(2)]
        RW = TOK + 4 * (CONV_K // 2)
        CW = RW - (CONV_K - 1)
        raw = [m.sb(f"raw{s}", [P, RW]) for s in range(2)]
        acc = m.sb("acc", [P, CW])
        xbc = [m.sb(f"xbc{s}", [P, TOK]) for s in range(2)]
        convw = m.sb("convw", [P, NCH, CONV_K + 1])
        xt = [m.sb(f"xt{s}", [P, KD, P]) for s in range(2)]
        qk = [m.sb(f"qk{s}", [P, 2 * HEADS, HD]) for s in range(2)]
        rope = m.sb("rope", [P, 4, 2 * HEADS, HALF_ROT])
        vt = [m.sb(f"vt{s}", [P, AW]) for s in range(2)]
        qkT = [m.sb(f"qkT{s}", [P, KD, P]) for s in range(2)]
        cs = m.sb("cs", [P, NT, 2, HALF_ROT])
        ident = m.sb("ident", [P, P])
        ps = m.ps("ps", [P, 8, 512])

        const_in = m.sem("const_in")
        x_in = m.sems("x_in", 3)
        wtm_in = m.sem("wtm_in")
        wfm_in = m.sems("wfm_in")
        fm_mm = m.sem("fm_mm")
        raw_ready = m.sem("raw_ready")
        margins = m.sem("margins")
        conv_step = m.sem("conv_step")
        xbc_ready = m.sem("xbc_ready")
        xbc_out = m.sem("xbc_out")
        xbc_free = m.sem("xbc_free")
        xt_in = m.sems("xt_in")
        tm_mm = m.sem("tm_mm")
        qk_ready = m.sem("qk_ready")
        v_ready = m.sem("v_ready")
        z_ready = m.sem("z_ready")
        dt_ready = m.sem("dt_ready")
        rope_step = m.sem("rope_step")
        tr_mm = m.sem("tr_mm")
        qkT_ready = m.sem("qkT_ready")
        vq_out = m.sem("vq_out")
        vq_free = m.sem("vq_free")
        wfm_src = dram["w_in"][:, 4 * 512:4 * 512 + CONV_CH].rearrange("(k p) (c n) -> p k c n", p=P, n=P)
        w_src = dram["w_in"].rearrange("(k p) n -> p k n", p=P)
        xT_src = dram["xT"].rearrange("(k p) t -> p k t", p=P)
        block = ctx.enter_context(nc.Block())
        ROPE_STEPS = 6

        @block.sync
        def _(sp):
            for g in range(3):
                if g == 0:
                    sp.dma_start(wfm[0][:], wfm_src[:, :, 0, :]).then_inc(wfm_in[0], 16)
                sp.dma_start(xT[:, :, 512 * g:512 * g + 512], xT_src[:, :, 512 * g:512 * g + 512]).then_inc(x_in[g], 16)
            sp.dma_start(wfm[1][:], wfm_src[:, :, 1, :]).then_inc(wfm_in[1], 16)
            with sp.Fori(1, NCH // 2) as cc:
                for s in range(2):
                    c = 2 * cc + s
                    sp.wait_ge(fm_mm, 3 * c + 3)
                    sp.dma_start(wfm[s][:], wfm_src[:, :, bass.ds(c, 1), :].rearrange("p k c n -> p k (c n)")).then_inc(wfm_in[s], 16)
            with sp.Fori(0, NT // 2) as tt:
                for s in range(2):
                    t = 2 * tt + s
                    sp.wait_ge(tm_mm, 5 * t + 5)
                    sp.dma_start(xt[s][:], xT_src[:, :, bass.ds(t * P, P)]).then_inc(xt_in[s], 16)

        @block.tensor
        def _(pe):
            pe.sem_inc(fm_mm, 6)
            pe.sem_inc(tm_mm, 10)
            pe.sem_inc(tr_mm, 2)
            for g in range(3):
                pe.wait_ge(x_in[g], 16)
            with pe.Fori(0, NCH // 2) as cc:
                for s in range(2):
                    c = 2 * cc + s
                    pe.wait_ge(wfm_in[s], 16 * cc + 16)
                    for g in range(3):
                        pe.wait_ge(raw_ready, 3 * c + g + 1)
                        for k in range(KD):
                            mm = pe.matmul(ps[:, 3 * s + g, :], wfm[s][:, k, :], xT[:, k, 512 * g:512 * g + 512],
                                           start=(k == 0), stop=(k == KD - 1))
                        mm.then_inc(fm_mm, 1)
            pe.wait_ge(raw_ready, 6 + 3 * NCH)
            pe.wait_ge(wtm_in, 32)
            pe.wait_ge(const_in, 48)
            with pe.Fori(0, NT // 2) as tt:
                for s in range(2):
                    t = 2 * tt + s
                    pe.wait_ge(xt_in[s], 16 * tt + 16)
                    for n in range(5):
                        if n < 2:
                            pe.wait_ge(qk_ready, 2 * t + n + 1)
                        if n == 2:
                            pe.wait_ge(v_ready, t + 1)
                        if n == 3:
                            pe.wait_ge(z_ready, t + 1)
                        if n == 4:
                            pe.wait_ge(dt_ready, t + 1)
                        w = 512 if n < 4 else NDT
                        for k in range(KD):
                            mm = pe.matmul(ps[:, n, 0:w], xt[s][:, k, :], wtm[:, k, 512 * n:512 * n + w],
                                           start=(k == 0), stop=(k == KD - 1))
                        mm.then_inc(tm_mm, 1)
                    pe.wait_ge(rope_step, ROPE_STEPS * t + ROPE_STEPS)
                    pe.wait_ge(qkT_ready, 2 * t + 2)
                    for j in range(KD):
                        src = qk[s][:, 2 * j:2 * j + 2, :].rearrange("p a e -> p (a e)")
                        mm = pe.transpose(ps[:, 6 + j // 4, P * (j % 4):P * (j % 4) + P], src, ident[:])
                    mm.then_inc(tr_mm, 1)

        @block.scalar
        def _(act):
            act.sem_inc(raw_ready, 6)
            act.sem_inc(xbc_ready, 1)
            act.sem_inc(qk_ready, 2)
            act.sem_inc(v_ready, 1)
            act.sem_inc(z_ready, 1)
            act.dma_start(wtm[:, :, 0:2048], w_src[:, :, 0:2048]).then_inc(wtm_in, 16)
            act.dma_start(wtm[:, :, 2048:TM_W], w_src[:, :, 2048 + CONV_CH:]).then_inc(wtm_in, 16)
            act.wait_ge(margins, 2)
            starts = (2, 2 + SEQS[0] + 4, 2 + SEQS[0] + 4 + 512)

            def silu_out(c, cc, s):
                act.wait_ge(conv_step, 10 + 5 * c + 5)
                act.wait_ge(xbc_free, c + 1)
                act.activation(xbc[s][:, 0:SEQS[0]], acc[:, 0:SEQS[0]], ACT.Silu)
                act.activation(xbc[s][:, SEQS[0]:], acc[:, SEQS[0] + 4:], ACT.Silu).then_inc(xbc_ready, 1)

            with act.Fori(0, NCH // 2) as cc:
                for s in range(2):
                    c = 2 * cc + s
                    act.wait_ge(conv_step, 5 * c + 5)
                    for g in range(3):
                        act.wait_ge(fm_mm, 6 + 3 * c + g + 1)
                        act.copy(raw[s][:, starts[g]:starts[g] + 512], ps[:, 3 * s + g, :]).then_inc(raw_ready, 1)
                    silu_out(c, cc, s)
            with act.Fori(0, NT // 2) as tt:
                for s in range(2):
                    t = 2 * tt + s
                    act.wait_ge(tr_mm, t + 1)
                    act.wait_ge(tm_mm, 10 + 5 * t + 1)
                    act.mul(qk[s][:, 0:HEADS, :], ps[:, 0, :].rearrange("p (h e) -> p h e", e=HD), HD ** -0.5).then_inc(qk_ready, 1)
                    act.wait_ge(tm_mm, 10 + 5 * t + 2)
                    act.copy(qk[s][:, HEADS:, :], ps[:, 1, :].rearrange("p (h e) -> p h e", e=HD)).then_inc(qk_ready, 1)
                    act.wait_ge(tm_mm, 10 + 5 * t + 3)
                    act.wait_ge(vq_free, t + 1)
                    act.copy(vt[s][:], ps[:, 2, :]).then_inc(v_ready, 1)
                    act.wait_ge(tm_mm, 10 + 5 * t + 4)
                    act.activation(res["z"][:, bass.ds(t, 1), :], ps[:, 3:4, :], ACT.Silu).then_inc(z_ready, 1)

        @block.vector
        def _(dve):
            dve.sem_inc(conv_step, 10)
            dve.sem_inc(dt_ready, 1)
            dve.sem_inc(qkT_ready, 2)
            for s in range(2):
                dve.memset(raw[s][:, 0:2], 0.0)
                dve.memset(raw[s][:, 2 + SEQS[0]:2 + SEQS[0] + 4], 0.0)
                dve.memset(raw[s][:, RW - 2:RW], 0.0).then_inc(margins, 1)
            dve.wait_ge(margins, 2)
            dve.wait_ge(const_in, 48)
            with dve.Fori(0, NCH // 2) as cc:
                for s in range(2):
                    c = 2 * cc + s
                    dve.wait_ge(raw_ready, 6 + 3 * c + 3)
                    dve.wait_ge(xbc_ready, c + 1)
                    dve.tensor_scalar(acc[:], raw[s][:, 0:CW], convw[:, bass.ds(c, 1), 0], convw[:, bass.ds(c, 1), CONV_K],
                                      ALU.mult, ALU.add).then_inc(conv_step, 1)
                    for k in range(1, CONV_K):
                        dve.wait_ge(conv_step, 10 + 5 * c + k)
                        dve.scalar_tensor_tensor(acc[:], raw[s][:, k:k + CW], convw[:, bass.ds(c, 1), k], acc[:],
                                                 ALU.mult, ALU.add).then_inc(conv_step, 1)
            with dve.Fori(0, NT // 2) as tt:
                for s in range(2):
                    t = 2 * tt + s
                    n0 = ROPE_STEPS * t
                    dve.wait_ge(qk_ready, 2 + 2 * t + 2)
                    t1 = qk[s][:, :, 0:HALF_ROT]
                    t2 = qk[s][:, :, HALF_ROT:ROT]
                    cos = cs[:, bass.ds(t, 1), 0, :].broadcast_to([P, 2 * HEADS, HALF_ROT])
                    sin = cs[:, bass.ds(t, 1), 1, :].broadcast_to([P, 2 * HEADS, HALF_ROT])
                    for n, (a, b) in enumerate(((t1, cos), (t2, sin), (t2, cos), (t1, sin))):
                        dve.tensor_tensor(rope[:, n], a, b, ALU.mult).then_inc(rope_step, 1)
                    dve.wait_ge(rope_step, n0 + 4)
                    dve.tensor_tensor(t1, rope[:, 0], rope[:, 1], ALU.subtract).then_inc(rope_step, 1)
                    dve.tensor_tensor(t2, rope[:, 2], rope[:, 3], ALU.add).then_inc(rope_step, 1)
                    dve.wait_ge(rope_step, n0 + 6)
                    dve.wait_ge(tm_mm, 10 + 5 * t + 5)
                    dve.tensor_copy(res["dt"][:, bass.ds(t, 1), :], ps[:, 4:5, 0:NDT]).then_inc(dt_ready, 1)
                    dve.wait_ge(tr_mm, 2 + t + 1)
                    dve.wait_ge(vq_free, t + 1)
                    for b in range(2):
                        dve.tensor_copy(qkT[s][:, 4 * b:4 * b + 4, :],
                                        ps[:, 6 + b, :].rearrange("p (j t) -> p j t", j=4)).then_inc(qkT_ready, 1)

        @block.gpsimd
        def _(pool):
            pool.sem_inc(xbc_free, 2)
            pool.sem_inc(vq_free, 2)
            pool.dma_start(cs[:], dram["rope"]).then_inc(const_in, 16)
            pool.dma_start(convw[:], dram["conv"]).then_inc(const_in, 16)
            pool.dma_start(ident[:], dram["ident"]).then_inc(const_in, 16)
            with pool.Fori(0, NCH // 2) as cc:
                for s in range(2):
                    c = 2 * cc + s
                    pool.wait_ge(xbc_ready, 1 + c + 1)
                    dst = dram["xbc"][bass.ds(c * P, P), :]
                    pool.dma_start(dst, xbc[s][:]).then_inc(xbc_out, 16)
                    pool.wait_ge(xbc_out, 16 * c + 16)
                    pool.sem_inc(xbc_free, 1)
            with pool.Fori(0, NT // 2) as tt:
                for s in range(2):
                    t = 2 * tt + s
                    pool.wait_ge(v_ready, 1 + t + 1)
                    pool.dma_start(dram["v"][bass.ds(t * P, P), :], vt[s][:]).then_inc(vq_out, 16)
                    pool.wait_ge(qkT_ready, 2 + 2 * t + 2)
                    pool.dma_start(dram["qkT"][:, bass.ds(t * P, P)].rearrange("(k p) t -> p k t", p=P), qkT[s][:]).then_inc(vq_out, 16)
                    pool.wait_ge(vq_out, 32 * t + 32)
                    pool.sem_inc(vq_free, 1)
            pool.wait_ge(dt_ready, 1 + NT)
            pool.wait_ge(z_ready, 1 + NT)


def stage_attend(nc, dram, res):
    ITEMS = NT
    PV0 = 2 * ITEMS
    first_item = (0, SEQS[0] // P)

    def shape_of(j):
        return (0, SEQS[0], j) if j < first_item[1] else (SEQS[0], SEQS[1], j - first_item[1])

    with ExitStack() as ctx:
        m = Mem(nc, ctx, "att")
        qT = [m.sb(f"qT{s}", [HD, TOK]) for s in range(2)]
        kT = [m.sb(f"kT{s}", [HD, TOK]) for s in range(2)]
        v = [m.sb(f"v{s}", [P, NT, HD]) for s in range(2)]
        mask = m.sb("mask", [P, MASK_W])
        ident = m.sb("ident", [P, P])
        neg = [m.sb(f"neg{s}", [P, SEQS[1]]) for s in range(2)]
        negmax = m.sb("negmax", [P, 2])
        probs = [m.sb(f"probs{s}", [P, SEQS[1]]) for s in range(2)]
        pT = [m.sb(f"pT{s}", [P, 2, 4, P]) for s in range(2)]
        den = m.sb("den", [P, 4])
        rden = m.sb("rden", [P, 2])
        sc = [m.ps(f"sc{s}", [P, SEQS[1]]) for s in range(2)]
        trA = m.ps("trA", [P, 4, P])
        trB = m.ps("trB", [P, 4, P])
        o = [m.ps(f"o{s}", [P, 512]) for s in range(2)]

        const_in = m.sem("const_in")
        qkv_in = m.sems("qkv_in")
        score_mm = m.sem("score_mm")
        masked = m.sem("masked")
        exp_done = m.sem("exp_done")
        tr_mm = m.sem("tr_mm")
        copyA = m.sem("copyA")
        copyB = m.sem("copyB")
        pv_mm = m.sem("pv_mm")
        recip = m.sem("recip")
        normed = m.sem("normed")
        held = m.sem("held")
        block = ctx.enter_context(nc.Block())

        def heads(eng, body):
            with eng.Fori(0, HEADS // 2 - 1) as hh:
                for s in range(2):
                    body(2 * hh + s, hh, s, False)
            body(HEADS - 2, HEADS // 2 - 1, 0, False)
            body(HEADS - 1, HEADS // 2 - 1, 1, True)

        @block.sync
        def _(sp):
            sp.dma_start(mask[:], dram["mask"]).then_inc(const_in, 16)
            sp.dma_start(ident[:], dram["ident"]).then_inc(const_in, 16)
            with sp.Fori(0, HEADS // 2) as hh:
                for s in range(2):
                    h = 2 * hh + s
                    sp.wait_ge(pv_mm, ITEMS * h + ITEMS)
                    sp.dma_start(qT[s][:], dram["qkT"][bass.ds(h * HD, HD), :]).then_inc(qkv_in[s], 16)
                    sp.dma_start(kT[s][:], dram["qkT"][bass.ds(AW + h * HD, HD), :]).then_inc(qkv_in[s], 16)
                    sp.dma_start(v[s][:], dram["v"][:, bass.ds(h * HD, HD)].rearrange("(t p) e -> p t e", p=P)).then_inc(qkv_in[s], 16)

        @block.tensor
        def _(pe):
            pe.sem_inc(tr_mm, 2)
            pe.sem_inc(pv_mm, PV0)

            def scores(h, hh, s, j):
                n = ITEMS * h + j
                t0, S, i = shape_of(j)
                if j == 0:
                    pe.wait_ge(qkv_in[s], 48 * hh + 48)
                pe.wait_ge(masked, n + 1)
                for b in range(S // 512):
                    mm = pe.matmul(sc[j % 2][:, 512 * b:512 * b + 512], qT[s][:, t0 + P * i:t0 + P * i + P],
                                   kT[s][:, t0 + 512 * b:t0 + 512 * b + 512], start=True, stop=True)
                mm.then_inc(score_mm, 1)

            def transposes(h, j):
                n = ITEMS * h + j
                nb = shape_of(j)[1] // P
                pe.wait_ge(exp_done, 2 + n + 1)
                pe.wait_ge(copyA, n + 1)
                pe.wait_ge(copyB, n + 1)
                for b in range(nb):
                    bank = trA if b < nb // 2 else trB
                    mm = pe.transpose(bank[:, b % (nb // 2), :], probs[j % 2][:, P * b:P * b + P], ident[:])
                mm.then_inc(tr_mm, 1)

            def values(h, s, j):
                n = ITEMS * h + j
                t0, S, i = shape_of(j)
                nb = S // P
                pe.wait_ge(copyA, 1 + n + 1)
                pe.wait_ge(copyB, 1 + n + 1)
                pe.wait_ge(normed, n + 3)
                for b in range(nb):
                    mm = pe.matmul(o[j % 2][:, 0:HD], pT[j % 2][:, b // (nb // 2), b % (nb // 2), :],
                                   v[s][:, t0 // P + b, :], start=(b == 0), stop=(b == nb - 1))
                mm.then_inc(pv_mm, 1)

            def body(h, hh, s, last):
                for j in range(ITEMS):
                    if j + 2 < ITEMS:
                        scores(h, hh, s, j + 2)
                    elif not last:
                        scores(h + 1, hh + s, 1 - s, j + 2 - ITEMS)
                    if j + 1 < ITEMS:
                        transposes(h, j + 1)
                    elif not last:
                        transposes(h + 1, 0)
                    values(h, s, j)

            pe.wait_ge(const_in, 32)
            scores(0, 0, 0, 0)
            scores(0, 0, 0, 1)
            transposes(0, 0)
            heads(pe, body)

        @block.vector
        def _(dve):
            dve.sem_inc(masked, 2)
            dve.sem_inc(copyA, 1)
            dve.sem_inc(normed, 4)

            def mask_scores(h, j):
                n = ITEMS * h + j
                t0, S, i = shape_of(j)
                dve.wait_ge(score_mm, n + 1)
                dve.wait_ge(exp_done, n + 1)
                dve.sem_inc(held, 1)
                at = MASK_0 - P * i
                dve.tensor_tensor_reduce(neg[j % 2][:, 0:S], sc[j % 2][:, 0:S], mask[:, at:at + S], -1.0, 3.0e38,
                                         ALU.add, ALU.min, negmax[:, j % 2:j % 2 + 1]).then_inc(masked, 1)

            def copy_half(h, j):
                n = ITEMS * h + j
                nb = shape_of(j)[1] // P
                dve.wait_ge(tr_mm, 2 + n + 1)
                dve.wait_ge(pv_mm, PV0 - 2 + n + 1)
                dve.tensor_copy(pT[j % 2][:, 0, 0:nb // 2, :], trA[:, 0:nb // 2, :]).then_inc(copyA, 1)

            def normalise(h, j):
                n = ITEMS * h + j
                dve.wait_ge(exp_done, 2 + n + 1)
                dve.wait_ge(normed, 4 + n - 1)
                dve.reciprocal(rden[:, j % 2:j % 2 + 1], den[:, j % 4:j % 4 + 1]).then_inc(recip, 1)
                dve.wait_ge(recip, n + 1)
                dve.wait_ge(pv_mm, PV0 + n + 1)
                out = res["att"][:, j, bass.ds(h * HD, HD)]
                dve.tensor_scalar(out, o[j % 2][:, 0:HD], rden[:, j % 2:j % 2 + 1], None, ALU.mult).then_inc(normed, 1)

            def body(h, hh, s, last):
                for j in range(ITEMS):
                    if j + 2 < ITEMS:
                        mask_scores(h, j + 2)
                    elif not last:
                        mask_scores(h + 1, j + 2 - ITEMS)
                    if j + 1 < ITEMS:
                        copy_half(h, j + 1)
                    elif not last:
                        copy_half(h + 1, 0)
                    normalise(h, j)

            dve.wait_ge(const_in, 32)
            mask_scores(0, 0)
            mask_scores(0, 1)
            copy_half(0, 0)
            heads(dve, body)

        @block.scalar
        def _(act):
            act.sem_inc(exp_done, 2)
            act.sem_inc(copyB, 1)

            def exponent(h, j):
                n = ITEMS * h + j
                S = shape_of(j)[1]
                act.wait_ge(masked, 2 + n + 1)
                act.wait_ge(tr_mm, n + 1)
                act.wait_ge(normed, n + 1)
                act.activation(probs[j % 2][:, 0:S], neg[j % 2][:, 0:S], ACT.Exp, bias=negmax[:, j % 2:j % 2 + 1],
                               scale=-1.0, accum_out=den[:, j % 4:j % 4 + 1]).then_inc(exp_done, 1)

            def copy_half(h, j):
                n = ITEMS * h + j
                nb = shape_of(j)[1] // P
                act.wait_ge(tr_mm, 2 + n + 1)
                act.wait_ge(pv_mm, PV0 - 2 + n + 1)
                act.copy(pT[j % 2][:, 1, 0:nb // 2, :], trB[:, 0:nb // 2, :]).then_inc(copyB, 1)

            def body(h, hh, s, last):
                for j in range(ITEMS):
                    if j + 2 < ITEMS:
                        exponent(h, j + 2)
                    elif not last:
                        exponent(h + 1, j + 2 - ITEMS)
                    if j + 1 < ITEMS:
                        copy_half(h, j + 1)
                    elif not last:
                        copy_half(h + 1, 0)

            exponent(0, 0)
            exponent(0, 1)
            copy_half(0, 0)
            heads(act, body)


def stage_ssd(nc, dram, res):
    GH = HEADS // GROUPS
    HP = GH * HD
    LT, LE, GT, GE, ONE = range(5)
    TO_END, TO_START, FROM_START, FROM_END, ALL_F, ALL_B = range(6)
    LOG_TERMS = 9

    with ExitStack() as ctx:
        m = Mem(nc, ctx, "ssd")
        tri = m.sb("tri", [P, 5, P])
        ident = m.sb("ident", [P, P])
        dtb = m.sb("dtb", [P, NDT])
        alog = m.sb("alog", [P, NDT])
        dsk = m.sb("dsk", [P, HEADS])
        dtr = res["dt"]
        w1 = m.sb("w1", [P, NT, NDT])
        w2 = m.sb("w2", [P, NT, NDT])
        w3 = m.sb("w3", [P, NT, NDT])
        w4 = m.sb("w4", [P, NT, NDT])
        dt = m.sb("dt", [P, NT, NDT])
        dtA = m.sb("dtA", [P, NT, NDT])
        ex = m.sb("ex", [P, 6, NT, HEADS])
        wdt = m.sb("wdt", [P, 2, NT, HEADS])
        xb = [m.sb(f"xb{s}", [P, NCH, P]) for s in range(2)]
        rf = [m.sb(f"rf{s}", [P, HEADS, P]) for s in range(2)]
        rb = [m.sb(f"rb{s}", [P, HEADS, P]) for s in range(2)]
        E = [m.sb(f"E{s}", [P, GROUPS, GH, P]) for s in range(2)]
        cb = [m.sb(f"cb{s}", [P, 2, GROUPS, P]) for s in range(2)]
        W = [m.sb(f"W{s}", [P, 2, HEADS, P]) for s in range(2)]
        xtok = [m.sb(f"xtok{s}", [P, HEADS, HD]) for s in range(2)]
        btok = [m.sb(f"btok{s}", [P, GROUPS, P]) for s in range(2)]
        xdt = [m.sb(f"xdt{s}", [P, 3, HEADS, HD]) for s in range(2)]
        xst = [m.sb(f"xst{s}", [P, 2, HEADS, HD]) for s in range(2)]
        Sf = m.sb("Sf", [P, HEADS, HD])
        Sb = m.sb("Sb", [P, HEADS, HD])
        stb = m.sb("stb", [P, NT, HEADS, HD])
        yo = m.sb("yo", [P, HEADS, HD])
        cT = [m.sb(f"cT{s}", [P, GROUPS, P]) for s in range(2)]
        psx = m.ps("psx", [P, 512])
        psb = m.ps("psb", [P, 2, GROUPS, P])
        seg = m.ps("seg", [P, HEADS, P])
        psy = m.ps("psy", [P, HEADS, HD])
        psf = m.ps("psf", [P, HEADS, HD])
        pss = m.ps("pss", [P, HEADS, HD])
        pso = m.ps("pso", [P, HEADS, HD])

        const_in = m.sem("const_in")
        pre = m.sem("pre")
        pre_exp = m.sem("pre_exp")
        sums_mm = m.sem("sums_mm")
        tables = m.sem("tables")
        xb_in = m.sems("xb_in")
        tok_mm = m.sem("tok_mm")
        tok_ready = m.sem("tok_ready")
        cb_mm = m.sem("cb_mm")
        cb_ready = m.sem("cb_ready")
        rf_ready = m.sem("rf_ready")
        rb_ready = m.sem("rb_ready")
        seg_mm = m.sem("seg_mm")
        e_ready = m.sem("e_ready")
        w_ready = m.sem("w_ready")
        xdt_ready = m.sem("xdt_ready")
        xst_ready = m.sem("xst_ready")
        y_mm = m.sem("y_mm")
        st_mm = m.sem("st_mm")
        off_mm = m.sem("off_mm")
        stb_ready = m.sem("stb_ready")
        sf_zero = m.sem("sf_zero")
        sf_step = m.sem("sf_step")
        y_step = m.sem("y_step")
        cT_in = m.sems("cT_in")
        offb_mm = m.sem("offb_mm")
        sb_zero = m.sem("sb_zero")
        sb_step = m.sem("sb_step")
        yb_step = m.sem("yb_step")
        held_sp = m.sem("held_sp")
        held_dve = m.sem("held_dve")
        block = ctx.enter_context(nc.Block())
        FIRST = FIRST_TILE[1]

        def chunks(eng, body, between):
            with eng.Fori(0, FIRST // 2) as tt:
                for s in range(2):
                    body(2 * tt + s, tt, s, False)
            between()
            with eng.Fori(FIRST // 2, NT // 2 - 1) as tt:
                for s in range(2):
                    body(2 * tt + s, tt, s, False)
            body(NT - 2, NT // 2 - 1, 0, False)
            body(NT - 1, NT // 2 - 1, 1, True)

        def back(eng, body, between):
            with eng.Fori(0, (NT - FIRST) // 2) as ii:
                for s in range(2):
                    body(2 * ii + s, ii, s)
            between()
            with eng.Fori((NT - FIRST) // 2, NT // 2) as ii:
                for s in range(2):
                    body(2 * ii + s, ii, s)

        @block.sync
        def _(sp):
            for dst, name in ((tri, "tri"), (ident, "ident"), (dtb, "dt_bias"), (alog, "a_log"), (dsk, "d_skip")):
                sp.dma_start(dst[:], dram[name]).then_inc(const_in, 16)
            src = dram["xbc"].rearrange("(c p) t -> p c t", p=P)
            with sp.Fori(0, NT // 2) as tt:
                for s in range(2):
                    t = 2 * tt + s
                    sp.wait_ge(off_mm, t + 1)
                    sp.dma_start(xb[s][:], src[:, :, bass.ds(t * P, P)]).then_inc(xb_in[s], 16)
            with sp.Fori(0, NT // 2) as ii:
                for s in range(2):
                    i = 2 * ii + s
                    sp.wait_ge(offb_mm, i + 1)
                    sp.sem_inc(held_sp, 1)
                    at = (NT - 1) * P - i * P
                    sp.dma_start(cT[s][:], src[:, NCH - GROUPS:, bass.ds(at, P)]).then_inc(cT_in[s], 16)

        @block.tensor
        def _(pe):
            for sem, n in ((seg_mm, 2), (y_mm, 2), (st_mm, 2), (off_mm, 2), (offb_mm, 2)):
                pe.sem_inc(sem, n)
            pe.wait_ge(const_in, 80)
            pe.wait_ge(tables, 1)
            sums = ((GT, 0), (LT, HEADS), (LE, 0), (GE, HEADS), (ONE, 0), (ONE, HEADS))
            flat = seg[:].rearrange("p h l -> p (h l)")
            for n, (tr, off) in enumerate(sums):
                at = 512 * (n // 3) + NT * HEADS * (n % 3)
                mm = pe.matmul(flat[:, at:at + NT * HEADS], tri[:, tr, :], dtA[:, :, off:off + HEADS], start=True, stop=True)
            mm.then_inc(sums_mm, 1)
            pe.wait_ge(pre_exp, 4)

            def to_tokens(t, tt, s):
                pe.wait_ge(xb_in[s], 16 * tt + 16)
                pe.wait_ge(tok_ready, 2 * t + 2)
                pe.wait_ge(cb_ready, 2 * t + 2)
                for j in range(SSM_W // P):
                    pe.transpose(psx[:, P * j:P * j + P], xb[s][:, j, :], ident[:])
                for g in range(GROUPS):
                    mm = pe.transpose(psb[:, 0, g, :], xb[s][:, SSM_W // P + g, :], ident[:])
                mm.then_inc(tok_mm, 1)

            def products(t, s):
                pe.wait_ge(tok_ready, 2 + 2 * t + 2)
                for g in range(GROUPS):
                    mm = pe.matmul(psb[:, 1, g, :], xb[s][:, SSM_W // P + g, :], xb[s][:, SSM_W // P + GROUPS + g, :],
                                   start=True, stop=True)
                mm.then_inc(cb_mm, 1)

            def segments(t, s):
                pe.wait_ge(rf_ready, t + 1)
                pe.wait_ge(rb_ready, t + 1)
                pe.wait_ge(e_ready, t + 1)
                for half in range(2):
                    hs = slice(GH * half, GH * half + GH)
                    pe.matmul(seg[:, hs, :], tri[:, GT, :], rf[s][:, hs, :], start=True, stop=False)
                    mm = pe.matmul(seg[:, hs, :], tri[:, LT, :], rb[s][:, hs, :], start=False, stop=True)
                mm.then_inc(seg_mm, 1)

            def body(t, tt, s, last):
                if not last:
                    to_tokens(t + 1, tt + s, 1 - s)
                    segments(t + 1, 1 - s)
                    products(t + 1, 1 - s)
                pe.wait_ge(sf_step, 2 * t + 2)
                pe.wait_ge(y_step, 3 * t + 1)
                for g in range(GROUPS):
                    gs = slice(GH * g, GH * g + GH)
                    mm = pe.matmul(pso[:, gs, :], xb[s][:, SSM_W // P + GROUPS + g, :], Sf[:, gs, :], start=True, stop=True)
                mm.then_inc(off_mm, 1)
                pe.wait_ge(xst_ready, 4 + 2 * t + 2)
                pe.wait_ge(tok_ready, 2 + 2 * t + 2)
                pe.wait_ge(stb_ready, t + 1)
                for ps_, d in ((psf, 0), (pss, 1)):
                    for g in range(GROUPS):
                        gs = slice(GH * g, GH * g + GH)
                        mm = pe.matmul(ps_[:, gs, :], btok[s][:, g, :], xst[s][:, d, gs, :], start=True, stop=True)
                mm.then_inc(st_mm, 1)
                pe.wait_ge(w_ready, 4 + 2 * t + 2)
                pe.wait_ge(xdt_ready, 6 + 3 * t + 3)
                pe.wait_ge(y_step, 3 * t + 2)
                for h in range(HEADS):
                    for d in range(2):
                        mm = pe.matmul(psy[:, h, :], W[s][:, d, h, :], xdt[s][:, d, h, :], start=(d == 0), stop=(d == 1))
                mm.then_inc(y_mm, 1)

            pe.wait_ge(sf_zero, 1)
            to_tokens(0, 0, 0)
            segments(0, 0)
            products(0, 0)
            chunks(pe, body, lambda: pe.wait_ge(sf_zero, 2))

            def body_back(i, ii, s):
                pe.wait_ge(cT_in[s], 16 * ii + 16)
                pe.wait_ge(sb_step, 2 * i + 2)
                pe.wait_ge(yb_step, 2 * i + 1)
                for g in range(GROUPS):
                    gs = slice(GH * g, GH * g + GH)
                    mm = pe.matmul(pso[:, gs, :], cT[s][:, g, :], Sb[:, gs, :], start=True, stop=True)
                mm.then_inc(offb_mm, 1)

            pe.wait_ge(y_step, 3 + 3 * NT)
            pe.wait_ge(sb_zero, 1)
            back(pe, body_back, lambda: pe.wait_ge(sb_zero, 2))

        @block.scalar
        def _(act):
            for sem, n in ((tok_ready, 2), (e_ready, 1), (stb_ready, 1)):
                act.sem_inc(sem, n)
            act.wait_ge(const_in, 80)
            act.activation(alog[:], alog[:], ACT.Exp).then_inc(pre_exp, 1)
            act.wait_ge(pre, 2)
            act.activation(w3[:], w2[:], ACT.Exp, scale=-1.0).then_inc(pre_exp, 1)
            act.wait_ge(sums_mm, 1)
            flat = seg[:].rearrange("p h l -> p (h l)")
            for n in range(2):
                act.activation(ex[:, 3 * n:3 * n + 3, :, :].rearrange("p n t h -> p (n t h)"),
                               flat[:, 512 * n:512 * n + 3 * NT * HEADS], ACT.Exp).then_inc(pre_exp, 1)

            def tokens(t, s):
                act.wait_ge(tok_mm, t + 1)
                act.wait_ge(xdt_ready, 3 * t + 3)
                act.wait_ge(xst_ready, 2 * t + 2)
                act.wait_ge(st_mm, t + 1)
                act.copy(xtok[s][:].rearrange("p h e -> p (h e)"), psx[:]).then_inc(tok_ready, 1)
                act.copy(btok[s][:], psb[:, 0]).then_inc(tok_ready, 1)

            def exponent(t, s):
                act.wait_ge(seg_mm, 2 + t + 1)
                act.wait_ge(w_ready, 2 * t + 2)
                act.activation(E[s][:].rearrange("p g h l -> p (g h) l"), seg[:], ACT.Exp).then_inc(e_ready, 1)

            def body(t, tt, s, last):
                if not last:
                    tokens(t + 1, 1 - s)
                    exponent(t + 1, 1 - s)
                act.wait_ge(st_mm, 2 + t + 1)
                act.copy(stb[:, bass.ds(t, 1), :, :].rearrange("p t h e -> p (t h) e"), pss[:]).then_inc(stb_ready, 1)

            tokens(0, 0)
            exponent(0, 0)
            chunks(act, body, lambda: None)

        @block.gpsimd
        def _(pool):
            pool.sem_inc(xst_ready, 4)
            pool.wait_ge(const_in, 80)
            pool.wait_ge(tables, 3)

            def sources(t, s):
                pool.wait_ge(seg_mm, t + 1)
                a = dtA[:, bass.ds(t, 1), 0:HEADS].rearrange("p t h -> p (t h)").unsqueeze(2).broadcast_to([P, HEADS, P])
                pool.tensor_tensor(rf[s][:], a, tri[:, LE:LE + 1, :].broadcast_to([P, HEADS, P]), ALU.mult).then_inc(rf_ready, 1)

            def body(t, tt, s, last):
                if not last:
                    sources(t + 1, 1 - s)
                pool.wait_ge(tok_ready, 2 + 2 * t + 1)
                pool.wait_ge(st_mm, t + 1)
                for d in range(2):
                    a = wdt[:, d, bass.ds(t, 1), :].rearrange("p t h -> p (t h)").unsqueeze(2).broadcast_to([P, HEADS, HD])
                    pool.tensor_tensor(xst[s][:, d], xtok[s][:], a, ALU.mult).then_inc(xst_ready, 1)

            sources(0, 0)
            chunks(pool, body, lambda: None)

        @block.vector
        def _(dve):
            for sem, n in ((cb_ready, 2), (w_ready, 4), (xdt_ready, 6), (y_step, 3), (sf_step, 2), (sb_step, 2), (yb_step, 2)):
                dve.sem_inc(sem, n)
            dve.memset(Sf[:], 0.0).then_inc(sf_zero, 1)
            dve.memset(Sb[:], 0.0).then_inc(sb_zero, 1)
            dve.wait_ge(const_in, 80)
            per_tile = [P, NT, NDT]
            dve.tensor_tensor(w1[:], dtr[:], dtb[:].unsqueeze(1).broadcast_to(per_tile), ALU.add).then_inc(pre, 1)
            dve.wait_ge(pre, 1)
            dve.scalar_tensor_tensor(w2[:], w1[:], -1.0, w1[:], ALU.mult, ALU.max).then_inc(pre, 1)
            dve.wait_ge(pre_exp, 2)
            dve.tensor_scalar(w2[:], w3[:], 2.0, None, ALU.add).then_inc(pre, 1)
            dve.wait_ge(pre, 3)
            dve.reciprocal(w2[:], w2[:]).then_inc(pre, 1)
            dve.wait_ge(pre, 4)
            dve.tensor_tensor(w3[:], w3[:], w2[:], ALU.mult).then_inc(pre, 1)
            dve.wait_ge(pre, 5)
            dve.tensor_tensor(w2[:], w3[:], w3[:], ALU.mult).then_inc(pre, 1)
            dve.wait_ge(pre, 6)
            dve.tensor_scalar(w4[:], w2[:], 1.0 / (2 * LOG_TERMS + 1), None, ALU.mult).then_inc(pre, 1)
            for n in range(LOG_TERMS - 1, 0, -1):
                dve.wait_ge(pre, 6 + LOG_TERMS - n)
                dve.scalar_tensor_tensor(w4[:], w4[:], 1.0 / (2 * n + 1), w2[:], ALU.add, ALU.mult).then_inc(pre, 1)
            dve.wait_ge(pre, 6 + LOG_TERMS)
            dve.scalar_tensor_tensor(w4[:], w4[:], 1.0, w3[:], ALU.add, ALU.mult).then_inc(pre, 1)
            dve.tensor_scalar(w1[:], w1[:], 0.0, None, ALU.max).then_inc(pre, 1)
            dve.wait_ge(pre, 8 + LOG_TERMS)
            dve.scalar_tensor_tensor(dt[:], w4[:], 2.0, w1[:], ALU.mult, ALU.add).then_inc(pre, 1)
            dve.wait_ge(pre, 9 + LOG_TERMS)
            dve.scalar_tensor_tensor(dtA[:], dt[:], -1.0, alog[:].unsqueeze(1).broadcast_to(per_tile), ALU.mult, ALU.mult).then_inc(tables, 1)
            dve.wait_ge(pre_exp, 4)
            for d in range(2):
                dve.tensor_tensor(wdt[:, d], dt[:, :, HEADS * d:HEADS * d + HEADS], ex[:, TO_END + d], ALU.mult).then_inc(tables, 1)
            dve.wait_ge(tables, 3)

            def over(a, shape):
                return a.rearrange("p t h -> p (t h)").unsqueeze(2).broadcast_to(shape)

            def sources(t, s):
                dve.wait_ge(seg_mm, t + 1)
                dve.tensor_tensor(rb[s][:], over(dtA[:, bass.ds(t, 1), HEADS:], [P, HEADS, P]),
                                  tri[:, GE:GE + 1, :].broadcast_to([P, HEADS, P]), ALU.mult).then_inc(rb_ready, 1)

            def mask_cb(t, s):
                dve.wait_ge(cb_mm, t + 1)
                dve.wait_ge(w_ready, 2 * t + 2)
                for d, tr in ((0, LE), (1, GE)):
                    dve.tensor_tensor(cb[s][:, d], psb[:, 1], tri[:, tr:tr + 1, :].broadcast_to([P, GROUPS, P]),
                                      ALU.mult).then_inc(cb_ready, 1)

            def body(t, tt, s, last):
                if not last:
                    sources(t + 1, 1 - s)
                dve.wait_ge(e_ready, 1 + t + 1)
                dve.wait_ge(cb_ready, 2 + 2 * t + 2)
                dve.wait_ge(y_mm, t + 1)
                for d in range(2):
                    dve.tensor_tensor(W[s][:, d].rearrange("p (g r) l -> p g r l", g=GROUPS), E[s][:],
                                      cb[s][:, d].unsqueeze(2).broadcast_to([P, GROUPS, GH, P]), ALU.mult).then_inc(w_ready, 1)
                dve.wait_ge(tok_ready, 2 + 2 * t + 1)
                dve.wait_ge(y_step, 3 * t + 3)
                for d in range(3):
                    a = over(dt[:, bass.ds(t, 1), HEADS * d:HEADS * d + HEADS], [P, HEADS, HD]) if d < 2 else \
                        dsk[:].unsqueeze(2).broadcast_to([P, HEADS, HD])
                    dve.tensor_tensor(xdt[s][:, d], xtok[s][:], a, ALU.mult).then_inc(xdt_ready, 1)
                if not last:
                    mask_cb(t + 1, 1 - s)
                dve.wait_ge(off_mm, 2 + t + 1)
                dve.tensor_tensor(yo[:], pso[:], over(ex[:, FROM_START, bass.ds(t, 1), :], [P, HEADS, HD]), ALU.mult).then_inc(y_step, 1)
                dve.wait_ge(sf_step, 2 + 2 * t)
                dve.tensor_tensor(Sf[:], Sf[:], over(ex[:, ALL_F, bass.ds(t, 1), :], [P, HEADS, HD]), ALU.mult).then_inc(sf_step, 1)
                dve.wait_ge(st_mm, 2 + t + 1)
                dve.wait_ge(sf_step, 2 + 2 * t + 1)
                dve.tensor_tensor(Sf[:], Sf[:], psf[:], ALU.add).then_inc(sf_step, 1)
                dve.wait_ge(y_mm, 2 + t + 1)
                dve.wait_ge(y_step, 3 + 3 * t + 1)
                dve.tensor_tensor(yo[:], yo[:], psy[:], ALU.add).then_inc(y_step, 1)
                dve.wait_ge(y_step, 3 + 3 * t + 2)
                dve.wait_ge(xdt_ready, 6 + 3 * t + 3)
                out = res["y"][:, bass.ds(t, 1), :].rearrange("p t (h e) -> p (t h) e", e=HD)
                dve.tensor_tensor(out, yo[:], xdt[s][:, 2], ALU.add).then_inc(y_step, 1)

            def restart():
                dve.wait_ge(sf_step, 2 + 2 * FIRST)
                dve.memset(Sf[:], 0.0).then_inc(sf_zero, 1)
                dve.wait_ge(sf_zero, 2)

            dve.wait_ge(sf_zero, 1)
            sources(0, 0)
            mask_cb(0, 0)
            chunks(dve, body, restart)

            def body_back(i, ii, s):
                t = (NT - 1) - i
                dve.wait_ge(offb_mm, 2 + i + 1)
                dve.wait_ge(yb_step, 2 * i + 2)
                dve.sem_inc(held_dve, 1)
                dve.tensor_tensor(yo[:], pso[:], over(ex[:, FROM_END, bass.ds(t, 1), :], [P, HEADS, HD]), ALU.mult).then_inc(yb_step, 1)
                dve.wait_ge(sb_step, 2 * i + 2)
                dve.tensor_tensor(Sb[:], Sb[:], over(ex[:, ALL_B, bass.ds(t, 1), :], [P, HEADS, HD]), ALU.mult).then_inc(sb_step, 1)
                dve.wait_ge(sb_step, 2 * i + 3)
                dve.tensor_tensor(Sb[:], Sb[:], stb[:, bass.ds(t, 1), :, :].rearrange("p t h e -> p (t h) e"), ALU.add).then_inc(sb_step, 1)
                dve.wait_ge(yb_step, 2 * i + 3)
                out = res["y"][:, bass.ds(t, 1), :].rearrange("p t (h e) -> p (t h) e", e=HD)
                dve.tensor_tensor(out, out, yo[:], ALU.add).then_inc(yb_step, 1)

            def restart_back():
                dve.wait_ge(sb_step, 2 + 2 * (NT - FIRST))
                dve.memset(Sb[:], 0.0).then_inc(sb_zero, 1)
                dve.wait_ge(sb_zero, 2)

            dve.wait_ge(stb_ready, 1 + NT)
            dve.wait_ge(sb_zero, 1)
            dve.wait_ge(y_step, 3 + 3 * NT)
            back(dve, body_back, restart_back)
            dve.wait_ge(yb_step, 2 + 2 * NT)


def stage_mix(nc, dram, res):
    with ExitStack() as ctx:
        m = Mem(nc, ctx, "mix")
        wout = m.sb("wout", [P, KD, D])
        wr = m.sb("wr", [P, KD, EXPERTS])
        normw = m.sb("normw", [P, SSM_W])
        ln = m.sb("ln", [P, 2, D])
        ident = m.sb("ident", [P, P])
        half = m.sb("half", [P, 1])
        xr = [m.sb(f"xr{s}", [P, D]) for s in range(2)]
        mixin = [m.sb(f"mixin{s}", [P, D]) for s in range(2)]
        sq = m.sb("sq", [P, SSM_W])
        ss = m.sb("ss", [P, 2])
        rs = m.sb("rs", [P, 2])
        mT = [m.sb(f"mT{s}", [P, KD, P]) for s in range(2)]
        r = m.sb("r", [P, D])
        stats = m.sb("stats", [P, 2, 6])
        mv = m.sb("mv", [P, 2])
        rstd = m.sb("rstd", [P, 1])
        h = [m.sb(f"h{s}", [P, D]) for s in range(2)]
        ah = [m.sb(f"ah{s}", [P, D]) for s in range(2)]
        hT = m.sb("hT", [P, KD, P])
        nmx = m.sb("nmx", [P, 1])
        er = m.sb("er", [P, EXPERTS])
        den = m.sb("den", [P, 1])
        rden = m.sb("rden", [P, 1])
        aff = m.sb("aff", [P, NT, EXPERTS])
        trA = m.ps("trA", [P, 4, P])
        trB = m.ps("trB", [P, 4, P])
        hrA = m.ps("hrA", [P, 4, P])
        hrB = m.ps("hrB", [P, 4, P])
        po = m.ps("po", [P, D])
        pr = m.ps("pr", [P, 512])

        const_in = m.sem("const_in")
        xr_in = m.sems("xr_in")
        x_free = m.sem("x_free")
        half_set = m.sem("half_set")
        held_dve = m.sem("held_dve")
        held_pool = m.sem("held_pool")
        gated = m.sem("gated")
        squared = m.sem("squared")
        rs_ready = m.sem("rs_ready")
        rs_tmp = m.sem("rs_tmp")
        mix_att = m.sem("mix_att")
        mix_ssm = m.sem("mix_ssm")
        tr_mm = m.sem("tr_mm")
        mA = m.sem("mA")
        mB = m.sem("mB")
        out_mm = m.sem("out_mm")
        r_ready = m.sem("r_ready")
        ln_step = m.sem("ln_step")
        rstd_tmp = m.sem("rstd_tmp")
        rstd_ready = m.sem("rstd_ready")
        scaled = m.sem("scaled")
        gained = m.sem("gained")
        h_ready = m.sem("h_ready")
        ah_ready = m.sem("ah_ready")
        h_out = m.sem("h_out")
        h_free = m.sem("h_free")
        ht_mm = m.sem("ht_mm")
        hA = m.sem("hA")
        hB = m.sem("hB")
        rt_mm = m.sem("rt_mm")
        nmx_ready = m.sem("nmx_ready")
        er_ready = m.sem("er_ready")
        aff_step = m.sem("aff_step")
        aff_ready = m.sem("aff_ready")
        at_mm = m.sem("at_mm")
        at_done = m.sem("at_done")
        block = ctx.enter_context(nc.Block())

        def tiles(eng, body):
            with eng.Fori(0, NT // 2 - 1) as tt:
                for s in range(2):
                    body(2 * tt + s, tt, s, False)
            body(NT - 2, NT // 2 - 1, 0, False)
            body(NT - 1, NT // 2 - 1, 1, True)

        @block.sync
        def _(sp):
            sp.dma_start(ident[:], dram["ident"]).then_inc(const_in, 16)
            sp.dma_start(normw[:], dram["norm_w"]).then_inc(const_in, 16)
            sp.dma_start(ln[:], dram["ln"][:, 0:2, :]).then_inc(const_in, 16)
            sp.dma_start(wr[:], dram["w_router"].rearrange("(k p) e -> p k e", p=P)).then_inc(const_in, 16)
            sp.dma_start(wout[:], dram["w_out"].rearrange("(k p) n -> p k n", p=P)).then_inc(const_in, 16)
            with sp.Fori(0, NT // 2) as tt:
                for s in range(2):
                    t = 2 * tt + s
                    sp.wait_ge(x_free, t + 1)
                    sp.dma_start(xr[s][:], dram["x"][bass.ds(t * P, P), :]).then_inc(xr_in[s], 16)

        @block.tensor
        def _(pe):
            for sem, n in ((tr_mm, 2), (out_mm, 2), (ht_mm, 2), (rt_mm, 1)):
                pe.sem_inc(sem, n)

            def project(t, s):
                pe.wait_ge(mix_att, t + 1)
                pe.wait_ge(mix_ssm, t + 1)
                pe.wait_ge(mA, t + 1)
                pe.wait_ge(mB, t + 1)
                for j in range(KD):
                    bank = trA if j < 4 else trB
                    mm = pe.transpose(bank[:, j % 4, :], mixin[s][:, P * j:P * j + P], ident[:])
                mm.then_inc(tr_mm, 1)
                pe.wait_ge(mA, 1 + t + 1)
                pe.wait_ge(mB, 1 + t + 1)
                pe.wait_ge(r_ready, t + 1)
                for n in range(2):
                    for k in range(KD):
                        mm = pe.matmul(po[:, 512 * n:512 * n + 512], mT[s][:, k, :], wout[:, k, 512 * n:512 * n + 512],
                                       start=(k == 0), stop=(k == KD - 1))
                mm.then_inc(out_mm, 1)

            def body(t, tt, s, last):
                if not last:
                    project(t + 1, 1 - s)
                pe.wait_ge(h_ready, t + 1)
                pe.wait_ge(hA, t + 1)
                pe.wait_ge(hB, t + 1)
                for j in range(KD):
                    bank = hrA if j < 4 else hrB
                    mm = pe.transpose(bank[:, j % 4, :], h[s][:, P * j:P * j + P], ident[:])
                mm.then_inc(ht_mm, 1)
                pe.wait_ge(hA, 1 + t + 1)
                pe.wait_ge(hB, 1 + t + 1)
                pe.wait_ge(aff_ready, t + 1)
                for k in range(KD):
                    mm = pe.matmul(pr[:, 0:EXPERTS], hT[:, k, :], wr[:, k, :], start=(k == 0), stop=(k == KD - 1))
                mm.then_inc(rt_mm, 1)

            pe.wait_ge(const_in, 80)
            project(0, 0)
            tiles(pe, body)
            pe.wait_ge(aff_ready, 1 + NT)
            for t in range(NT):
                bank = (trA, trB, hrA)[t // 4]
                mm = pe.transpose(bank[0:EXPERTS, t % 4, :], aff[:, t, :], ident[:])
            mm.then_inc(at_mm, 1)

        @block.scalar
        def _(act):
            for sem, n in ((squared, 1), (mB, 1), (hB, 1)):
                act.sem_inc(sem, n)

            def inputs(t, s):
                act.wait_ge(tr_mm, t + 1)
                act.copy(mixin[s][:, 0:AW], res["att"][:, bass.ds(t, 1), :].rearrange("p t n -> p (t n)")).then_inc(mix_att, 1)
                act.wait_ge(gated, t + 1)
                act.wait_ge(squared, t + 1)
                act.activation(sq[:], mixin[s][:, AW:], ACT.Square, accum_out=ss[:, s:s + 1]).then_inc(squared, 1)

            def copies(t, s):
                act.wait_ge(tr_mm, 2 + t + 1)
                act.wait_ge(out_mm, t + 1)
                act.copy(mT[s][:, 4:, :], trB[:]).then_inc(mB, 1)

            def body(t, tt, s, last):
                if not last:
                    inputs(t + 1, 1 - s)
                    copies(t + 1, 1 - s)
                act.wait_ge(h_ready, t + 1)
                act.wait_ge(h_free, t + 1)
                act.mul(ah[s][:], h[s][:], ALPHA).then_inc(ah_ready, 1)
                act.wait_ge(ht_mm, 2 + t + 1)
                act.wait_ge(rt_mm, t + 1)
                act.copy(hT[:, 4:, :], hrB[:]).then_inc(hB, 1)
                act.wait_ge(nmx_ready, t + 1)
                act.wait_ge(aff_ready, t + 1)
                act.activation(er[:], pr[:, 0:EXPERTS], ACT.Exp, bias=nmx[:], accum_out=den[:]).then_inc(er_ready, 1)

            inputs(0, 0)
            copies(0, 0)
            tiles(act, body)

        @block.gpsimd
        def _(pool):
            pool.sem_inc(h_free, 2)
            pool.memset(half[:], -0.5).then_inc(half_set, 1)
            pool.wait_ge(half_set, 1)
            pool.wait_ge(const_in, 80)

            def root(t, s):
                pool.wait_ge(squared, 1 + t + 1)
                pool.sem_inc(held_pool, 1)
                pool.tensor_scalar(rs[:, s:s + 1], ss[:, s:s + 1], 1.0 / SSM_W, RMS_EPS, ALU.mult, ALU.add).then_inc(rs_tmp, 1)
                pool.wait_ge(rs_tmp, t + 1)
                pool.tensor_tensor(rs[:, s:s + 1], rs[:, s:s + 1], half[:], ALU.pow).then_inc(rs_ready, 1)

            def body(t, tt, s, last):
                if not last:
                    root(t + 1, 1 - s)
                pool.wait_ge(ln_step, 3 * t + 3)
                pool.sem_inc(held_pool, 1)
                pool.tensor_scalar(rstd[:], mv[:, 1:2], 1.0, LN_EPS, ALU.mult, ALU.add).then_inc(rstd_tmp, 1)
                pool.wait_ge(rstd_tmp, t + 1)
                pool.tensor_tensor(rstd[:], rstd[:], half[:], ALU.pow).then_inc(rstd_ready, 1)
                pool.wait_ge(scaled, t + 1)
                pool.tensor_tensor(h[s][:], h[s][:], ln[:, 0, :], ALU.mult).then_inc(gained, 1)
                pool.wait_ge(h_ready, t + 1)
                pool.sem_inc(held_pool, 1)
                pool.dma_start(dram["h"][bass.ds(t * P, P), :], h[s][:]).then_inc(h_out, 16)
                pool.wait_ge(ah_ready, t + 1)
                pool.sem_inc(held_pool, 1)
                pool.dma_start(dram["acc"][bass.ds(t * P, P), :], ah[s][:]).then_inc(h_out, 16)
                pool.wait_ge(h_out, 32 * t + 32)
                pool.sem_inc(h_free, 1)

            root(0, 0)
            tiles(pool, body)

        @block.vector
        def _(dve):
            for sem, n in ((mA, 1), (hA, 1), (r_ready, 1), (aff_ready, 1), (x_free, 2)):
                dve.sem_inc(sem, n)

            def gate(t, s):
                dve.wait_ge(tr_mm, t + 1)
                dve.tensor_tensor(mixin[s][:, AW:], res["y"][:, bass.ds(t, 1), :].rearrange("p t n -> p (t n)"),
                                  res["z"][:, bass.ds(t, 1), :].rearrange("p t n -> p (t n)"), ALU.mult).then_inc(gated, 1)

            def norm(t, s):
                dve.wait_ge(rs_ready, t + 1)
                dve.wait_ge(squared, 1 + t + 1)
                dve.scalar_tensor_tensor(mixin[s][:, AW:], mixin[s][:, AW:], rs[:, s:s + 1], normw[:], ALU.mult, ALU.mult).then_inc(mix_ssm, 1)

            def copies(t, s):
                dve.wait_ge(tr_mm, 2 + t + 1)
                dve.wait_ge(out_mm, t + 1)
                dve.tensor_copy(mT[s][:, 0:4, :], trA[:]).then_inc(mA, 1)

            def body(t, tt, s, last):
                if not last:
                    gate(t + 1, 1 - s)
                    norm(t + 1, 1 - s)
                    copies(t + 1, 1 - s)
                dve.wait_ge(out_mm, 2 + t + 1)
                dve.wait_ge(xr_in[s], 16 * tt + 16)
                dve.scalar_tensor_tensor(r[:], xr[s][:], ALPHA, po[:], ALU.mult, ALU.add).then_inc(r_ready, 1)
                dve.wait_ge(r_ready, 1 + t + 1)
                dve.sem_inc(x_free, 1)
                dve.bn_stats(stats[:, 0], r[:, 0:512]).then_inc(ln_step, 1)
                dve.bn_stats(stats[:, 1], r[:, 512:]).then_inc(ln_step, 1)
                dve.wait_ge(ln_step, 3 * t + 2)
                dve.sem_inc(held_dve, 1)
                dve.bn_aggr(mv[:], stats[:]).then_inc(ln_step, 1)
                dve.wait_ge(rstd_ready, t + 1)
                dve.wait_ge(h_free, t + 1)
                dve.wait_ge(ht_mm, t + 1)
                dve.wait_ge(ln_step, 3 * t + 3)
                dve.tensor_scalar(h[s][:], r[:], mv[:, 0:1], rstd[:], ALU.subtract, ALU.mult).then_inc(scaled, 1)
                dve.wait_ge(gained, t + 1)
                dve.tensor_tensor(h[s][:], h[s][:], ln[:, 1, :], ALU.add).then_inc(h_ready, 1)
                dve.wait_ge(ht_mm, 2 + t + 1)
                dve.wait_ge(rt_mm, t + 1)
                dve.tensor_copy(hT[:, 0:4, :], hrA[:]).then_inc(hA, 1)
                dve.wait_ge(rt_mm, 1 + t + 1)
                dve.tensor_reduce(nmx[:], pr[:, 0:EXPERTS], mybir.AxisListType.X, ALU.max, negate=True).then_inc(nmx_ready, 1)
                dve.wait_ge(er_ready, t + 1)
                dve.reciprocal(rden[:], den[:]).then_inc(aff_step, 1)
                dve.wait_ge(aff_step, t + 1)
                dve.tensor_scalar(aff[:, bass.ds(t, 1), :], er[:].unsqueeze(1), rden[:], None, ALU.mult).then_inc(aff_ready, 1)

            dve.wait_ge(const_in, 80)
            gate(0, 0)
            norm(0, 0)
            copies(0, 0)
            tiles(dve, body)
            dve.wait_ge(at_mm, 1)
            for b, bank in enumerate((trA, trB, hrA)):
                dve.tensor_copy(res["affT"][:, 512 * b:512 * b + 512], bank[0:EXPERTS].rearrange("e j t -> e (j t)")).then_inc(at_done, 1)
            dve.wait_ge(at_done, 3)


def stage_choose(nc, dram, res):
    with ExitStack() as ctx:
        m = Mem(nc, ctx, "top")
        ident = m.sb("ident", [P, P])
        val = m.sb("val", [EXPERTS, CAP])
        idx = m.sb("idx", [EXPERTS, CAP], U32)
        idxf = m.sb("idxf", [EXPERTS, CAP])
        ps = m.ps("ps", [P, 4, EXPERTS])
        const_in = m.sem("const_in")
        step = m.sem("step")
        float_ready = m.sem("float_ready")
        tr_mm = m.sem("tr_mm")
        done = m.sem("done")
        block = ctx.enter_context(nc.Block())
        parts = ((1, 0, CAPS[1]), (0, CAPS[1], CAPS[0]))

        @block.sync
        def _(sp):
            sp.dma_start(ident[:], dram["ident"]).then_inc(const_in, 16)

        @block.vector
        def _(dve):
            n = 0
            for q, c0, cap in parts:
                work = res["affT"][:, sum(SEQS[:q]):sum(SEQS[:q]) + SEQS[q]]
                for r in range(cap // 8):
                    at = slice(c0 + 8 * r, c0 + 8 * r + 8)
                    dve.max(val[:, at], work).then_inc(step, 1)
                    dve.wait_ge(step, n + 1)
                    dve.max_index(idx[:, at], val[:, at], work).then_inc(step, 1)
                    dve.wait_ge(step, n + 2)
                    dve.match_replace(work, val[:, at], work, -1.0).then_inc(step, 1)
                    dve.wait_ge(step, n + 3)
                    n += 3
            dve.tensor_scalar(idxf[:, 0:CAPS[1]], idx[:, 0:CAPS[1]], float(SEQS[0]), None, ALU.add).then_inc(float_ready, 1)
            dve.tensor_copy(idxf[:, CAPS[1]:], idx[:, CAPS[1]:]).then_inc(float_ready, 1)
            dve.wait_ge(tr_mm, 1)
            for i, (q, c0, cap) in enumerate(parts):
                dve.tensor_copy(res["gates"][i][:], ps[0:cap, 2 * i, :]).then_inc(done, 1)
                dve.tensor_copy(res["rows"][i][:], ps[0:cap, 2 * i + 1, :]).then_inc(done, 1)
            dve.wait_ge(done, 4)

        @block.tensor
        def _(pe):
            pe.wait_ge(const_in, 16)
            pe.wait_ge(float_ready, 2)
            for i, (q, c0, cap) in enumerate(parts):
                pe.transpose(ps[0:cap, 2 * i, :], val[:, c0:c0 + cap], ident[0:EXPERTS, 0:EXPERTS])
                mm = pe.transpose(ps[0:cap, 2 * i + 1, :], idxf[:, c0:c0 + cap], ident[0:EXPERTS, 0:EXPERTS])
            mm.then_inc(tr_mm, 1)


def stage_experts(nc, dram, res):
    UNITS = EXPERTS * FCH
    NS, NP_ = CAPS[1], CAPS[0]
    with ExitStack() as ctx:
        m = Mem(nc, ctx, "moe")
        wgu = [m.sb(f"wgu{s}", [P, 2, KD, P]) for s in range(2)]
        wd = [m.sb(f"wd{s}", [P, KD, P]) for s in range(2)]
        ident = m.sb("ident", [P, P])
        grow = [m.sb("grow_s", [NS, 1], U32), m.sb("grow_p", [NP_, 1], U32)]
        srow = [m.sb("srow_s", [NS, 1], U32), m.sb("srow_p", [NP_, 1], U32)]
        xg = [m.sb("xg_s", [NS, D]), m.sb("xg_p", [NP_, D])]
        xgT = [m.sb(f"xgT{s}", [P, KD, CAP]) for s in range(2)]
        act_g = [m.sb(f"act_g{s}", [P, CAP]) for s in range(2)]
        hid = [m.sb(f"hid{s}", [P, CAP]) for s in range(2)]
        oT = m.sb("oT", [P, KD, CAP])
        og = [m.sb("og_s", [NS, D]), m.sb("og_p", [NP_, D])]
        gu = [m.ps(f"gu{s}", [P, 2, 256]) for s in range(2)]
        acc = [m.ps(f"acc{b}", [P, 2, 256]) for b in range(4)]
        trA = m.ps("trA", [P, 512])
        trB = m.ps("trB", [P, 512])

        const_in = m.sem("const_in")
        wgu_in = m.sems("wgu_in")
        wd_in = m.sems("wd_in")
        grow_ready = m.sem("grow_ready")
        xg_in = m.sem("xg_in")
        srow_ready = m.sem("srow_ready")
        scat_out = m.sem("scat_out")
        scat_free = m.sem("scat_free")
        gu_mm = m.sem("gu_mm")
        silu = m.sem("silu")
        hid_ready = m.sem("hid_ready")
        dn_mm = m.sem("dn_mm")
        accA = m.sem("accA")
        accB = m.sem("accB")
        fillA = m.sem("fillA")
        fillB = m.sem("fillB")
        drainA = m.sem("drainA")
        drainB = m.sem("drainB")
        held_pe = m.sem("held_pe")
        held_pool = m.sem("held_pool")
        block = ctx.enter_context(nc.Block())

        def experts(eng, body):
            body(0, 0, True, False)
            with eng.Fori(0, EXPERTS // 2 - 1) as ee:
                for q in range(2):
                    body(2 * ee + 1 + q, 1 - q, False, False)
            body(EXPERTS - 1, 1, False, True)

        def fills_before(e, first):
            return 2 if first else 4 * e

        @block.sync
        def _(sp):
            sp.dma_start(ident[:], dram["ident"]).then_inc(const_in, 16)
            gu_src = dram["w_gu"].rearrange("u p n -> u p n")
            with sp.Fori(0, UNITS // 2) as uu:
                for s in range(2):
                    u = 2 * uu + s
                    sp.wait_ge(gu_mm, u + 1)
                    sp.dma_start(wgu[s][:].rearrange("p a k n -> p (a k n)"),
                                 gu_src[bass.ds(u, 1), :, :].rearrange("u p n -> p (u n)")).then_inc(wgu_in[s], 16)
                    sp.wait_ge(dn_mm, u + 1)
                    sp.dma_start(wd[s][:].rearrange("p k n -> p (k n)"),
                                 dram["w_down"][bass.ds(u * P, P), :]).then_inc(wd_in[s], 16)

        @block.gpsimd
        def _(pool):
            pool.sem_inc(scat_free, 1)

            def gather(e):
                for i in range(2):
                    pool.tensor_copy(grow[i][:], res["rows"][i][:, bass.ds(e, 1)]).then_inc(grow_ready, 1)
                pool.wait_ge(grow_ready, 2 * e + 2)
                pool.sem_inc(held_pool, 1)
                for i in range(2):
                    pool.indirect_dma_start(xg[i][:], None, dram["h"], bass.IndirectOffsetOnAxis(ap=grow[i][:], axis=0)).then_inc(xg_in, 16)

            def scatter(e, n):
                for i in range(2):
                    pool.tensor_copy(srow[i][:], res["rows"][i][:, bass.ds(e, 1)]).then_inc(srow_ready, 1)
                pool.wait_ge(srow_ready, 2 * e + 2)
                pool.wait_ge(drainA, 1 + n + 2)
                pool.wait_ge(drainB, 1 + n + 2)
                pool.sem_inc(held_pool, 1)
                for i in range(2):
                    pool.indirect_dma_start(dram["acc"], bass.IndirectOffsetOnAxis(ap=srow[i][:], axis=0), og[i][:], None,
                                            compute_op=ALU.add).then_inc(scat_out, 16)
                pool.wait_ge(scat_out, 32 * e + 32)
                pool.sem_inc(scat_free, 1)

            def body(e, q, first, last):
                n = fills_before(e, first)
                if not last:
                    pool.wait_ge(fillA, n + 2)
                    pool.wait_ge(fillB, n + 2)
                    n = n + 2
                if not (last or first):
                    gather_next(e)
                elif first:
                    gather(2)
                if not first:
                    scatter(e - 1, n)

            def gather_next(e):
                gather(e + 2)

            gather(0)
            pool.wait_ge(fillA, 2)
            pool.wait_ge(fillB, 2)
            gather(1)
            body(0, 0, True, False)
            with pool.Fori(0, EXPERTS // 2 - 2) as ee:
                for q in range(2):
                    body(2 * ee + 1 + q, 1 - q, False, False)
            body(EXPERTS - 3, 1, False, False)
            pool.wait_ge(fillA, 4 * (EXPERTS - 2) + 2)
            pool.wait_ge(fillB, 4 * (EXPERTS - 2) + 2)
            scatter(EXPERTS - 3, 4 * (EXPERTS - 2) + 2)
            scatter(EXPERTS - 2, 4 * (EXPERTS - 1))
            scatter(EXPERTS - 1, 4 * (EXPERTS - 1) + 2)

        @block.tensor
        def _(pe):
            for sem, n in ((gu_mm, 2), (dn_mm, 2)):
                pe.sem_inc(sem, n)

            def fill_tokens(e, q, b, n):
                bank, drain, fill = ((trA, drainA, fillA), (trB, drainB, fillB))[b % 2]
                if b == 0:
                    pe.wait_ge(xg_in, 32 * e + 32)
                pe.wait_ge(drain, n + 1)
                for j in range(2):
                    k = 2 * b + j
                    pe.transpose(bank[:, CAP * j:CAP * j + NS], xg[0][:, P * k:P * k + P], ident[:])
                    mm = pe.transpose(bank[:, CAP * j + NS:CAP * j + CAP], xg[1][:, P * k:P * k + P], ident[0:NP_, 0:NP_])
                mm.then_inc(fill, 1)

            def fill_rows(e, b, n):
                bank, drain, fill = ((trA, drainA, fillA), (trB, drainB, fillB))[b % 2]
                if b == 0:
                    pe.wait_ge(accA, 2 + 2 * e + 2)
                    pe.wait_ge(accB, 2 + 2 * e + 2)
                pe.wait_ge(drain, n + 1)
                pe.sem_inc(held_pe, 1)
                lo, hi = (0, NS) if b < 2 else (NS, CAP)
                for j in range(4):
                    mm = pe.transpose(bank[0:hi - lo, P * j:P * j + P], oT[:, 4 * (b % 2) + j, lo:hi], ident[:])
                mm.then_inc(fill, 1)

            def gate_up(u, uu, s, q):
                pe.wait_ge(wgu_in[s], 16 * uu + 16)
                pe.wait_ge(hid_ready, u + 1)
                for a in range(2):
                    for k in range(KD):
                        mm = pe.matmul(gu[s][:, a, 0:CAP], wgu[s][:, a, k, :], xgT[q][:, k, :], start=(k == 0), stop=(k == KD - 1))
                mm.then_inc(gu_mm, 1)

            def down(u, uu, s, first, last):
                pe.wait_ge(wd_in[s], 16 * uu + 16)
                pe.wait_ge(hid_ready, 2 + u + 1)
                for j in range(KD):
                    mm = pe.matmul(acc[j // 2][:, j % 2, 0:CAP], wd[s][:, j, :], hid[s][:], start=(first and j % 2 == 0),
                                   stop=last, skip_group_check=True)
                mm.then_inc(dn_mm, 1)

            def body(e, q, first, last):
                u, uu = FCH * e, FCH // 2 * e
                n = fills_before(e, first)
                if not last:
                    fill_tokens(e + 1, 1 - q, 0, n)
                    fill_tokens(e + 1, 1 - q, 1, n)
                gate_up(u + 1, uu, 1, q)
                pe.wait_ge(accA, 2 * e + 2)
                pe.wait_ge(accB, 2 * e + 2)
                down(u, uu, 0, True, False)
                if not last:
                    fill_tokens(e + 1, 1 - q, 2, n + 1)
                    fill_tokens(e + 1, 1 - q, 3, n + 1)
                    n = n + 2
                gate_up(u + 2, uu + 1, 0, q)
                if not first:
                    fill_rows(e - 1, 0, n)
                    fill_rows(e - 1, 1, n)
                down(u + 1, uu, 1, False, False)
                gate_up(u + 3, uu + 1, 1, q)
                if not first:
                    fill_rows(e - 1, 2, n + 1)
                    fill_rows(e - 1, 3, n + 1)
                down(u + 2, uu + 1, 0, False, False)
                with pe.Fori(2, FCH // 2) as ff:
                    gate_up(u + 2 * ff, uu + ff, 0, q)
                    down(u + 2 * ff - 1, uu + ff - 1, 1, False, False)
                    gate_up(u + 2 * ff + 1, uu + ff, 1, q)
                    down(u + 2 * ff, uu + ff, 0, False, False)
                if not last:
                    pe.wait_ge(drainA, 1 + n)
                    pe.wait_ge(drainB, 1 + n)
                    gate_up(u + FCH, uu + FCH // 2, 0, 1 - q)
                down(u + FCH - 1, uu + FCH // 2 - 1, 1, False, True)

            pe.wait_ge(const_in, 16)
            fill_tokens(0, 0, 0, 0)
            fill_tokens(0, 0, 1, 0)
            fill_tokens(0, 0, 2, 1)
            fill_tokens(0, 0, 3, 1)
            pe.wait_ge(drainA, 1 + 2)
            pe.wait_ge(drainB, 1 + 2)
            gate_up(0, 0, 0, 0)
            experts(pe, body)
            for b in range(4):
                fill_rows(EXPERTS - 1, b, 4 * (EXPERTS - 1) + 2 + b // 2)

        def evacuate(eng, mine, copy, scale, fill, drain, accd, bank, silu_unit):

            def tokens(e, q, n):
                for b in range(2):
                    eng.wait_ge(fill, n + b + 1)
                    k = 4 * b + 2 * mine
                    copy(xgT[q][:, k:k + 2, :], bank[:, 0:2 * CAP].rearrange("p (j c) -> p j c", j=2)).then_inc(drain, 1)

            def rows(e, n):
                eng.wait_ge(scat_free, e + 1)
                for i in range(2):
                    eng.wait_ge(fill, n + i + 1)
                    c = CAPS[1 - i]
                    scale(og[i][:, 512 * mine:512 * mine + 512], bank[0:c, :], res["gates"][i][:, bass.ds(e, 1)]).then_inc(drain, 1)

            def results(e, n):
                eng.wait_ge(dn_mm, 2 + FCH * e + FCH)
                for b in range(2):
                    copy(oT[:, 4 * mine + 2 * b:4 * mine + 2 * b + 2, :], acc[2 * mine + b][:, :, 0:CAP]).then_inc(accd, 1)

            def body(e, q, first, last):
                u = FCH * e
                n = fills_before(e, first)
                if not last:
                    tokens(e + 1, 1 - q, n)
                    n = n + 2
                silu_unit(u + 1, 1)
                silu_unit(u + 2, 0)
                if not first:
                    rows(e - 1, n)
                silu_unit(u + 3, 1)
                with eng.Fori(2, FCH // 2) as ff:
                    silu_unit(u + 2 * ff, 0)
                    silu_unit(u + 2 * ff + 1, 1)
                if not last:
                    silu_unit(u + FCH, 0)
                results(e, n)

            tokens(0, 0, 0)
            silu_unit(0, 0)
            experts(eng, body)
            rows(EXPERTS - 1, 4 * (EXPERTS - 1) + 2)

        @block.scalar
        def _(act):
            act.sem_inc(accB, 2)
            act.sem_inc(drainB, 1)

            def silu_unit(u, s):
                act.wait_ge(gu_mm, 2 + u + 1)
                act.wait_ge(hid_ready, u + 1)
                act.activation(act_g[s][:], gu[s][:, 0, 0:CAP], ACT.Silu).then_inc(silu, 1)

            evacuate(act, 1, lambda o, i: act.copy(o, i), lambda o, i, g: act.mul(o, i, g), fillB, drainB, accB, trB, silu_unit)

        @block.vector
        def _(dve):
            dve.sem_inc(accA, 2)
            dve.sem_inc(drainA, 1)
            dve.sem_inc(hid_ready, 2)

            def times_up(u, s):
                dve.wait_ge(silu, u + 1)
                dve.wait_ge(dn_mm, u + 1)
                dve.tensor_tensor(hid[s][:], act_g[s][:], gu[s][:, 1, 0:CAP], ALU.mult).then_inc(hid_ready, 1)

            evacuate(dve, 0, lambda o, i: dve.tensor_copy(o, i), lambda o, i, g: dve.tensor_scalar(o, i, g, None, ALU.mult),
                     fillA, drainA, accA, trA, times_up)


def stage_finish(nc, dram, res):
    with ExitStack() as ctx:
        m = Mem(nc, ctx, "fin")
        ln = m.sb("ln", [P, 2, D])
        half = m.sb("half", [P, 1])
        r = [m.sb(f"r{s}", [P, D]) for s in range(2)]
        o = [m.sb(f"o{s}", [P, D]) for s in range(2)]
        stats = m.sb("stats", [P, 2, 6])
        mv = [m.sb(f"mv{s}", [P, 2]) for s in range(2)]
        rstd = [m.sb(f"rstd{s}", [P, 1]) for s in range(2)]
        const_in = m.sem("const_in")
        half_set = m.sem("half_set")
        held_dve = m.sem("held_dve")
        held_pool = m.sem("held_pool")
        r_in = m.sems("r_in")
        ln_step = m.sem("ln_step")
        rstd_tmp = m.sem("rstd_tmp")
        rstd_ready = m.sem("rstd_ready")
        scaled = m.sem("scaled")
        gained = m.sem("gained")
        o_ready = m.sem("o_ready")
        o_out = m.sems("o_out")
        block = ctx.enter_context(nc.Block())

        @block.sync
        def _(sp):
            sp.dma_start(ln[:], dram["ln"][:, 2:4, :]).then_inc(const_in, 16)
            with sp.Fori(0, NT // 2) as tt:
                for s in range(2):
                    t = 2 * tt + s
                    sp.wait_ge(scaled, t + 1)
                    sp.dma_start(r[s][:], dram["acc"][bass.ds(t * P, P), :]).then_inc(r_in[s], 16)

        @block.scalar
        def _(act):
            for s in range(2):
                act.sem_inc(o_out[s], 16)
            with act.Fori(0, NT // 2) as tt:
                for s in range(2):
                    t = 2 * tt + s
                    act.wait_ge(o_ready, t + 1)
                    act.dma_start(dram["out"][bass.ds(t * P, P), :], o[s][:]).then_inc(o_out[s], 16)
            for s in range(2):
                act.wait_ge(o_out[s], 16 + 16 * (NT // 2))

        @block.gpsimd
        def _(pool):
            pool.memset(half[:], -0.5).then_inc(half_set, 1)
            pool.wait_ge(half_set, 1)
            pool.wait_ge(const_in, 16)
            with pool.Fori(0, NT // 2) as tt:
                for s in range(2):
                    t = 2 * tt + s
                    pool.wait_ge(ln_step, 3 * t + 3)
                    pool.sem_inc(held_pool, 1)
                    pool.tensor_scalar(rstd[s][:], mv[s][:, 1:2], 1.0, LN_EPS, ALU.mult, ALU.add).then_inc(rstd_tmp, 1)
                    pool.wait_ge(rstd_tmp, t + 1)
                    pool.tensor_tensor(rstd[s][:], rstd[s][:], half[:], ALU.pow).then_inc(rstd_ready, 1)

        @block.vector
        def _(dve):
            dve.sem_inc(scaled, 2)
            dve.wait_ge(const_in, 16)

            def measure(t, tt, s):
                dve.wait_ge(r_in[s], 16 * tt + 16)
                dve.bn_stats(stats[:, 0], r[s][:, 0:512]).then_inc(ln_step, 1)
                dve.bn_stats(stats[:, 1], r[s][:, 512:]).then_inc(ln_step, 1)
                dve.wait_ge(ln_step, 3 * t + 2)
                dve.sem_inc(held_dve, 1)
                dve.bn_aggr(mv[s][:], stats[:]).then_inc(ln_step, 1)
                dve.wait_ge(ln_step, 3 * t + 3)

            def body(t, tt, s, last):
                if not last:
                    measure(t + 1, tt + s, 1 - s)
                dve.wait_ge(rstd_ready, t + 1)
                dve.wait_ge(o_out[s], 16 * tt + 16)
                dve.tensor_scalar(o[s][:], r[s][:], mv[s][:, 0:1], rstd[s][:], ALU.subtract, ALU.mult).then_inc(scaled, 1)
                dve.wait_ge(scaled, 2 + t + 1)
                dve.tensor_tensor(o[s][:], o[s][:], ln[:, 0, :], ALU.mult).then_inc(gained, 1)
                dve.wait_ge(gained, t + 1)
                dve.tensor_tensor(o[s][:], o[s][:], ln[:, 1, :], ALU.add).then_inc(o_ready, 1)

            measure(0, 0, 0)
            with dve.Fori(0, NT // 2 - 1) as tt:
                for s in range(2):
                    body(2 * tt + s, tt, s, False)
            body(NT - 2, NT // 2 - 1, 0, False)
            body(NT - 1, NT // 2 - 1, 1, True)


def residents_first(nc, ctx):
    m = Mem(nc, ctx, "res")
    return {
        "z": m.sb("z", [P, NT, 512]),
        "dt": m.sb("dt", [P, NT, NDT]),
    }


def residents_later(nc, ctx):
    m = Mem(nc, ctx, "res")
    return {
        "affT": m.sb("affT", [EXPERTS, TOK]),
        "gates": [m.sb("gates_s", [CAPS[1], EXPERTS]), m.sb("gates_p", [CAPS[0], EXPERTS])],
        "rows": [m.sb("rows_s", [CAPS[1], EXPERTS], U32), m.sb("rows_p", [CAPS[0], EXPERTS], U32)],
        "att": m.sb("att", [P, NT, AW]),
        "y": m.sb("y", [P, NT, SSM_W]),
    }


def layouts(x_prompt, x_sample, w_in, conv_w, conv_b, dt_bias, a_log, d_skip, ssm_norm_w, w_out,
            ln1_g, ln1_b, w_router, w_gate, w_up, w_down, ln2_g, ln2_b):
    a = {}
    x = np.concatenate([np.asarray(x_prompt)[0], np.asarray(x_sample)[0]], axis=0)
    a["x"] = np.ascontiguousarray(x)
    a["xT"] = np.ascontiguousarray(x.T)
    a["w_in"] = np.asarray(w_in)[0]
    taps = np.concatenate([np.asarray(conv_w)[0], np.asarray(conv_b)[0][None]], axis=0)
    a["conv"] = np.ascontiguousarray(taps.T.reshape(NCH, P, CONV_K + 1).transpose(1, 0, 2))
    rows = lambda v: np.ascontiguousarray(np.broadcast_to(np.asarray(v).reshape(1, -1), (P, np.asarray(v).size)))
    a["dt_bias"] = rows(dt_bias)
    a["a_log"] = rows(a_log)
    a["d_skip"] = rows(d_skip)
    a["norm_w"] = rows(ssm_norm_w)
    a["ln"] = np.ascontiguousarray(np.stack([rows(ln1_g), rows(ln1_b), rows(ln2_g), rows(ln2_b)], axis=1))
    a["w_out"] = np.asarray(w_out)[0]
    a["w_router"] = np.asarray(w_router)[0]
    gu = np.stack([np.asarray(w_gate)[0], np.asarray(w_up)[0]])
    gu = gu.reshape(2, EXPERTS, KD, P, FCH, P).transpose(1, 4, 3, 0, 2, 5)
    a["w_gu"] = np.ascontiguousarray(gu).reshape(EXPERTS * FCH, P, 2 * KD * P)
    a["w_down"] = np.asarray(w_down)[0].reshape(EXPERTS * FF, D)
    pos = np.concatenate([np.arange(s) for s in SEQS]).astype(np.float32)
    inv = np.float32(500000.0) ** (-np.arange(HALF_ROT, dtype=np.float32) * np.float32(2.0) / np.float32(ROT))
    ang = (pos[:, None] * inv.astype(np.float32)[None, :]).astype(np.float32)
    cs = np.stack([np.cos(ang), np.sin(ang)], axis=1).astype(np.float32)
    a["rope"] = np.ascontiguousarray(cs.reshape(NT, P, 2, HALF_ROT).transpose(1, 0, 2, 3))
    delta = np.abs(np.arange(MASK_W)[None, :] - MASK_0 - np.arange(P)[:, None])
    times = sum(((delta % dil == 0) & (delta <= window // 2)).astype(np.float64) for window, dil in PATTERNS)
    a["mask"] = np.where(times > 0, np.log(np.maximum(times, 1)), NEG).astype(np.float32)
    i = np.arange(P)
    lt, le = i[:, None] < i[None, :], i[:, None] <= i[None, :]
    a["tri"] = np.ascontiguousarray(np.stack([lt, le, lt.T, le.T, lt | lt.T | le], axis=1).astype(np.float32))
    a["ident"] = np.eye(P, dtype=np.float32)
    return a


def build(nc, dram):
    with ExitStack() as ctx:
        res = residents_first(nc, ctx)
        stage_project(nc, dram, res)
        res.update(residents_later(nc, ctx))
        stage_attend(nc, dram, res)
        stage_ssd(nc, dram, res)
        stage_mix(nc, dram, res)
        stage_choose(nc, dram, res)
        stage_experts(nc, dram, res)
        stage_finish(nc, dram, res)


def kernel(**inputs):
    import concourse.bacc as bacc
    from concourse.bass_utils import run_bass_kernel_spmd

    nc = bacc.Bacc("TRN2", target_bir_lowering=False, num_devices=1)
    arrays = layouts(**inputs)
    dram = {name: nc.dram_tensor(f"in_{name}", a.shape, mybir.dt.from_np(a.dtype), kind="ExternalInput").ap()
            for name, a in arrays.items()}
    scratch = {"v": [TOK, AW], "qkT": [2 * AW, TOK], "xbc": [CONV_CH, TOK], "h": [TOK, D], "acc": [TOK, D]}
    for name, shape in scratch.items():
        dram[name] = nc.dram_tensor(f"tmp_{name}", shape, F32, kind="Internal").ap()
    dram["out"] = nc.dram_tensor("out", [TOK, D], F32, kind="ExternalOutput").ap()
    build(nc, dram)
    r = run_bass_kernel_spmd(nc, [{f"in_{k}": v for k, v in arrays.items()}], core_ids=[0])
    out = np.asarray(r.results[0]["out"])
    return out[None, :SEQS[0]], out[None, SEQS[0]:]
```

```python
from contextlib import ExitStack

import numpy as np
import concourse.bass as bass
from concourse import mybir

F32 = mybir.dt.float32
F32R = mybir.dt.float32r
U32 = mybir.dt.uint32
ALU = mybir.AluOpType
ACT = mybir.ActivationFunctionType

P = 128
SEQS = (512, 1024)
TOK = sum(SEQS)
NT = TOK // P
FIRST_TILE = (0, SEQS[0] // P)
D = 1024
KD = D // P
HEADS, HD = 8, 64
AW = HEADS * HD
ROT = HD // 4
HALF_ROT = ROT // 2
GROUPS, STATE = 2, 128
SSM_W = 512
CONV_CH = SSM_W + 2 * GROUPS * STATE
NCH = CONV_CH // P
CONV_K = 5
NDT = 16
TM_W = 4 * 512 + NDT
EXPERTS = 16
CAPS = tuple(2 * s // EXPERTS for s in SEQS)
CAP = sum(CAPS)
FF = 2816
FCH = FF // P
LN_EPS = 1e-5
RMS_EPS = 1e-5
ALPHA = 2.0 ** 0.25
PATTERNS = ((128, 1), (512, 4), (2048, 16))
MASK_W = 2 * SEQS[1] - P
MASK_0 = SEQS[1] - P
NEG = -1.0e30


class Mem:

    def __init__(self, nc, ctx, tag):
        self.nc, self.ctx, self.tag = nc, ctx, tag

    def sb(self, name, shape, dt=F32):
        return self.ctx.enter_context(self.nc.sbuf_tensor(f"{self.tag}_{name}", shape, dt))

    def ps(self, name, shape, dt=F32):
        return self.ctx.enter_context(self.nc.psum_tensor(f"{self.tag}_{name}", shape, dt))

    def sem(self, name):
        return self.ctx.enter_context(self.nc.semaphore(f"{self.tag}_{name}"))

    def sems(self, name, n=2):
        return [self.sem(f"{name}{i}") for i in range(n)]


def stage_project(nc, dram, res):
    with ExitStack() as ctx:
        m = Mem(nc, ctx, "prj")
        xT = m.sb("xT", [P, KD, TOK])
        wtm = m.sb("wtm", [P, KD, TM_W])
        wfm = [m.sb(f"wfm{s}", [P, KD, P]) for s in range(2)]
        RW = TOK + 4 * (CONV_K // 2)
        CW = RW - (CONV_K - 1)
        raw = [m.sb(f"raw{s}", [P, RW]) for s in range(2)]
        acc = m.sb("acc", [P, CW])
        xbc = [m.sb(f"xbc{s}", [P, TOK]) for s in range(2)]
        convw = m.sb("convw", [P, NCH, CONV_K + 1])
        xt = [m.sb(f"xt{s}", [P, KD, P]) for s in range(2)]
        qk = [m.sb(f"qk{s}", [P, 2 * HEADS, HD]) for s in range(2)]
        rope = m.sb("rope", [P, 4, 2 * HEADS, HALF_ROT])
        vt = [m.sb(f"vt{s}", [P, AW]) for s in range(2)]
        qkT = [m.sb(f"qkT{s}", [P, KD, P]) for s in range(2)]
        cs = m.sb("cs", [P, NT, 2, HALF_ROT])
        ident = m.sb("ident", [P, P])
        ps = m.ps("ps", [P, 8, 512])

        const_in = m.sem("const_in")
        x_in = m.sems("x_in", 3)
        wtm_in = m.sem("wtm_in")
        wfm_in = m.sems("wfm_in")
        fm_mm = m.sem("fm_mm")
        raw_ready = m.sem("raw_ready")
        margins = m.sem("margins")
        conv_step = m.sem("conv_step")
        xbc_ready = m.sem("xbc_ready")
        xbc_out = m.sem("xbc_out")
        xbc_free = m.sem("xbc_free")
        xt_in = m.sems("xt_in")
        tm_mm = m.sem("tm_mm")
        qk_ready = m.sem("qk_ready")
        v_ready = m.sem("v_ready")
        z_ready = m.sem("z_ready")
        dt_ready = m.sem("dt_ready")
        rope_step = m.sem("rope_step")
        tr_mm = m.sem("tr_mm")
        qkT_ready = m.sem("qkT_ready")
        vq_out = m.sem("vq_out")
        vq_free = m.sem("vq_free")
        wfm_src = dram["w_in"][:, 4 * 512:4 * 512 + CONV_CH].rearrange("(k p) (c n) -> p k c n", p=P, n=P)
        w_src = dram["w_in"].rearrange("(k p) n -> p k n", p=P)
        xT_src = dram["xT"].rearrange("(k p) t -> p k t", p=P)
        block = ctx.enter_context(nc.Block())
        ROPE_STEPS = 6

        @block.sync
        def _(sp):
            for g in range(3):
                if g == 0:
                    sp.dma_start(wfm[0][:], wfm_src[:, :, 0, :]).then_inc(wfm_in[0], 16)
                sp.dma_start(xT[:, :, 512 * g:512 * g + 512], xT_src[:, :, 512 * g:512 * g + 512]).then_inc(x_in[g], 16)
            sp.dma_start(wfm[1][:], wfm_src[:, :, 1, :]).then_inc(wfm_in[1], 16)
            with sp.Fori(1, NCH // 2) as cc:
                for s in range(2):
                    c = 2 * cc + s
                    sp.wait_ge(fm_mm, 3 * c + 3)
                    sp.dma_start(wfm[s][:], wfm_src[:, :, bass.ds(c, 1), :].rearrange("p k c n -> p k (c n)")).then_inc(wfm_in[s], 16)
            with sp.Fori(0, NT // 2) as tt:
                for s in range(2):
                    t = 2 * tt + s
                    sp.wait_ge(tm_mm, 5 * t + 5)
                    sp.dma_start(xt[s][:], xT_src[:, :, bass.ds(t * P, P)]).then_inc(xt_in[s], 16)

        @block.tensor
        def _(pe):
            pe.sem_inc(fm_mm, 6)
            pe.sem_inc(tm_mm, 10)
            pe.sem_inc(tr_mm, 2)
            for g in range(3):
                pe.wait_ge(x_in[g], 16)
            with pe.Fori(0, NCH // 2) as cc:
                for s in range(2):
                    c = 2 * cc + s
                    pe.wait_ge(wfm_in[s], 16 * cc + 16)
                    for g in range(3):
                        pe.wait_ge(raw_ready, 3 * c + g + 1)
                        for k in range(KD):
                            mm = pe.matmul(ps[:, 3 * s + g, :], wfm[s][:, k, :], xT[:, k, 512 * g:512 * g + 512],
                                           start=(k == 0), stop=(k == KD - 1))
                        mm.then_inc(fm_mm, 1)
            pe.wait_ge(raw_ready, 6 + 3 * NCH)
            pe.wait_ge(wtm_in, 32)
            pe.wait_ge(const_in, 48)
            with pe.Fori(0, NT // 2) as tt:
                for s in range(2):
                    t = 2 * tt + s
                    pe.wait_ge(xt_in[s], 16 * tt + 16)
                    for n in range(5):
                        if n < 2:
                            pe.wait_ge(qk_ready, 2 * t + n + 1)
                        if n == 2:
                            pe.wait_ge(v_ready, t + 1)
                        if n == 3:
                            pe.wait_ge(z_ready, t + 1)
                        if n == 4:
                            pe.wait_ge(dt_ready, t + 1)
                        w = 512 if n < 4 else NDT
                        for k in range(KD):
                            mm = pe.matmul(ps[:, n, 0:w], xt[s][:, k, :], wtm[:, k, 512 * n:512 * n + w],
                                           start=(k == 0), stop=(k == KD - 1))
                        mm.then_inc(tm_mm, 1)
                    pe.wait_ge(rope_step, ROPE_STEPS * t + ROPE_STEPS)
                    pe.wait_ge(qkT_ready, 2 * t + 2)
                    for j in range(KD):
                        src = qk[s][:, 2 * j:2 * j + 2, :].rearrange("p a e -> p (a e)")
                        mm = pe.transpose(ps[:, 6 + j // 4, P * (j % 4):P * (j % 4) + P], src, ident[:])
                    mm.then_inc(tr_mm, 1)

        @block.scalar
        def _(act):
            act.sem_inc(raw_ready, 6)
            act.sem_inc(xbc_ready, 1)
            act.sem_inc(qk_ready, 2)
            act.sem_inc(v_ready, 1)
            act.sem_inc(z_ready, 1)
            act.dma_start(wtm[:, :, 0:2048], w_src[:, :, 0:2048]).then_inc(wtm_in, 16)
            act.dma_start(wtm[:, :, 2048:TM_W], w_src[:, :, 2048 + CONV_CH:]).then_inc(wtm_in, 16)
            act.wait_ge(margins, 2)
            starts = (2, 2 + SEQS[0] + 4, 2 + SEQS[0] + 4 + 512)

            def silu_out(c, cc, s):
                act.wait_ge(conv_step, 10 + 5 * c + 5)
                act.wait_ge(xbc_free, c + 1)
                act.activation(xbc[s][:, 0:SEQS[0]], acc[:, 0:SEQS[0]], ACT.Silu)
                act.activation(xbc[s][:, SEQS[0]:], acc[:, SEQS[0] + 4:], ACT.Silu).then_inc(xbc_ready, 1)

            with act.Fori(0, NCH // 2) as cc:
                for s in range(2):
                    c = 2 * cc + s
                    act.wait_ge(conv_step, 5 * c + 5)
                    for g in range(3):
                        act.wait_ge(fm_mm, 6 + 3 * c + g + 1)
                        act.copy(raw[s][:, starts[g]:starts[g] + 512], ps[:, 3 * s + g, :]).then_inc(raw_ready, 1)
                    silu_out(c, cc, s)
            with act.Fori(0, NT // 2) as tt:
                for s in range(2):
                    t = 2 * tt + s
                    act.wait_ge(tr_mm, t + 1)
                    act.wait_ge(tm_mm, 10 + 5 * t + 1)
                    act.mul(qk[s][:, 0:HEADS, :], ps[:, 0, :].rearrange("p (h e) -> p h e", e=HD), HD ** -0.5).then_inc(qk_ready, 1)
                    act.wait_ge(tm_mm, 10 + 5 * t + 2)
                    act.copy(qk[s][:, HEADS:, :], ps[:, 1, :].rearrange("p (h e) -> p h e", e=HD)).then_inc(qk_ready, 1)
                    act.wait_ge(tm_mm, 10 + 5 * t + 3)
                    act.wait_ge(vq_free, t + 1)
                    act.copy(vt[s][:], ps[:, 2, :]).then_inc(v_ready, 1)
                    act.wait_ge(tm_mm, 10 + 5 * t + 4)
                    act.activation(res["z"][:, bass.ds(t, 1), :], ps[:, 3:4, :], ACT.Silu).then_inc(z_ready, 1)

        @block.vector
        def _(dve):
            dve.sem_inc(conv_step, 10)
            dve.sem_inc(dt_ready, 1)
            dve.sem_inc(qkT_ready, 2)
            for s in range(2):
                dve.memset(raw[s][:, 0:2], 0.0)
                dve.memset(raw[s][:, 2 + SEQS[0]:2 + SEQS[0] + 4], 0.0)
                dve.memset(raw[s][:, RW - 2:RW], 0.0).then_inc(margins, 1)
            dve.wait_ge(margins, 2)
            dve.wait_ge(const_in, 48)
            with dve.Fori(0, NCH // 2) as cc:
                for s in range(2):
                    c = 2 * cc + s
                    dve.wait_ge(raw_ready, 6 + 3 * c + 3)
                    dve.wait_ge(xbc_ready, c + 1)
                    dve.tensor_scalar(acc[:], raw[s][:, 0:CW], convw[:, bass.ds(c, 1), 0], convw[:, bass.ds(c, 1), CONV_K],
                                      ALU.mult, ALU.add).then_inc(conv_step, 1)
                    for k in range(1, CONV_K):
                        dve.wait_ge(conv_step, 10 + 5 * c + k)
                        dve.scalar_tensor_tensor(acc[:], raw[s][:, k:k + CW], convw[:, bass.ds(c, 1), k], acc[:],
                                                 ALU.mult, ALU.add).then_inc(conv_step, 1)
            with dve.Fori(0, NT // 2) as tt:
                for s in range(2):
                    t = 2 * tt + s
                    n0 = ROPE_STEPS * t
                    dve.wait_ge(qk_ready, 2 + 2 * t + 2)
                    t1 = qk[s][:, :, 0:HALF_ROT]
                    t2 = qk[s][:, :, HALF_ROT:ROT]
                    cos = cs[:, bass.ds(t, 1), 0, :].broadcast_to([P, 2 * HEADS, HALF_ROT])
                    sin = cs[:, bass.ds(t, 1), 1, :].broadcast_to([P, 2 * HEADS, HALF_ROT])
                    for n, (a, b) in enumerate(((t1, cos), (t2, sin), (t2, cos), (t1, sin))):
                        dve.tensor_tensor(rope[:, n], a, b, ALU.mult).then_inc(rope_step, 1)
                    dve.wait_ge(rope_step, n0 + 4)
                    dve.tensor_tensor(t1, rope[:, 0], rope[:, 1], ALU.subtract).then_inc(rope_step, 1)
                    dve.tensor_tensor(t2, rope[:, 2], rope[:, 3], ALU.add).then_inc(rope_step, 1)
                    dve.wait_ge(rope_step, n0 + 6)
                    dve.wait_ge(tm_mm, 10 + 5 * t + 5)
                    dve.tensor_copy(res["dt"][:, bass.ds(t, 1), :], ps[:, 4:5, 0:NDT]).then_inc(dt_ready, 1)
                    dve.wait_ge(tr_mm, 2 + t + 1)
                    dve.wait_ge(vq_free, t + 1)
                    for b in range(2):
                        dve.tensor_copy(qkT[s][:, 4 * b:4 * b + 4, :],
                                        ps[:, 6 + b, :].rearrange("p (j t) -> p j t", j=4)).then_inc(qkT_ready, 1)

        @block.gpsimd
        def _(pool):
            pool.sem_inc(xbc_free, 2)
            pool.sem_inc(vq_free, 2)
            pool.dma_start(cs[:], dram["rope"]).then_inc(const_in, 16)
            pool.dma_start(convw[:], dram["conv"]).then_inc(const_in, 16)
            pool.dma_start(ident[:], dram["ident"]).then_inc(const_in, 16)
            with pool.Fori(0, NCH // 2) as cc:
                for s in range(2):
                    c = 2 * cc + s
                    pool.wait_ge(xbc_ready, 1 + c + 1)
                    dst = dram["xbc"][bass.ds(c * P, P), :]
                    pool.dma_start(dst, xbc[s][:]).then_inc(xbc_out, 16)
                    pool.wait_ge(xbc_out, 16 * c + 16)
                    pool.sem_inc(xbc_free, 1)
            with pool.Fori(0, NT // 2) as tt:
                for s in range(2):
                    t = 2 * tt + s
                    pool.wait_ge(v_ready, 1 + t + 1)
                    pool.dma_start(dram["v"][bass.ds(t * P, P), :], vt[s][:]).then_inc(vq_out, 16)
                    pool.wait_ge(qkT_ready, 2 + 2 * t + 2)
                    pool.dma_start(dram["qkT"][:, bass.ds(t * P, P)].rearrange("(k p) t -> p k t", p=P), qkT[s][:]).then_inc(vq_out, 16)
                    pool.wait_ge(vq_out, 32 * t + 32)
                    pool.sem_inc(vq_free, 1)
            pool.wait_ge(dt_ready, 1 + NT)
            pool.wait_ge(z_ready, 1 + NT)


def stage_attend(nc, dram, res):
    ITEMS = NT
    PV0 = 2 * ITEMS
    first_item = (0, SEQS[0] // P)

    def shape_of(j):
        return (0, SEQS[0], j) if j < first_item[1] else (SEQS[0], SEQS[1], j - first_item[1])

    with ExitStack() as ctx:
        m = Mem(nc, ctx, "att")
        qT = [m.sb(f"qT{s}", [HD, TOK]) for s in range(2)]
        kT = [m.sb(f"kT{s}", [HD, TOK]) for s in range(2)]
        v = [m.sb(f"v{s}", [P, NT, HD]) for s in range(2)]
        mask = m.sb("mask", [P, MASK_W])
        ident = m.sb("ident", [P, P])
        neg = [m.sb(f"neg{s}", [P, SEQS[1]]) for s in range(2)]
        negmax = m.sb("negmax", [P, 2])
        probs = [m.sb(f"probs{s}", [P, SEQS[1]]) for s in range(2)]
        pT = [m.sb(f"pT{s}", [P, 2, 4, P]) for s in range(2)]
        den = m.sb("den", [P, 4])
        rden = m.sb("rden", [P, 2])
        sc = [m.ps(f"sc{s}", [P, SEQS[1]]) for s in range(2)]
        trA = m.ps("trA", [P, 4, P])
        trB = m.ps("trB", [P, 4, P])
        o = [m.ps(f"o{s}", [P, 512]) for s in range(2)]

        const_in = m.sem("const_in")
        qkv_in = m.sems("qkv_in")
        score_mm = m.sem("score_mm")
        masked = m.sem("masked")
        exp_done = m.sem("exp_done")
        tr_mm = m.sem("tr_mm")
        copyA = m.sem("copyA")
        copyB = m.sem("copyB")
        pv_mm = m.sem("pv_mm")
        recip = m.sem("recip")
        normed = m.sem("normed")
        held = m.sem("held")
        block = ctx.enter_context(nc.Block())

        def heads(eng, body):
            with eng.Fori(0, HEADS // 2 - 1) as hh:
                for s in range(2):
                    body(2 * hh + s, hh, s, False)
            body(HEADS - 2, HEADS // 2 - 1, 0, False)
            body(HEADS - 1, HEADS // 2 - 1, 1, True)

        @block.sync
        def _(sp):
            sp.dma_start(mask[:], dram["mask"]).then_inc(const_in, 16)
            sp.dma_start(ident[:], dram["ident"]).then_inc(const_in, 16)
            with sp.Fori(0, HEADS // 2) as hh:
                for s in range(2):
                    h = 2 * hh + s
                    sp.wait_ge(pv_mm, ITEMS * h + ITEMS)
                    sp.dma_start(qT[s][:], dram["qkT"][bass.ds(h * HD, HD), :]).then_inc(qkv_in[s], 16)
                    sp.dma_start(kT[s][:], dram["qkT"][bass.ds(AW + h * HD, HD), :]).then_inc(qkv_in[s], 16)
                    sp.dma_start(v[s][:], dram["v"][:, bass.ds(h * HD, HD)].rearrange("(t p) e -> p t e", p=P)).then_inc(qkv_in[s], 16)

        @block.tensor
        def _(pe):
            pe.sem_inc(tr_mm, 2)
            pe.sem_inc(pv_mm, PV0)

            def scores(h, hh, s, j):
                n = ITEMS * h + j
                t0, S, i = shape_of(j)
                if j == 0:
                    pe.wait_ge(qkv_in[s], 48 * hh + 48)
                pe.wait_ge(masked, n + 1)
                for b in range(S // 512):
                    mm = pe.matmul(sc[j % 2][:, 512 * b:512 * b + 512], qT[s][:, t0 + P * i:t0 + P * i + P],
                                   kT[s][:, t0 + 512 * b:t0 + 512 * b + 512], start=True, stop=True)
                mm.then_inc(score_mm, 1)

            def transposes(h, j):
                n = ITEMS * h + j
                nb = shape_of(j)[1] // P
                pe.wait_ge(exp_done, 2 + n + 1)
                pe.wait_ge(copyA, n + 1)
                pe.wait_ge(copyB, n + 1)
                for b in range(nb):
                    bank = trA if b < nb // 2 else trB
                    mm = pe.transpose(bank[:, b % (nb // 2), :], probs[j % 2][:, P * b:P * b + P], ident[:])
                mm.then_inc(tr_mm, 1)

            def values(h, s, j):
                n = ITEMS * h + j
                t0, S, i = shape_of(j)
                nb = S // P
                pe.wait_ge(copyA, 1 + n + 1)
                pe.wait_ge(copyB, 1 + n + 1)
                pe.wait_ge(normed, n + 3)
                for b in range(nb):
                    mm = pe.matmul(o[j % 2][:, 0:HD], pT[j % 2][:, b // (nb // 2), b % (nb // 2), :],
                                   v[s][:, t0 // P + b, :], start=(b == 0), stop=(b == nb - 1))
                mm.then_inc(pv_mm, 1)

            def body(h, hh, s, last):
                for j in range(ITEMS):
                    if j + 2 < ITEMS:
                        scores(h, hh, s, j + 2)
                    elif not last:
                        scores(h + 1, hh + s, 1 - s, j + 2 - ITEMS)
                    if j + 1 < ITEMS:
                        transposes(h, j + 1)
                    elif not last:
                        transposes(h + 1, 0)
                    values(h, s, j)

            pe.wait_ge(const_in, 32)
            scores(0, 0, 0, 0)
            scores(0, 0, 0, 1)
            transposes(0, 0)
            heads(pe, body)

        @block.vector
        def _(dve):
            dve.sem_inc(masked, 2)
            dve.sem_inc(copyA, 1)
            dve.sem_inc(normed, 4)

            def mask_scores(h, j):
                n = ITEMS * h + j
                t0, S, i = shape_of(j)
                dve.wait_ge(score_mm, n + 1)
                dve.wait_ge(exp_done, n + 1)
                dve.sem_inc(held, 1)
                at = MASK_0 - P * i
                dve.tensor_tensor_reduce(neg[j % 2][:, 0:S], sc[j % 2][:, 0:S], mask[:, at:at + S], -1.0, 3.0e38,
                                         ALU.add, ALU.min, negmax[:, j % 2:j % 2 + 1]).then_inc(masked, 1)

            def copy_half(h, j):
                n = ITEMS * h + j
                nb = shape_of(j)[1] // P
                dve.wait_ge(tr_mm, 2 + n + 1)
                dve.wait_ge(pv_mm, PV0 - 2 + n + 1)
                dve.tensor_copy(pT[j % 2][:, 0, 0:nb // 2, :], trA[:, 0:nb // 2, :]).then_inc(copyA, 1)

            def normalise(h, j):
                n = ITEMS * h + j
                dve.wait_ge(exp_done, 2 + n + 1)
                dve.wait_ge(normed, 4 + n - 1)
                dve.reciprocal(rden[:, j % 2:j % 2 + 1], den[:, j % 4:j % 4 + 1]).then_inc(recip, 1)
                dve.wait_ge(recip, n + 1)
                dve.wait_ge(pv_mm, PV0 + n + 1)
                out = res["att"][:, j, bass.ds(h * HD, HD)]
                dve.tensor_scalar(out, o[j % 2][:, 0:HD], rden[:, j % 2:j % 2 + 1], None, ALU.mult).then_inc(normed, 1)

            def body(h, hh, s, last):
                for j in range(ITEMS):
                    if j + 2 < ITEMS:
                        mask_scores(h, j + 2)
                    elif not last:
                        mask_scores(h + 1, j + 2 - ITEMS)
                    if j + 1 < ITEMS:
                        copy_half(h, j + 1)
                    elif not last:
                        copy_half(h + 1, 0)
                    normalise(h, j)

            dve.wait_ge(const_in, 32)
            mask_scores(0, 0)
            mask_scores(0, 1)
            copy_half(0, 0)
            heads(dve, body)

        @block.scalar
        def _(act):
            act.sem_inc(exp_done, 2)
            act.sem_inc(copyB, 1)

            def exponent(h, j):
                n = ITEMS * h + j
                S = shape_of(j)[1]
                act.wait_ge(masked, 2 + n + 1)
                act.wait_ge(tr_mm, n + 1)
                act.wait_ge(normed, n + 1)
                act.activation(probs[j % 2][:, 0:S], neg[j % 2][:, 0:S], ACT.Exp, bias=negmax[:, j % 2:j % 2 + 1],
                               scale=-1.0, accum_out=den[:, j % 4:j % 4 + 1]).then_inc(exp_done, 1)

            def copy_half(h, j):
                n = ITEMS * h + j
                nb = shape_of(j)[1] // P
                act.wait_ge(tr_mm, 2 + n + 1)
                act.wait_ge(pv_mm, PV0 - 2 + n + 1)
                act.copy(pT[j % 2][:, 1, 0:nb // 2, :], trB[:, 0:nb // 2, :]).then_inc(copyB, 1)

            def body(h, hh, s, last):
                for j in range(ITEMS):
                    if j + 2 < ITEMS:
                        exponent(h, j + 2)
                    elif not last:
                        exponent(h + 1, j + 2 - ITEMS)
                    if j + 1 < ITEMS:
                        copy_half(h, j + 1)
                    elif not last:
                        copy_half(h + 1, 0)

            exponent(0, 0)
            exponent(0, 1)
            copy_half(0, 0)
            heads(act, body)


def stage_ssd(nc, dram, res):
    GH = HEADS // GROUPS
    HP = GH * HD
    LT, LE, GT, GE, ONE = range(5)
    TO_END, TO_START, FROM_START, FROM_END, ALL_F, ALL_B = range(6)
    LOG_TERMS = 9

    with ExitStack() as ctx:
        m = Mem(nc, ctx, "ssd")
        tri = m.sb("tri", [P, 5, P])
        ident = m.sb("ident", [P, P])
        dtb = m.sb("dtb", [P, NDT])
        alog = m.sb("alog", [P, NDT])
        dsk = m.sb("dsk", [P, HEADS])
        dtr = res["dt"]
        w1 = m.sb("w1", [P, NT, NDT])
        w2 = m.sb("w2", [P, NT, NDT])
        w3 = m.sb("w3", [P, NT, NDT])
        w4 = m.sb("w4", [P, NT, NDT])
        dt = m.sb("dt", [P, NT, NDT])
        dtA = m.sb("dtA", [P, NT, NDT])
        ex = m.sb("ex", [P, 6, NT, HEADS])
        wdt = m.sb("wdt", [P, 2, NT, HEADS])
        xb = [m.sb(f"xb{s}", [P, NCH, P]) for s in range(2)]
        rf = [m.sb(f"rf{s}", [P, HEADS, P]) for s in range(2)]
        rb = [m.sb(f"rb{s}", [P, HEADS, P]) for s in range(2)]
        E = [m.sb(f"E{s}", [P, GROUPS, GH, P]) for s in range(2)]
        cb = [m.sb(f"cb{s}", [P, 2, GROUPS, P]) for s in range(2)]
        W = [m.sb(f"W{s}", [P, 2, HEADS, P]) for s in range(2)]
        xtok = [m.sb(f"xtok{s}", [P, HEADS, HD]) for s in range(2)]
        btok = [m.sb(f"btok{s}", [P, GROUPS, P]) for s in range(2)]
        xdt = [m.sb(f"xdt{s}", [P, 3, HEADS, HD]) for s in range(2)]
        xst = [m.sb(f"xst{s}", [P, 2, HEADS, HD]) for s in range(2)]
        Sf = m.sb("Sf", [P, HEADS, HD])
        Sb = m.sb("Sb", [P, HEADS, HD])
        stb = m.sb("stb", [P, NT, HEADS, HD])
        yo = m.sb("yo", [P, HEADS, HD])
        cT = [m.sb(f"cT{s}", [P, GROUPS, P]) for s in range(2)]
        psx = m.ps("psx", [P, 512])
        psb = m.ps("psb", [P, 2, GROUPS, P])
        seg = m.ps("seg", [P, HEADS, P])
        psy = m.ps("psy", [P, HEADS, HD])
        psf = m.ps("psf", [P, HEADS, HD])
        pss = m.ps("pss", [P, HEADS, HD])
        pso = m.ps("pso", [P, HEADS, HD])

        const_in = m.sem("const_in")
        pre = m.sem("pre")
        pre_exp = m.sem("pre_exp")
        sums_mm = m.sem("sums_mm")
        tables = m.sem("tables")
        xb_in = m.sems("xb_in")
        tok_mm = m.sem("tok_mm")
        tok_ready = m.sem("tok_ready")
        cb_mm = m.sem("cb_mm")
        cb_ready = m.sem("cb_ready")
        rf_ready = m.sem("rf_ready")
        rb_ready = m.sem("rb_ready")
        seg_mm = m.sem("seg_mm")
        e_ready = m.sem("e_ready")
        w_ready = m.sem("w_ready")
        xdt_ready = m.sem("xdt_ready")
        xst_ready = m.sem("xst_ready")
        y_mm = m.sem("y_mm")
        st_mm = m.sem("st_mm")
        off_mm = m.sem("off_mm")
        stb_ready = m.sem("stb_ready")
        sf_zero = m.sem("sf_zero")
        sf_step = m.sem("sf_step")
        y_step = m.sem("y_step")
        cT_in = m.sems("cT_in")
        offb_mm = m.sem("offb_mm")
        sb_zero = m.sem("sb_zero")
        sb_step = m.sem("sb_step")
        yb_step = m.sem("yb_step")
        held_sp = m.sem("held_sp")
        held_dve = m.sem("held_dve")
        block = ctx.enter_context(nc.Block())
        FIRST = FIRST_TILE[1]

        def chunks(eng, body, between):
            with eng.Fori(0, FIRST // 2) as tt:
                for s in range(2):
                    body(2 * tt + s, tt, s, False)
            between()
            with eng.Fori(FIRST // 2, NT // 2 - 1) as tt:
                for s in range(2):
                    body(2 * tt + s, tt, s, False)
            body(NT - 2, NT // 2 - 1, 0, False)
            body(NT - 1, NT // 2 - 1, 1, True)

        def back(eng, body, between):
            with eng.Fori(0, (NT - FIRST) // 2) as ii:
                for s in range(2):
                    body(2 * ii + s, ii, s)
            between()
            with eng.Fori((NT - FIRST) // 2, NT // 2) as ii:
                for s in range(2):
                    body(2 * ii + s, ii, s)

        @block.sync
        def _(sp):
            for dst, name in ((tri, "tri"), (ident, "ident"), (dtb, "dt_bias"), (alog, "a_log"), (dsk, "d_skip")):
                sp.dma_start(dst[:], dram[name]).then_inc(const_in, 16)
            src = dram["xbc"].rearrange("(c p) t -> p c t", p=P)
            with sp.Fori(0, NT // 2) as tt:
                for s in range(2):
                    t = 2 * tt + s
                    sp.wait_ge(off_mm, t + 1)
                    sp.dma_start(xb[s][:], src[:, :, bass.ds(t * P, P)]).then_inc(xb_in[s], 16)
            with sp.Fori(0, NT // 2) as ii:
                for s in range(2):
                    i = 2 * ii + s
                    sp.wait_ge(offb_mm, i + 1)
                    sp.sem_inc(held_sp, 1)
                    at = (NT - 1) * P - i * P
                    sp.dma_start(cT[s][:], src[:, NCH - GROUPS:, bass.ds(at, P)]).then_inc(cT_in[s], 16)

        @block.tensor
        def _(pe):
            for sem, n in ((seg_mm, 2), (y_mm, 2), (st_mm, 2), (off_mm, 2), (offb_mm, 2)):
                pe.sem_inc(sem, n)
            pe.wait_ge(const_in, 80)
            pe.wait_ge(tables, 1)
            sums = ((GT, 0), (LT, HEADS), (LE, 0), (GE, HEADS), (ONE, 0), (ONE, HEADS))
            flat = seg[:].rearrange("p h l -> p (h l)")
            for n, (tr, off) in enumerate(sums):
                at = 512 * (n // 3) + NT * HEADS * (n % 3)
                mm = pe.matmul(flat[:, at:at + NT * HEADS], tri[:, tr, :], dtA[:, :, off:off + HEADS], start=True, stop=True)
            mm.then_inc(sums_mm, 1)
            pe.wait_ge(pre_exp, 4)

            def to_tokens(t, tt, s):
                pe.wait_ge(xb_in[s], 16 * tt + 16)
                pe.wait_ge(tok_ready, 2 * t + 2)
                pe.wait_ge(cb_ready, 2 * t + 2)
                for j in range(SSM_W // P):
                    pe.transpose(psx[:, P * j:P * j + P], xb[s][:, j, :], ident[:])
                for g in range(GROUPS):
                    mm = pe.transpose(psb[:, 0, g, :], xb[s][:, SSM_W // P + g, :], ident[:])
                mm.then_inc(tok_mm, 1)

            def products(t, s):
                pe.wait_ge(tok_ready, 2 + 2 * t + 2)
                for g in range(GROUPS):
                    mm = pe.matmul(psb[:, 1, g, :], xb[s][:, SSM_W // P + g, :], xb[s][:, SSM_W // P + GROUPS + g, :],
                                   start=True, stop=True)
                mm.then_inc(cb_mm, 1)

            def segments(t, s):
                pe.wait_ge(rf_ready, t + 1)
                pe.wait_ge(rb_ready, t + 1)
                pe.wait_ge(e_ready, t + 1)
                for half in range(2):
                    hs = slice(GH * half, GH * half + GH)
                    pe.matmul(seg[:, hs, :], tri[:, GT, :], rf[s][:, hs, :], start=True, stop=False)
                    mm = pe.matmul(seg[:, hs, :], tri[:, LT, :], rb[s][:, hs, :], start=False, stop=True)
                mm.then_inc(seg_mm, 1)

            def body(t, tt, s, last):
                if not last:
                    to_tokens(t + 1, tt + s, 1 - s)
                    segments(t + 1, 1 - s)
                    products(t + 1, 1 - s)
                pe.wait_ge(sf_step, 2 * t + 2)
                pe.wait_ge(y_step, 3 * t + 1)
                for g in range(GROUPS):
                    gs = slice(GH * g, GH * g + GH)
                    mm = pe.matmul(pso[:, gs, :], xb[s][:, SSM_W // P + GROUPS + g, :], Sf[:, gs, :], start=True, stop=True)
                mm.then_inc(off_mm, 1)
                pe.wait_ge(xst_ready, 4 + 2 * t + 2)
                pe.wait_ge(tok_ready, 2 + 2 * t + 2)
                pe.wait_ge(stb_ready, t + 1)
                for ps_, d in ((psf, 0), (pss, 1)):
                    for g in range(GROUPS):
                        gs = slice(GH * g, GH * g + GH)
                        mm = pe.matmul(ps_[:, gs, :], btok[s][:, g, :], xst[s][:, d, gs, :], start=True, stop=True)
                mm.then_inc(st_mm, 1)
                pe.wait_ge(w_ready, 4 + 2 * t + 2)
                pe.wait_ge(xdt_ready, 6 + 3 * t + 3)
                pe.wait_ge(y_step, 3 * t + 2)
                for h in range(HEADS):
                    for d in range(2):
                        mm = pe.matmul(psy[:, h, :], W[s][:, d, h, :], xdt[s][:, d, h, :], start=(d == 0), stop=(d == 1))
                mm.then_inc(y_mm, 1)

            pe.wait_ge(sf_zero, 1)
            to_tokens(0, 0, 0)
            segments(0, 0)
            products(0, 0)
            chunks(pe, body, lambda: pe.wait_ge(sf_zero, 2))

            def body_back(i, ii, s):
                pe.wait_ge(cT_in[s], 16 * ii + 16)
                pe.wait_ge(sb_step, 2 * i + 2)
                pe.wait_ge(yb_step, 2 * i + 1)
                for g in range(GROUPS):
                    gs = slice(GH * g, GH * g + GH)
                    mm = pe.matmul(pso[:, gs, :], cT[s][:, g, :], Sb[:, gs, :], start=True, stop=True)
                mm.then_inc(offb_mm, 1)

            pe.wait_ge(y_step, 3 + 3 * NT)
            pe.wait_ge(sb_zero, 1)
            back(pe, body_back, lambda: pe.wait_ge(sb_zero, 2))

        @block.scalar
        def _(act):
            for sem, n in ((tok_ready, 2), (e_ready, 1), (stb_ready, 1)):
                act.sem_inc(sem, n)
            act.wait_ge(const_in, 80)
            act.activation(alog[:], alog[:], ACT.Exp).then_inc(pre_exp, 1)
            act.wait_ge(pre, 2)
            act.activation(w3[:], w2[:], ACT.Exp, scale=-1.0).then_inc(pre_exp, 1)
            act.wait_ge(sums_mm, 1)
            flat = seg[:].rearrange("p h l -> p (h l)")
            for n in range(2):
                act.activation(ex[:, 3 * n:3 * n + 3, :, :].rearrange("p n t h -> p (n t h)"),
                               flat[:, 512 * n:512 * n + 3 * NT * HEADS], ACT.Exp).then_inc(pre_exp, 1)

            def tokens(t, s):
                act.wait_ge(tok_mm, t + 1)
                act.wait_ge(xdt_ready, 3 * t + 3)
                act.wait_ge(xst_ready, 2 * t + 2)
                act.wait_ge(st_mm, t + 1)
                act.copy(xtok[s][:].rearrange("p h e -> p (h e)"), psx[:]).then_inc(tok_ready, 1)
                act.copy(btok[s][:], psb[:, 0]).then_inc(tok_ready, 1)

            def exponent(t, s):
                act.wait_ge(seg_mm, 2 + t + 1)
                act.wait_ge(w_ready, 2 * t + 2)
                act.activation(E[s][:].rearrange("p g h l -> p (g h) l"), seg[:], ACT.Exp).then_inc(e_ready, 1)

            def body(t, tt, s, last):
                if not last:
                    tokens(t + 1, 1 - s)
                    exponent(t + 1, 1 - s)
                act.wait_ge(st_mm, 2 + t + 1)
                act.copy(stb[:, bass.ds(t, 1), :, :].rearrange("p t h e -> p (t h) e"), pss[:]).then_inc(stb_ready, 1)

            tokens(0, 0)
            exponent(0, 0)
            chunks(act, body, lambda: None)

        @block.gpsimd
        def _(pool):
            pool.sem_inc(xst_ready, 4)
            pool.wait_ge(const_in, 80)
            pool.wait_ge(tables, 3)

            def sources(t, s):
                pool.wait_ge(seg_mm, t + 1)
                a = dtA[:, bass.ds(t, 1), 0:HEADS].rearrange("p t h -> p (t h)").unsqueeze(2).broadcast_to([P, HEADS, P])
                pool.tensor_tensor(rf[s][:], a, tri[:, LE:LE + 1, :].broadcast_to([P, HEADS, P]), ALU.mult).then_inc(rf_ready, 1)

            def body(t, tt, s, last):
                if not last:
                    sources(t + 1, 1 - s)
                pool.wait_ge(tok_ready, 2 + 2 * t + 1)
                pool.wait_ge(st_mm, t + 1)
                for d in range(2):
                    a = wdt[:, d, bass.ds(t, 1), :].rearrange("p t h -> p (t h)").unsqueeze(2).broadcast_to([P, HEADS, HD])
                    pool.tensor_tensor(xst[s][:, d], xtok[s][:], a, ALU.mult).then_inc(xst_ready, 1)

            sources(0, 0)
            chunks(pool, body, lambda: None)

        @block.vector
        def _(dve):
            for sem, n in ((cb_ready, 2), (w_ready, 4), (xdt_ready, 6), (y_step, 3), (sf_step, 2), (sb_step, 2), (yb_step, 2)):
                dve.sem_inc(sem, n)
            dve.memset(Sf[:], 0.0).then_inc(sf_zero, 1)
            dve.memset(Sb[:], 0.0).then_inc(sb_zero, 1)
            dve.wait_ge(const_in, 80)
            per_tile = [P, NT, NDT]
            dve.tensor_tensor(w1[:], dtr[:], dtb[:].unsqueeze(1).broadcast_to(per_tile), ALU.add).then_inc(pre, 1)
            dve.wait_ge(pre, 1)
            dve.scalar_tensor_tensor(w2[:], w1[:], -1.0, w1[:], ALU.mult, ALU.max).then_inc(pre, 1)
            dve.wait_ge(pre_exp, 2)
            dve.tensor_scalar(w2[:], w3[:], 2.0, None, ALU.add).then_inc(pre, 1)
            dve.wait_ge(pre, 3)
            dve.reciprocal(w2[:], w2[:]).then_inc(pre, 1)
            dve.wait_ge(pre, 4)
            dve.tensor_tensor(w3[:], w3[:], w2[:], ALU.mult).then_inc(pre, 1)
            dve.wait_ge(pre, 5)
            dve.tensor_tensor(w2[:], w3[:], w3[:], ALU.mult).then_inc(pre, 1)
            dve.wait_ge(pre, 6)
            dve.tensor_scalar(w4[:], w2[:], 1.0 / (2 * LOG_TERMS + 1), None, ALU.mult).then_inc(pre, 1)
            for n in range(LOG_TERMS - 1, 0, -1):
                dve.wait_ge(pre, 6 + LOG_TERMS - n)
                dve.scalar_tensor_tensor(w4[:], w4[:], 1.0 / (2 * n + 1), w2[:], ALU.add, ALU.mult).then_inc(pre, 1)
            dve.wait_ge(pre, 6 + LOG_TERMS)
            dve.scalar_tensor_tensor(w4[:], w4[:], 1.0, w3[:], ALU.add, ALU.mult).then_inc(pre, 1)
            dve.tensor_scalar(w1[:], w1[:], 0.0, None, ALU.max).then_inc(pre, 1)
            dve.wait_ge(pre, 8 + LOG_TERMS)
            dve.scalar_tensor_tensor(dt[:], w4[:], 2.0, w1[:], ALU.mult, ALU.add).then_inc(pre, 1)
            dve.wait_ge(pre, 9 + LOG_TERMS)
            dve.scalar_tensor_tensor(dtA[:], dt[:], -1.0, alog[:].unsqueeze(1).broadcast_to(per_tile), ALU.mult, ALU.mult).then_inc(tables, 1)
            dve.wait_ge(pre_exp, 4)
            for d in range(2):
                dve.tensor_tensor(wdt[:, d], dt[:, :, HEADS * d:HEADS * d + HEADS], ex[:, TO_END + d], ALU.mult).then_inc(tables, 1)
            dve.wait_ge(tables, 3)

            def over(a, shape):
                return a.rearrange("p t h -> p (t h)").unsqueeze(2).broadcast_to(shape)

            def sources(t, s):
                dve.wait_ge(seg_mm, t + 1)
                dve.tensor_tensor(rb[s][:], over(dtA[:, bass.ds(t, 1), HEADS:], [P, HEADS, P]),
                                  tri[:, GE:GE + 1, :].broadcast_to([P, HEADS, P]), ALU.mult).then_inc(rb_ready, 1)

            def mask_cb(t, s):
                dve.wait_ge(cb_mm, t + 1)
                dve.wait_ge(w_ready, 2 * t + 2)
                for d, tr in ((0, LE), (1, GE)):
                    dve.tensor_tensor(cb[s][:, d], psb[:, 1], tri[:, tr:tr + 1, :].broadcast_to([P, GROUPS, P]),
                                      ALU.mult).then_inc(cb_ready, 1)

            def body(t, tt, s, last):
                if not last:
                    sources(t + 1, 1 - s)
                dve.wait_ge(e_ready, 1 + t + 1)
                dve.wait_ge(cb_ready, 2 + 2 * t + 2)
                dve.wait_ge(y_mm, t + 1)
                for d in range(2):
                    dve.tensor_tensor(W[s][:, d].rearrange("p (g r) l -> p g r l", g=GROUPS), E[s][:],
                                      cb[s][:, d].unsqueeze(2).broadcast_to([P, GROUPS, GH, P]), ALU.mult).then_inc(w_ready, 1)
                dve.wait_ge(tok_ready, 2 + 2 * t + 1)
                dve.wait_ge(y_step, 3 * t + 3)
                for d in range(3):
                    a = over(dt[:, bass.ds(t, 1), HEADS * d:HEADS * d + HEADS], [P, HEADS, HD]) if d < 2 else \
                        dsk[:].unsqueeze(2).broadcast_to([P, HEADS, HD])
                    dve.tensor_tensor(xdt[s][:, d], xtok[s][:], a, ALU.mult).then_inc(xdt_ready, 1)
                if not last:
                    mask_cb(t + 1, 1 - s)
                dve.wait_ge(off_mm, 2 + t + 1)
                dve.tensor_tensor(yo[:], pso[:], over(ex[:, FROM_START, bass.ds(t, 1), :], [P, HEADS, HD]), ALU.mult).then_inc(y_step, 1)
                dve.wait_ge(sf_step, 2 + 2 * t)
                dve.tensor_tensor(Sf[:], Sf[:], over(ex[:, ALL_F, bass.ds(t, 1), :], [P, HEADS, HD]), ALU.mult).then_inc(sf_step, 1)
                dve.wait_ge(st_mm, 2 + t + 1)
                dve.wait_ge(sf_step, 2 + 2 * t + 1)
                dve.tensor_tensor(Sf[:], Sf[:], psf[:], ALU.add).then_inc(sf_step, 1)
                dve.wait_ge(y_mm, 2 + t + 1)
                dve.wait_ge(y_step, 3 + 3 * t + 1)
                dve.tensor_tensor(yo[:], yo[:], psy[:], ALU.add).then_inc(y_step, 1)
                dve.wait_ge(y_step, 3 + 3 * t + 2)
                dve.wait_ge(xdt_ready, 6 + 3 * t + 3)
                out = res["y"][:, bass.ds(t, 1), :].rearrange("p t (h e) -> p (t h) e", e=HD)
                dve.tensor_tensor(out, yo[:], xdt[s][:, 2], ALU.add).then_inc(y_step, 1)

            def restart():
                dve.wait_ge(sf_step, 2 + 2 * FIRST)
                dve.memset(Sf[:], 0.0).then_inc(sf_zero, 1)
                dve.wait_ge(sf_zero, 2)

            dve.wait_ge(sf_zero, 1)
            sources(0, 0)
            mask_cb(0, 0)
            chunks(dve, body, restart)

            def body_back(i, ii, s):
                t = (NT - 1) - i
                dve.wait_ge(offb_mm, 2 + i + 1)
                dve.wait_ge(yb_step, 2 * i + 2)
                dve.sem_inc(held_dve, 1)
                dve.tensor_tensor(yo[:], pso[:], over(ex[:, FROM_END, bass.ds(t, 1), :], [P, HEADS, HD]), ALU.mult).then_inc(yb_step, 1)
                dve.wait_ge(sb_step, 2 * i + 2)
                dve.tensor_tensor(Sb[:], Sb[:], over(ex[:, ALL_B, bass.ds(t, 1), :], [P, HEADS, HD]), ALU.mult).then_inc(sb_step, 1)
                dve.wait_ge(sb_step, 2 * i + 3)
                dve.tensor_tensor(Sb[:], Sb[:], stb[:, bass.ds(t, 1), :, :].rearrange("p t h e -> p (t h) e"), ALU.add).then_inc(sb_step, 1)
                dve.wait_ge(yb_step, 2 * i + 3)
                out = res["y"][:, bass.ds(t, 1), :].rearrange("p t (h e) -> p (t h) e", e=HD)
                dve.tensor_tensor(out, out, yo[:], ALU.add).then_inc(yb_step, 1)

            def restart_back():
                dve.wait_ge(sb_step, 2 + 2 * (NT - FIRST))
                dve.memset(Sb[:], 0.0).then_inc(sb_zero, 1)
                dve.wait_ge(sb_zero, 2)

            dve.wait_ge(stb_ready, 1 + NT)
            dve.wait_ge(sb_zero, 1)
            dve.wait_ge(y_step, 3 + 3 * NT)
            back(dve, body_back, restart_back)
            dve.wait_ge(yb_step, 2 + 2 * NT)


def stage_mix(nc, dram, res):
    with ExitStack() as ctx:
        m = Mem(nc, ctx, "mix")
        wout = m.sb("wout", [P, KD, D])
        wr = m.sb("wr", [P, KD, EXPERTS])
        normw = m.sb("normw", [P, SSM_W])
        ln = m.sb("ln", [P, 2, D])
        ident = m.sb("ident", [P, P])
        half = m.sb("half", [P, 1])
        xr = [m.sb(f"xr{s}", [P, D]) for s in range(2)]
        mixin = [m.sb(f"mixin{s}", [P, D]) for s in range(2)]
        sq = m.sb("sq", [P, SSM_W])
        ss = m.sb("ss", [P, 2])
        rs = m.sb("rs", [P, 2])
        mT = [m.sb(f"mT{s}", [P, KD, P]) for s in range(2)]
        r = m.sb("r", [P, D])
        stats = m.sb("stats", [P, 2, 6])
        mv = m.sb("mv", [P, 2])
        rstd = m.sb("rstd", [P, 1])
        h = [m.sb(f"h{s}", [P, D]) for s in range(2)]
        ah = [m.sb(f"ah{s}", [P, D]) for s in range(2)]
        hT = m.sb("hT", [P, KD, P])
        nmx = m.sb("nmx", [P, 1])
        er = m.sb("er", [P, EXPERTS])
        den = m.sb("den", [P, 1])
        rden = m.sb("rden", [P, 1])
        aff = m.sb("aff", [P, NT, EXPERTS])
        trA = m.ps("trA", [P, 4, P])
        trB = m.ps("trB", [P, 4, P])
        hrA = m.ps("hrA", [P, 4, P])
        hrB = m.ps("hrB", [P, 4, P])
        po = m.ps("po", [P, D])
        pr = m.ps("pr", [P, 512])

        const_in = m.sem("const_in")
        xr_in = m.sems("xr_in")
        x_free = m.sem("x_free")
        half_set = m.sem("half_set")
        held_dve = m.sem("held_dve")
        held_pool = m.sem("held_pool")
        gated = m.sem("gated")
        squared = m.sem("squared")
        rs_ready = m.sem("rs_ready")
        rs_tmp = m.sem("rs_tmp")
        mix_att = m.sem("mix_att")
        mix_ssm = m.sem("mix_ssm")
        tr_mm = m.sem("tr_mm")
        mA = m.sem("mA")
        mB = m.sem("mB")
        out_mm = m.sem("out_mm")
        r_ready = m.sem("r_ready")
        ln_step = m.sem("ln_step")
        rstd_tmp = m.sem("rstd_tmp")
        rstd_ready = m.sem("rstd_ready")
        scaled = m.sem("scaled")
        gained = m.sem("gained")
        h_ready = m.sem("h_ready")
        ah_ready = m.sem("ah_ready")
        h_out = m.sem("h_out")
        h_free = m.sem("h_free")
        ht_mm = m.sem("ht_mm")
        hA = m.sem("hA")
        hB = m.sem("hB")
        rt_mm = m.sem("rt_mm")
        nmx_ready = m.sem("nmx_ready")
        er_ready = m.sem("er_ready")
        aff_step = m.sem("aff_step")
        aff_ready = m.sem("aff_ready")
        at_mm = m.sem("at_mm")
        at_done = m.sem("at_done")
        block = ctx.enter_context(nc.Block())

        def tiles(eng, body):
            with eng.Fori(0, NT // 2 - 1) as tt:
                for s in range(2):
                    body(2 * tt + s, tt, s, False)
            body(NT - 2, NT // 2 - 1, 0, False)
            body(NT - 1, NT // 2 - 1, 1, True)

        @block.sync
        def _(sp):
            sp.dma_start(ident[:], dram["ident"]).then_inc(const_in, 16)
            sp.dma_start(normw[:], dram["norm_w"]).then_inc(const_in, 16)
            sp.dma_start(ln[:], dram["ln"][:, 0:2, :]).then_inc(const_in, 16)
            sp.dma_start(wr[:], dram["w_router"].rearrange("(k p) e -> p k e", p=P)).then_inc(const_in, 16)
            sp.dma_start(wout[:], dram["w_out"].rearrange("(k p) n -> p k n", p=P)).then_inc(const_in, 16)
            with sp.Fori(0, NT // 2) as tt:
                for s in range(2):
                    t = 2 * tt + s
                    sp.wait_ge(x_free, t + 1)
                    sp.dma_start(xr[s][:], dram["x"][bass.ds(t * P, P), :]).then_inc(xr_in[s], 16)

        @block.tensor
        def _(pe):
            for sem, n in ((tr_mm, 2), (out_mm, 2), (ht_mm, 2), (rt_mm, 1)):
                pe.sem_inc(sem, n)

            def project(t, s):
                pe.wait_ge(mix_att, t + 1)
                pe.wait_ge(mix_ssm, t + 1)
                pe.wait_ge(mA, t + 1)
                pe.wait_ge(mB, t + 1)
                for j in range(KD):
                    bank = trA if j < 4 else trB
                    mm = pe.transpose(bank[:, j % 4, :], mixin[s][:, P * j:P * j + P], ident[:])
                mm.then_inc(tr_mm, 1)
                pe.wait_ge(mA, 1 + t + 1)
                pe.wait_ge(mB, 1 + t + 1)
                pe.wait_ge(r_ready, t + 1)
                for n in range(2):
                    for k in range(KD):
                        mm = pe.matmul(po[:, 512 * n:512 * n + 512], mT[s][:, k, :], wout[:, k, 512 * n:512 * n + 512],
                                       start=(k == 0), stop=(k == KD - 1))
                mm.then_inc(out_mm, 1)

            def body(t, tt, s, last):
                if not last:
                    project(t + 1, 1 - s)
                pe.wait_ge(h_ready, t + 1)
                pe.wait_ge(hA, t + 1)
                pe.wait_ge(hB, t + 1)
                for j in range(KD):
                    bank = hrA if j < 4 else hrB
                    mm = pe.transpose(bank[:, j % 4, :], h[s][:, P * j:P * j + P], ident[:])
                mm.then_inc(ht_mm, 1)
                pe.wait_ge(hA, 1 + t + 1)
                pe.wait_ge(hB, 1 + t + 1)
                pe.wait_ge(aff_ready, t + 1)
                for k in range(KD):
                    mm = pe.matmul(pr[:, 0:EXPERTS], hT[:, k, :], wr[:, k, :], start=(k == 0), stop=(k == KD - 1))
                mm.then_inc(rt_mm, 1)

            pe.wait_ge(const_in, 80)
            project(0, 0)
            tiles(pe, body)
            pe.wait_ge(aff_ready, 1 + NT)
            for t in range(NT):
                bank = (trA, trB, hrA)[t // 4]
                mm = pe.transpose(bank[0:EXPERTS, t % 4, :], aff[:, t, :], ident[:])
            mm.then_inc(at_mm, 1)

        @block.scalar
        def _(act):
            for sem, n in ((squared, 1), (mB, 1), (hB, 1)):
                act.sem_inc(sem, n)

            def inputs(t, s):
                act.wait_ge(tr_mm, t + 1)
                act.copy(mixin[s][:, 0:AW], res["att"][:, bass.ds(t, 1), :].rearrange("p t n -> p (t n)")).then_inc(mix_att, 1)
                act.wait_ge(gated, t + 1)
                act.wait_ge(squared, t + 1)
                act.activation(sq[:], mixin[s][:, AW:], ACT.Square, accum_out=ss[:, s:s + 1]).then_inc(squared, 1)

            def copies(t, s):
                act.wait_ge(tr_mm, 2 + t + 1)
                act.wait_ge(out_mm, t + 1)
                act.copy(mT[s][:, 4:, :], trB[:]).then_inc(mB, 1)

            def body(t, tt, s, last):
                if not last:
                    inputs(t + 1, 1 - s)
                    copies(t + 1, 1 - s)
                act.wait_ge(h_ready, t + 1)
                act.wait_ge(h_free, t + 1)
                act.mul(ah[s][:], h[s][:], ALPHA).then_inc(ah_ready, 1)
                act.wait_ge(ht_mm, 2 + t + 1)
                act.wait_ge(rt_mm, t + 1)
                act.copy(hT[:, 4:, :], hrB[:]).then_inc(hB, 1)
                act.wait_ge(nmx_ready, t + 1)
                act.wait_ge(aff_ready, t + 1)
                act.activation(er[:], pr[:, 0:EXPERTS], ACT.Exp, bias=nmx[:], accum_out=den[:]).then_inc(er_ready, 1)

            inputs(0, 0)
            copies(0, 0)
            tiles(act, body)

        @block.gpsimd
        def _(pool):
            pool.sem_inc(h_free, 2)
            pool.memset(half[:], -0.5).then_inc(half_set, 1)
            pool.wait_ge(half_set, 1)
            pool.wait_ge(const_in, 80)

            def root(t, s):
                pool.wait_ge(squared, 1 + t + 1)
                pool.sem_inc(held_pool, 1)
                pool.tensor_scalar(rs[:, s:s + 1], ss[:, s:s + 1], 1.0 / SSM_W, RMS_EPS, ALU.mult, ALU.add).then_inc(rs_tmp, 1)
                pool.wait_ge(rs_tmp, t + 1)
                pool.tensor_tensor(rs[:, s:s + 1], rs[:, s:s + 1], half[:], ALU.pow).then_inc(rs_ready, 1)

            def body(t, tt, s, last):
                if not last:
                    root(t + 1, 1 - s)
                pool.wait_ge(ln_step, 3 * t + 3)
                pool.sem_inc(held_pool, 1)
                pool.tensor_scalar(rstd[:], mv[:, 1:2], 1.0, LN_EPS, ALU.mult, ALU.add).then_inc(rstd_tmp, 1)
                pool.wait_ge(rstd_tmp, t + 1)
                pool.tensor_tensor(rstd[:], rstd[:], half[:], ALU.pow).then_inc(rstd_ready, 1)
                pool.wait_ge(scaled, t + 1)
                pool.tensor_tensor(h[s][:], h[s][:], ln[:, 0, :], ALU.mult).then_inc(gained, 1)
                pool.wait_ge(h_ready, t + 1)
                pool.sem_inc(held_pool, 1)
                pool.dma_start(dram["h"][bass.ds(t * P, P), :], h[s][:]).then_inc(h_out, 16)
                pool.wait_ge(ah_ready, t + 1)
                pool.sem_inc(held_pool, 1)
                pool.dma_start(dram["acc"][bass.ds(t * P, P), :], ah[s][:]).then_inc(h_out, 16)
                pool.wait_ge(h_out, 32 * t + 32)
                pool.sem_inc(h_free, 1)

            root(0, 0)
            tiles(pool, body)

        @block.vector
        def _(dve):
            for sem, n in ((mA, 1), (hA, 1), (r_ready, 1), (aff_ready, 1), (x_free, 2)):
                dve.sem_inc(sem, n)

            def gate(t, s):
                dve.wait_ge(tr_mm, t + 1)
                dve.tensor_tensor(mixin[s][:, AW:], res["y"][:, bass.ds(t, 1), :].rearrange("p t n -> p (t n)"),
                                  res["z"][:, bass.ds(t, 1), :].rearrange("p t n -> p (t n)"), ALU.mult).then_inc(gated, 1)

            def norm(t, s):
                dve.wait_ge(rs_ready, t + 1)
                dve.wait_ge(squared, 1 + t + 1)
                dve.scalar_tensor_tensor(mixin[s][:, AW:], mixin[s][:, AW:], rs[:, s:s + 1], normw[:], ALU.mult, ALU.mult).then_inc(mix_ssm, 1)

            def copies(t, s):
                dve.wait_ge(tr_mm, 2 + t + 1)
                dve.wait_ge(out_mm, t + 1)
                dve.tensor_copy(mT[s][:, 0:4, :], trA[:]).then_inc(mA, 1)

            def body(t, tt, s, last):
                if not last:
                    gate(t + 1, 1 - s)
                    norm(t + 1, 1 - s)
                    copies(t + 1, 1 - s)
                dve.wait_ge(out_mm, 2 + t + 1)
                dve.wait_ge(xr_in[s], 16 * tt + 16)
                dve.scalar_tensor_tensor(r[:], xr[s][:], ALPHA, po[:], ALU.mult, ALU.add).then_inc(r_ready, 1)
                dve.wait_ge(r_ready, 1 + t + 1)
                dve.sem_inc(x_free, 1)
                dve.bn_stats(stats[:, 0], r[:, 0:512]).then_inc(ln_step, 1)
                dve.bn_stats(stats[:, 1], r[:, 512:]).then_inc(ln_step, 1)
                dve.wait_ge(ln_step, 3 * t + 2)
                dve.sem_inc(held_dve, 1)
                dve.bn_aggr(mv[:], stats[:]).then_inc(ln_step, 1)
                dve.wait_ge(rstd_ready, t + 1)
                dve.wait_ge(h_free, t + 1)
                dve.wait_ge(ht_mm, t + 1)
                dve.wait_ge(ln_step, 3 * t + 3)
                dve.tensor_scalar(h[s][:], r[:], mv[:, 0:1], rstd[:], ALU.subtract, ALU.mult).then_inc(scaled, 1)
                dve.wait_ge(gained, t + 1)
                dve.tensor_tensor(h[s][:], h[s][:], ln[:, 1, :], ALU.add).then_inc(h_ready, 1)
                dve.wait_ge(ht_mm, 2 + t + 1)
                dve.wait_ge(rt_mm, t + 1)
                dve.tensor_copy(hT[:, 0:4, :], hrA[:]).then_inc(hA, 1)
                dve.wait_ge(rt_mm, 1 + t + 1)
                dve.tensor_reduce(nmx[:], pr[:, 0:EXPERTS], mybir.AxisListType.X, ALU.max, negate=True).then_inc(nmx_ready, 1)
                dve.wait_ge(er_ready, t + 1)
                dve.reciprocal(rden[:], den[:]).then_inc(aff_step, 1)
                dve.wait_ge(aff_step, t + 1)
                dve.tensor_scalar(aff[:, bass.ds(t, 1), :], er[:].unsqueeze(1), rden[:], None, ALU.mult).then_inc(aff_ready, 1)

            dve.wait_ge(const_in, 80)
            gate(0, 0)
            norm(0, 0)
            copies(0, 0)
            tiles(dve, body)
            dve.wait_ge(at_mm, 1)
            for b, bank in enumerate((trA, trB, hrA)):
                dve.tensor_copy(res["affT"][:, 512 * b:512 * b + 512], bank[0:EXPERTS].rearrange("e j t -> e (j t)")).then_inc(at_done, 1)
            dve.wait_ge(at_done, 3)


def stage_choose(nc, dram, res):
    with ExitStack() as ctx:
        m = Mem(nc, ctx, "top")
        ident = m.sb("ident", [P, P])
        val = m.sb("val", [EXPERTS, CAP])
        idx = m.sb("idx", [EXPERTS, CAP], U32)
        idxf = m.sb("idxf", [EXPERTS, CAP])
        ps = m.ps("ps", [P, 4, EXPERTS])
        const_in = m.sem("const_in")
        step = m.sem("step")
        float_ready = m.sem("float_ready")
        tr_mm = m.sem("tr_mm")
        done = m.sem("done")
        block = ctx.enter_context(nc.Block())
        parts = ((1, 0, CAPS[1]), (0, CAPS[1], CAPS[0]))

        @block.sync
        def _(sp):
            sp.dma_start(ident[:], dram["ident"]).then_inc(const_in, 16)

        @block.vector
        def _(dve):
            n = 0
            for q, c0, cap in parts:
                work = res["affT"][:, sum(SEQS[:q]):sum(SEQS[:q]) + SEQS[q]]
                for r in range(cap // 8):
                    at = slice(c0 + 8 * r, c0 + 8 * r + 8)
                    dve.max(val[:, at], work).then_inc(step, 1)
                    dve.wait_ge(step, n + 1)
                    dve.max_index(idx[:, at], val[:, at], work).then_inc(step, 1)
                    dve.wait_ge(step, n + 2)
                    dve.match_replace(work, val[:, at], work, -1.0).then_inc(step, 1)
                    dve.wait_ge(step, n + 3)
                    n += 3
            dve.tensor_scalar(idxf[:, 0:CAPS[1]], idx[:, 0:CAPS[1]], float(SEQS[0]), None, ALU.add).then_inc(float_ready, 1)
            dve.tensor_copy(idxf[:, CAPS[1]:], idx[:, CAPS[1]:]).then_inc(float_ready, 1)
            dve.wait_ge(tr_mm, 1)
            for i, (q, c0, cap) in enumerate(parts):
                dve.tensor_copy(res["gates"][i][:], ps[0:cap, 2 * i, :]).then_inc(done, 1)
                dve.tensor_copy(res["rows"][i][:], ps[0:cap, 2 * i + 1, :]).then_inc(done, 1)
            dve.wait_ge(done, 4)

        @block.tensor
        def _(pe):
            pe.wait_ge(const_in, 16)
            pe.wait_ge(float_ready, 2)
            for i, (q, c0, cap) in enumerate(parts):
                pe.transpose(ps[0:cap, 2 * i, :], val[:, c0:c0 + cap], ident[0:EXPERTS, 0:EXPERTS])
                mm = pe.transpose(ps[0:cap, 2 * i + 1, :], idxf[:, c0:c0 + cap], ident[0:EXPERTS, 0:EXPERTS])
            mm.then_inc(tr_mm, 1)


def stage_experts(nc, dram, res):
    NS, NP_ = CAPS[1], CAPS[0]
    HALF = FCH // 2
    STEPS = FCH + KD
    GR = 2 * STEPS
    PAIRS = FCH // 2
    with ExitStack() as ctx:
        m = Mem(nc, ctx, "moe")
        raw = [m.sb(f"raw{c}", [P, HALF, P]) for c in range(4)]
        whi = [m.sb(f"whi{c}", [P, HALF, P], F32R) for c in range(4)]
        wlo = [m.sb(f"wlo{c}", [P, HALF, P], F32R) for c in range(4)]
        ident = m.sb("ident", [P, P])
        grow = [m.sb("grow_s", [NS, 1], U32), m.sb("grow_p", [NP_, 1], U32)]
        srow = [m.sb("srow_s", [NS, 1], U32), m.sb("srow_p", [NP_, 1], U32)]
        xg = [m.sb("xg_s", [NS, D]), m.sb("xg_p", [NP_, D])]
        xgT = [m.sb(f"xgT{q}", [P, KD, 2 * CAP], F32R) for q in range(2)]
        part = [m.sb(f"part{s}", [P, 2, CAP]) for s in range(2)]
        guv = [m.sb(f"guv{s}", [P, 2, CAP]) for s in range(2)]
        prod = [m.sb(f"prod{s}", [P, CAP]) for s in range(2)]
        hid = m.sb("hid", [P, FCH, 2 * CAP], F32R)
        dpart = [m.sb(f"dpart{s}", [P, CAP]) for s in range(2)]
        oT = m.sb("oT", [P, KD, CAP])
        og = [m.sb("og_s", [NS, D]), m.sb("og_p", [NP_, D])]
        gu = [m.ps(f"gu{s}", [P, 2, 512]) for s in range(2)]
        dn = [m.ps(f"dn{s}", [P, 512]) for s in range(2)]
        tr = [m.ps(f"tr{b}", [P, 512]) for b in range(2)]

        const_in = m.sem("const_in")
        raw_in = m.sems("raw_in", 4)
        hi_done = m.sem("hi_done")
        lo_done = m.sem("lo_done")
        gran_mm = m.sem("gran_mm")
        part_out = m.sem("part_out")
        summed = m.sem("summed")
        silu = m.sem("silu")
        prod_ready = m.sem("prod_ready")
        hid_hi = m.sem("hid_hi")
        hid_lo = m.sem("hid_lo")
        dpart_out = m.sem("dpart_out")
        dsummed = m.sem("dsummed")
        grow_ready = m.sem("grow_ready")
        xg_in = m.sem("xg_in")
        tok_fill = m.sem("tok_fill")
        tok_hi = m.sem("tok_hi")
        tok_done = m.sem("tok_done")
        row_fill = m.sem("row_fill")
        held_act = m.sem("held_act")
        row_done = m.sem("row_done")
        srow_ready = m.sem("srow_ready")
        scat_out = m.sem("scat_out")
        scat_free = m.sem("scat_free")
        held_pe = m.sem("held_pe")
        held_pool = m.sem("held_pool")
        block = ctx.enter_context(nc.Block())

        def experts(eng, body):
            body(0, 0, True, False)
            with eng.Fori(0, EXPERTS // 2 - 1) as ee:
                for q in range(2):
                    body(2 * ee + 1 + q, 1 - q, False, False)
            body(EXPERTS - 1, 1, False, True)

        @block.sync
        def _(sp):
            sp.dma_start(ident[:], dram["ident"]).then_inc(const_in, 16)
            with sp.Fori(0, EXPERTS) as e:
                with sp.Fori(0, PAIRS) as mm:
                    for c in range(4):
                        sp.wait_ge(lo_done, GR * e + 4 * mm + c + 1)
                        sp.dma_start(raw[c][:, 0:KD, :].rearrange("p k n -> p (k n)"),
                                     dram["w_gu"][bass.ds(2 * FCH * e + 4 * mm + c, 1), :, :].rearrange("u p n -> p (u n)")).then_inc(raw_in[c], 16)
                with sp.Fori(0, KD // 2) as mm:
                    for c in range(4):
                        sp.wait_ge(lo_done, GR * e + 2 * FCH + 4 * mm + c + 1)
                        sp.dma_start(raw[c][:].rearrange("p k n -> p (k n)"),
                                     dram["w_dn"][bass.ds(2 * KD * e + 4 * mm + c, 1), :, :].rearrange("u p n -> p (u n)")).then_inc(raw_in[c], 16)

        @block.gpsimd
        def _(pool):
            pool.sem_inc(scat_free, 1)

            def gather(e):
                for i in range(2):
                    pool.tensor_copy(grow[i][:], res["rows"][i][:, bass.ds(e, 1)]).then_inc(grow_ready, 1)
                pool.wait_ge(grow_ready, 2 * e + 2)
                pool.sem_inc(held_pool, 1)
                for i in range(2):
                    pool.indirect_dma_start(xg[i][:], None, dram["h"], bass.IndirectOffsetOnAxis(ap=grow[i][:], axis=0)).then_inc(xg_in, 16)

            def scatter(e):
                for i in range(2):
                    pool.tensor_copy(srow[i][:], res["rows"][i][:, bass.ds(e, 1)]).then_inc(srow_ready, 1)
                pool.wait_ge(srow_ready, 2 * e + 2)
                pool.wait_ge(row_done, 8 + 4 * e + 4)
                pool.sem_inc(held_pool, 1)
                for i in range(2):
                    pool.indirect_dma_start(dram["acc"], bass.IndirectOffsetOnAxis(ap=srow[i][:], axis=0), og[i][:], None,
                                            compute_op=ALU.add).then_inc(scat_out, 16)
                pool.wait_ge(scat_out, 32 * e + 32)
                pool.sem_inc(scat_free, 1)

            gather(0)
            pool.wait_ge(tok_fill, 4)
            gather(1)
            pool.wait_ge(tok_fill, 8)
            gather(2)
            with pool.Fori(0, EXPERTS - 3) as e:
                scatter(e)
                pool.wait_ge(tok_fill, 4 * e + 12)
                gather(e + 3)
            for e in range(EXPERTS - 3, EXPERTS):
                scatter(e)

        @block.tensor
        def _(pe):
            def fill_tokens(e, b):
                for j in range(2):
                    k = 2 * b + j
                    pe.transpose(tr[b % 2][:, CAP * j:CAP * j + NS], xg[0][:, P * k:P * k + P], ident[:])
                    mm = pe.transpose(tr[b % 2][:, CAP * j + NS:CAP * j + CAP], xg[1][:, P * k:P * k + P], ident[0:NP_, 0:NP_])
                mm.then_inc(tok_fill, 1)

            def fill_rows(b):
                pe.sem_inc(held_pe, 1)
                lo, hi = (0, NS) if b < 2 else (NS, CAP)
                for j in range(4):
                    mm = pe.transpose(tr[b % 2][0:hi - lo, P * j:P * j + P], oT[:, 4 * (b % 2) + j, lo:hi], ident[:])
                mm.then_inc(row_fill, 1)

            def product(out, c, i, x, start, stop):
                pe.matmul(out[:, 0:2 * CAP], whi[c][:, i, :], x, start=start, stop=False)
                return pe.matmul(out[:, 0:CAP], wlo[c][:, i, :], x[:, 0:CAP], start=False, stop=stop)

            def gate_up(e, k, s, q):
                pe.wait_ge(summed, FCH * e + k + 1)
                for a in range(2):
                    pe.wait_ge(lo_done, 4 + GR * e + 2 * k + a + 1)
                    for i in range(KD):
                        mm = product(gu[s][:, a, :], 2 * s + a, i, xgT[q][:, i, :], i == 0, i == KD - 1)
                    mm.then_inc(gran_mm, 1)

            def down(e, j, s):
                pe.wait_ge(dsummed, KD * e + j + 1)
                for a in range(2):
                    pe.wait_ge(hid_lo, FCH * e + HALF * (a + 1))
                    pe.wait_ge(lo_done, 4 + GR * e + 2 * FCH + 2 * j + a + 1)
                    for i in range(HALF):
                        mm = product(dn[s][:], 2 * s + a, i, hid[:, HALF * a + i, :], a == 0 and i == 0, a == 1 and i == HALF - 1)
                    mm.then_inc(gran_mm, 1)

            def body(e, q, first, last):
                pe.wait_ge(tok_done, 4 * e + 4)
                gate_up(e, 0, 0, q)
                if not last:
                    pe.wait_ge(xg_in, 32 * e + 64)
                    pe.wait_ge(row_done, 4 * e + 3)
                    fill_tokens(e + 1, 0)
                    pe.wait_ge(row_done, 4 * e + 4)
                    fill_tokens(e + 1, 1)
                gate_up(e, 1, 1, q)
                if not last:
                    pe.wait_ge(tok_done, 4 * e + 5)
                    fill_tokens(e + 1, 2)
                    pe.wait_ge(tok_done, 4 * e + 6)
                    fill_tokens(e + 1, 3)
                gate_up(e, 2, 0, q)
                if not first:
                    pe.wait_ge(dsummed, 2 + KD * e)
                    if last:
                        pe.wait_ge(row_done, 4 * e + 4)
                    else:
                        pe.wait_ge(tok_done, 4 * e + 8)
                    fill_rows(0)
                    fill_rows(1)
                gate_up(e, 3, 1, q)
                if not first:
                    pe.wait_ge(row_done, 4 * e + 5)
                    fill_rows(2)
                    pe.wait_ge(row_done, 4 * e + 6)
                    fill_rows(3)
                with pe.Fori(2, PAIRS) as mm:
                    for s in range(2):
                        gate_up(e, 2 * mm + s, s, q)
                with pe.Fori(0, KD // 2) as mm:
                    for s in range(2):
                        down(e, 2 * mm + s, s)

            pe.wait_ge(const_in, 16)
            pe.wait_ge(xg_in, 32)
            for b in range(4):
                if b >= 2:
                    pe.wait_ge(tok_done, b - 1)
                fill_tokens(0, b)
            experts(pe, body)
            pe.wait_ge(dsummed, 2 + KD * EXPERTS)
            for b in range(4):
                pe.wait_ge(row_done, 4 * EXPERTS + 3 + b)
                fill_rows(b)

        def splitters(eng, body_part, tokens, rows, first_parts):

            def body(e, q, first, last):
                for k in range(4):
                    body_part(e, k, 0 if k < 2 else 1, k % 2, (e, k + 2, k // 2 + 1, KD))
                    if k < 2 and not last:
                        tokens(e + 1, 1 - q, 2 * k)
                        tokens(e + 1, 1 - q, 2 * k + 1)
                    if k >= 2 and not first:
                        rows(e - 1, 2 * k - 4)
                        rows(e - 1, 2 * k - 3)
                with eng.Fori(2, PAIRS - 1) as mm:
                    for s in range(2):
                        body_part(e, 2 * mm + s, mm, s, (e, 2 * mm + s + 2, mm + 1, KD))
                for s in range(2):
                    body_part(e, FCH - 2 + s, PAIRS - 1, s, (e, FCH + s, PAIRS, HALF))
                with eng.Fori(0, KD // 2 - 1) as mm:
                    for s in range(2):
                        body_part(e, FCH + 2 * mm + s, PAIRS + mm, s, (e, FCH + 2 * mm + s + 2, PAIRS + mm + 1, HALF), 2 * mm + s)
                for s in range(2):
                    j = KD - 2 + s
                    body_part(e, FCH + j, PAIRS + KD // 2 - 1, s, None if last else (e + 1, s, 0, KD), j)

            for b in range(4):
                tokens(0, 0, b)
            for s in range(2):
                for a in range(2):
                    first_parts(s, a)
            experts(eng, body)
            for b in range(4):
                rows(EXPERTS - 1, b)

        @block.scalar
        def _(act):
            act.sem_inc(row_done, 8)

            def split(e, k, mm, s, a, tiles):
                c = 2 * s + a
                act.wait_ge(raw_in[c], 16 * (GR // 4 * e + mm + 1))
                act.copy(whi[c][:, 0:tiles, :], raw[c][:, 0:tiles, :]).then_inc(hi_done, 1)

            def part_(e, k, mm, s, nxt, j=None):
                n = GR * e + 2 * k
                act.wait_ge(gran_mm, n + 2)
                if j is None:
                    f = FCH * e + k
                    act.wait_ge(summed, f + 1)
                    act.copy(part[s][:], gu[s][:, :, CAP:2 * CAP]).then_inc(part_out, 1)
                else:
                    act.wait_ge(dsummed, KD * e + j + 1)
                    act.copy(dpart[s][:], dn[s][:, CAP:2 * CAP]).then_inc(dpart_out, 1)
                if nxt:
                    split(*nxt[:3], s, 0, nxt[3])
                if j is None:
                    act.wait_ge(summed, 2 + f + 1)
                    act.activation(guv[s][:, 0, :], guv[s][:, 0, :], ACT.Silu).then_inc(silu, 1)
                if nxt:
                    split(*nxt[:3], s, 1, nxt[3])
                if j is None:
                    act.wait_ge(prod_ready, f + 1)
                    act.copy(hid[:, bass.ds(k, 1), 0:CAP], prod[s][:].unsqueeze(1)).then_inc(hid_hi, 1)

            def tokens(e, q, b):
                act.wait_ge(tok_fill, 4 * e + b + 1)
                act.copy(xgT[q][:, 2 * b:2 * b + 2, 0:CAP], tr[b % 2][:, 0:2 * CAP].rearrange("p (j c) -> p j c", j=2)).then_inc(tok_hi, 1)

            def rows(e, b):
                i = b // 2
                if b == 0:
                    act.wait_ge(scat_free, e + 1)
                act.wait_ge(row_fill, 4 * e + b + 1)
                act.sem_inc(held_act, 1)
                act.mul(og[i][:, 512 * (b % 2):512 * (b % 2) + 512], tr[b % 2][0:CAPS[1 - i], :],
                        res["gates"][i][:, bass.ds(e, 1)]).then_inc(row_done, 1)

            splitters(act, part_, tokens, rows, lambda s, a: split(0, s, 0, s, a, KD))

        @block.vector
        def _(dve):
            for sem, n in ((lo_done, 4), (summed, 2), (dsummed, 2)):
                dve.sem_inc(sem, n)

            def split(e, k, mm, s, a, tiles):
                c = 2 * s + a
                dve.wait_ge(hi_done, GR * e + 2 * k + a + 1)
                dve.tensor_tensor(wlo[c][:, 0:tiles, :], raw[c][:, 0:tiles, :], whi[c][:, 0:tiles, :].bitcast(F32),
                                  ALU.subtract).then_inc(lo_done, 1)

            def part_(e, k, mm, s, nxt, j=None):
                if j is None:
                    f = FCH * e + k
                    dve.wait_ge(part_out, f + 1)
                    dve.tensor_tensor(guv[s][:], gu[s][:, :, 0:CAP], part[s][:], ALU.add).then_inc(summed, 1)
                else:
                    if not isinstance(e, int) or e > 0:
                        dve.wait_ge(row_fill, 4 * e)
                    dve.wait_ge(dpart_out, KD * e + j + 1)
                    out = oT[:, bass.ds(j, 1), :].rearrange("p j c -> p (j c)")
                    dve.tensor_tensor(out, dn[s][:, 0:CAP], dpart[s][:], ALU.add).then_inc(dsummed, 1)
                if nxt:
                    split(*nxt[:3], s, 0, nxt[3])
                if j is None:
                    dve.wait_ge(silu, f + 1)
                    dve.tensor_tensor(prod[s][:], guv[s][:, 0, :], guv[s][:, 1, :], ALU.mult).then_inc(prod_ready, 1)
                if nxt:
                    split(*nxt[:3], s, 1, nxt[3])
                if j is None:
                    dve.wait_ge(hid_hi, f + 1)
                    ks = bass.ds(k, 1)
                    dve.tensor_tensor(hid[:, ks, CAP:2 * CAP], prod[s][:].unsqueeze(1), hid[:, ks, 0:CAP].bitcast(F32),
                                      ALU.subtract).then_inc(hid_lo, 1)

            def tokens(e, q, b):
                dve.wait_ge(tok_hi, 4 * e + b + 1)
                dve.tensor_tensor(xgT[q][:, 2 * b:2 * b + 2, CAP:2 * CAP], tr[b % 2][:, 0:2 * CAP].rearrange("p (j c) -> p j c", j=2),
                                  xgT[q][:, 2 * b:2 * b + 2, 0:CAP].bitcast(F32), ALU.subtract).then_inc(tok_done, 1)

            splitters(dve, part_, tokens, lambda e, b: None, lambda s, a: split(0, s, 0, s, a, KD))


def stage_finish(nc, dram, res):
    with ExitStack() as ctx:
        m = Mem(nc, ctx, "fin")
        ln = m.sb("ln", [P, 2, D])
        half = m.sb("half", [P, 1])
        r = [m.sb(f"r{s}", [P, D]) for s in range(2)]
        o = [m.sb(f"o{s}", [P, D]) for s in range(2)]
        stats = m.sb("stats", [P, 2, 6])
        mv = [m.sb(f"mv{s}", [P, 2]) for s in range(2)]
        rstd = [m.sb(f"rstd{s}", [P, 1]) for s in range(2)]
        const_in = m.sem("const_in")
        half_set = m.sem("half_set")
        held_dve = m.sem("held_dve")
        held_pool = m.sem("held_pool")
        r_in = m.sems("r_in")
        ln_step = m.sem("ln_step")
        rstd_tmp = m.sem("rstd_tmp")
        rstd_ready = m.sem("rstd_ready")
        scaled = m.sem("scaled")
        gained = m.sem("gained")
        o_ready = m.sem("o_ready")
        o_out = m.sems("o_out")
        block = ctx.enter_context(nc.Block())

        @block.sync
        def _(sp):
            sp.dma_start(ln[:], dram["ln"][:, 2:4, :]).then_inc(const_in, 16)
            with sp.Fori(0, NT // 2) as tt:
                for s in range(2):
                    t = 2 * tt + s
                    sp.wait_ge(scaled, t + 1)
                    sp.dma_start(r[s][:], dram["acc"][bass.ds(t * P, P), :]).then_inc(r_in[s], 16)

        @block.scalar
        def _(act):
            for s in range(2):
                act.sem_inc(o_out[s], 16)
            with act.Fori(0, NT // 2) as tt:
                for s in range(2):
                    t = 2 * tt + s
                    act.wait_ge(o_ready, t + 1)
                    act.dma_start(dram["out"][bass.ds(t * P, P), :], o[s][:]).then_inc(o_out[s], 16)
            for s in range(2):
                act.wait_ge(o_out[s], 16 + 16 * (NT // 2))

        @block.gpsimd
        def _(pool):
            pool.memset(half[:], -0.5).then_inc(half_set, 1)
            pool.wait_ge(half_set, 1)
            pool.wait_ge(const_in, 16)
            with pool.Fori(0, NT // 2) as tt:
                for s in range(2):
                    t = 2 * tt + s
                    pool.wait_ge(ln_step, 3 * t + 3)
                    pool.sem_inc(held_pool, 1)
                    pool.tensor_scalar(rstd[s][:], mv[s][:, 1:2], 1.0, LN_EPS, ALU.mult, ALU.add).then_inc(rstd_tmp, 1)
                    pool.wait_ge(rstd_tmp, t + 1)
                    pool.tensor_tensor(rstd[s][:], rstd[s][:], half[:], ALU.pow).then_inc(rstd_ready, 1)

        @block.vector
        def _(dve):
            dve.sem_inc(scaled, 2)
            dve.wait_ge(const_in, 16)

            def measure(t, tt, s):
                dve.wait_ge(r_in[s], 16 * tt + 16)
                dve.bn_stats(stats[:, 0], r[s][:, 0:512]).then_inc(ln_step, 1)
                dve.bn_stats(stats[:, 1], r[s][:, 512:]).then_inc(ln_step, 1)
                dve.wait_ge(ln_step, 3 * t + 2)
                dve.sem_inc(held_dve, 1)
                dve.bn_aggr(mv[s][:], stats[:]).then_inc(ln_step, 1)
                dve.wait_ge(ln_step, 3 * t + 3)

            def body(t, tt, s, last):
                if not last:
                    measure(t + 1, tt + s, 1 - s)
                dve.wait_ge(rstd_ready, t + 1)
                dve.wait_ge(o_out[s], 16 * tt + 16)
                dve.tensor_scalar(o[s][:], r[s][:], mv[s][:, 0:1], rstd[s][:], ALU.subtract, ALU.mult).then_inc(scaled, 1)
                dve.wait_ge(scaled, 2 + t + 1)
                dve.tensor_tensor(o[s][:], o[s][:], ln[:, 0, :], ALU.mult).then_inc(gained, 1)
                dve.wait_ge(gained, t + 1)
                dve.tensor_tensor(o[s][:], o[s][:], ln[:, 1, :], ALU.add).then_inc(o_ready, 1)

            measure(0, 0, 0)
            with dve.Fori(0, NT // 2 - 1) as tt:
                for s in range(2):
                    body(2 * tt + s, tt, s, False)
            body(NT - 2, NT // 2 - 1, 0, False)
            body(NT - 1, NT // 2 - 1, 1, True)


def residents_first(nc, ctx):
    m = Mem(nc, ctx, "res")
    return {
        "z": m.sb("z", [P, NT, 512]),
        "dt": m.sb("dt", [P, NT, NDT]),
    }


def residents_router(nc, ctx):
    m = Mem(nc, ctx, "rtr")
    return {
        "gates": [m.sb("gates_s", [CAPS[1], EXPERTS]), m.sb("gates_p", [CAPS[0], EXPERTS])],
        "rows": [m.sb("rows_s", [CAPS[1], EXPERTS], U32), m.sb("rows_p", [CAPS[0], EXPERTS], U32)],
    }


def residents_later(nc, ctx):
    m = Mem(nc, ctx, "res")
    return {
        "affT": m.sb("affT", [EXPERTS, TOK]),
        "att": m.sb("att", [P, NT, AW]),
        "y": m.sb("y", [P, NT, SSM_W]),
    }


def layouts(x_prompt, x_sample, w_in, conv_w, conv_b, dt_bias, a_log, d_skip, ssm_norm_w, w_out,
            ln1_g, ln1_b, w_router, w_gate, w_up, w_down, ln2_g, ln2_b):
    a = {}
    x = np.concatenate([np.asarray(x_prompt)[0], np.asarray(x_sample)[0]], axis=0)
    a["x"] = np.ascontiguousarray(x)
    a["xT"] = np.ascontiguousarray(x.T)
    a["w_in"] = np.asarray(w_in)[0]
    taps = np.concatenate([np.asarray(conv_w)[0], np.asarray(conv_b)[0][None]], axis=0)
    a["conv"] = np.ascontiguousarray(taps.T.reshape(NCH, P, CONV_K + 1).transpose(1, 0, 2))
    rows = lambda v: np.ascontiguousarray(np.broadcast_to(np.asarray(v).reshape(1, -1), (P, np.asarray(v).size)))
    a["dt_bias"] = rows(dt_bias)
    a["a_log"] = rows(a_log)
    a["d_skip"] = rows(d_skip)
    a["norm_w"] = rows(ssm_norm_w)
    a["ln"] = np.ascontiguousarray(np.stack([rows(ln1_g), rows(ln1_b), rows(ln2_g), rows(ln2_b)], axis=1))
    a["w_out"] = np.asarray(w_out)[0]
    a["w_router"] = np.asarray(w_router)[0]
    gu = np.stack([np.asarray(w_gate)[0], np.asarray(w_up)[0]])
    gu = gu.reshape(2, EXPERTS, KD, P, FCH, P).transpose(1, 4, 0, 3, 2, 5)
    a["w_gu"] = np.ascontiguousarray(gu).reshape(EXPERTS * FCH * 2, P, KD * P)
    dn = np.asarray(w_down)[0].reshape(EXPERTS, 2, FCH // 2, P, KD, P).transpose(0, 4, 1, 3, 2, 5)
    a["w_dn"] = np.ascontiguousarray(dn).reshape(EXPERTS * KD * 2, P, FCH // 2 * P)
    pos = np.concatenate([np.arange(s) for s in SEQS]).astype(np.float32)
    inv = np.float32(500000.0) ** (-np.arange(HALF_ROT, dtype=np.float32) * np.float32(2.0) / np.float32(ROT))
    ang = (pos[:, None] * inv.astype(np.float32)[None, :]).astype(np.float32)
    cs = np.stack([np.cos(ang), np.sin(ang)], axis=1).astype(np.float32)
    a["rope"] = np.ascontiguousarray(cs.reshape(NT, P, 2, HALF_ROT).transpose(1, 0, 2, 3))
    delta = np.abs(np.arange(MASK_W)[None, :] - MASK_0 - np.arange(P)[:, None])
    times = sum(((delta % dil == 0) & (delta <= window // 2)).astype(np.float64) for window, dil in PATTERNS)
    a["mask"] = np.where(times > 0, np.log(np.maximum(times, 1)), NEG).astype(np.float32)
    i = np.arange(P)
    lt, le = i[:, None] < i[None, :], i[:, None] <= i[None, :]
    a["tri"] = np.ascontiguousarray(np.stack([lt, le, lt.T, le.T, lt | lt.T | le], axis=1).astype(np.float32))
    a["ident"] = np.eye(P, dtype=np.float32)
    return a


def build(nc, dram):
    with ExitStack() as ctx:
        router = residents_router(nc, ctx)
        with ExitStack() as mixer:
            res = residents_first(nc, mixer)
            stage_project(nc, dram, res)
            res.update(residents_later(nc, mixer), **router)
            stage_attend(nc, dram, res)
            stage_ssd(nc, dram, res)
            stage_mix(nc, dram, res)
            stage_choose(nc, dram, res)
        stage_experts(nc, dram, router)
        stage_finish(nc, dram, res)


def kernel(**inputs):
    import concourse.bacc as bacc
    from concourse.bass_utils import run_bass_kernel_spmd

    nc = bacc.Bacc("TRN2", target_bir_lowering=False, num_devices=1)
    arrays = layouts(**inputs)
    dram = {name: nc.dram_tensor(f"in_{name}", a.shape, mybir.dt.from_np(a.dtype), kind="ExternalInput").ap()
            for name, a in arrays.items()}
    scratch = {"v": [TOK, AW], "qkT": [2 * AW, TOK], "xbc": [CONV_CH, TOK], "h": [TOK, D], "acc": [TOK, D]}
    for name, shape in scratch.items():
        dram[name] = nc.dram_tensor(f"tmp_{name}", shape, F32, kind="Internal").ap()
    dram["out"] = nc.dram_tensor("out", [TOK, D], F32, kind="ExternalOutput").ap()
    build(nc, dram)
    r = run_bass_kernel_spmd(nc, [{f"in_{k}": v for k, v in arrays.items()}], core_ids=[0])
    out = np.asarray(r.results[0]["out"])
    return out[None, :SEQS[0]], out[None, SEQS[0]:]
```

```python
from contextlib import ExitStack

import numpy as np
import concourse.bass as bass
from concourse import mybir

F32 = mybir.dt.float32
F32R = mybir.dt.float32r
U32 = mybir.dt.uint32
ALU = mybir.AluOpType
ACT = mybir.ActivationFunctionType

P = 128
SEQS = (512, 1024)
TOK = sum(SEQS)
NT = TOK // P
FIRST_TILE = (0, SEQS[0] // P)
D = 1024
KD = D // P
HEADS, HD = 8, 64
AW = HEADS * HD
ROT = HD // 4
HALF_ROT = ROT // 2
GROUPS, STATE = 2, 128
SSM_W = 512
CONV_CH = SSM_W + 2 * GROUPS * STATE
NCH = CONV_CH // P
CONV_K = 5
NDT = 16
TM_W = 4 * 512 + NDT
EXPERTS = 16
CAPS = tuple(2 * s // EXPERTS for s in SEQS)
CAP = sum(CAPS)
FF = 2816
FCH = FF // P
LN_EPS = 1e-5
RMS_EPS = 1e-5
ALPHA = 2.0 ** 0.25
PATTERNS = ((128, 1), (512, 4), (2048, 16))
MASK_W = 2 * SEQS[1] - P
MASK_0 = SEQS[1] - P
NEG = -1.0e30


class Mem:

    def __init__(self, nc, ctx, tag):
        self.nc, self.ctx, self.tag = nc, ctx, tag

    def sb(self, name, shape, dt=F32):
        return self.ctx.enter_context(self.nc.sbuf_tensor(f"{self.tag}_{name}", shape, dt))

    def ps(self, name, shape, dt=F32):
        return self.ctx.enter_context(self.nc.psum_tensor(f"{self.tag}_{name}", shape, dt))

    def sem(self, name):
        return self.ctx.enter_context(self.nc.semaphore(f"{self.tag}_{name}"))

    def sems(self, name, n=2):
        return [self.sem(f"{name}{i}") for i in range(n)]


def stage_project(nc, dram, res):
    with ExitStack() as ctx:
        m = Mem(nc, ctx, "prj")
        xT = m.sb("xT", [P, KD, TOK])
        wtm = m.sb("wtm", [P, KD, TM_W])
        wfm = [m.sb(f"wfm{s}", [P, KD, P]) for s in range(2)]
        RW = TOK + 4 * (CONV_K // 2)
        CW = RW - (CONV_K - 1)
        raw = [m.sb(f"raw{s}", [P, RW]) for s in range(2)]
        acc = m.sb("acc", [P, CW])
        xbc = [m.sb(f"xbc{s}", [P, TOK]) for s in range(2)]
        convw = m.sb("convw", [P, NCH, CONV_K + 1])
        xt = [m.sb(f"xt{s}", [P, KD, P]) for s in range(2)]
        qk = [m.sb(f"qk{s}", [P, 2 * HEADS, HD]) for s in range(2)]
        rope = m.sb("rope", [P, 4, 2 * HEADS, HALF_ROT])
        vt = [m.sb(f"vt{s}", [P, AW]) for s in range(2)]
        qkT = [m.sb(f"qkT{s}", [P, KD, P]) for s in range(2)]
        cs = m.sb("cs", [P, NT, 2, HALF_ROT])
        ident = m.sb("ident", [P, P])
        ps = m.ps("ps", [P, 8, 512])

        const_in = m.sem("const_in")
        x_in = m.sems("x_in", 3)
        wtm_in = m.sem("wtm_in")
        wfm_in = m.sems("wfm_in")
        fm_mm = m.sem("fm_mm")
        raw_ready = m.sem("raw_ready")
        margins = m.sem("margins")
        conv_step = m.sem("conv_step")
        xbc_ready = m.sem("xbc_ready")
        xbc_out = m.sem("xbc_out")
        xbc_free = m.sem("xbc_free")
        xt_in = m.sems("xt_in")
        tm_mm = m.sem("tm_mm")
        qk_ready = m.sem("qk_ready")
        v_ready = m.sem("v_ready")
        z_ready = m.sem("z_ready")
        dt_ready = m.sem("dt_ready")
        rope_step = m.sem("rope_step")
        tr_mm = m.sem("tr_mm")
        qkT_ready = m.sem("qkT_ready")
        vq_out = m.sem("vq_out")
        vq_free = m.sem("vq_free")
        wfm_src = dram["w_in"][:, 4 * 512:4 * 512 + CONV_CH].rearrange("(k p) (c n) -> p k c n", p=P, n=P)
        w_src = dram["w_in"].rearrange("(k p) n -> p k n", p=P)
        xT_src = dram["xT"].rearrange("(k p) t -> p k t", p=P)
        block = ctx.enter_context(nc.Block())
        ROPE_STEPS = 6

        @block.sync
        def _(sp):
            sp.dma_start(wfm[0][:], wfm_src[:, :, 0, :]).then_inc(wfm_in[0], 16)
            for g in range(3):
                sp.dma_start(xT[:, :, 512 * g:512 * g + 512], xT_src[:, :, 512 * g:512 * g + 512]).then_inc(x_in[g], 16)
            sp.dma_start(wfm[1][:], wfm_src[:, :, 1, :]).then_inc(wfm_in[1], 16)
            with sp.Fori(1, NCH // 2) as cc:
                for s in range(2):
                    c = 2 * cc + s
                    sp.wait_ge(fm_mm, 3 * c + 3)
                    sp.dma_start(wfm[s][:], wfm_src[:, :, bass.ds(c, 1), :].rearrange("p k c n -> p k (c n)")).then_inc(wfm_in[s], 16)
            with sp.Fori(0, NT // 2) as tt:
                for s in range(2):
                    t = 2 * tt + s
                    sp.wait_ge(tm_mm, 5 * t + 5)
                    sp.dma_start(xt[s][:], xT_src[:, :, bass.ds(t * P, P)]).then_inc(xt_in[s], 16)

        @block.tensor
        def _(pe):
            pe.sem_inc(fm_mm, 6)
            pe.sem_inc(tm_mm, 10)
            pe.sem_inc(tr_mm, 2)
            def channels(c, cc, s):
                pe.wait_ge(wfm_in[s], 16 * cc + 16)
                for g in range(3):
                    if isinstance(c, int) and c == 0:
                        pe.wait_ge(x_in[g], 16)
                    pe.wait_ge(raw_ready, 3 * c + g + 1)
                    for k in range(KD):
                        mm = pe.matmul(ps[:, 3 * s + g, :], wfm[s][:, k, :], xT[:, k, 512 * g:512 * g + 512],
                                       start=(k == 0), stop=(k == KD - 1))
                    mm.then_inc(fm_mm, 1)

            channels(0, 0, 0)
            channels(1, 0, 1)
            with pe.Fori(1, NCH // 2) as cc:
                for s in range(2):
                    channels(2 * cc + s, cc, s)
            pe.wait_ge(raw_ready, 6 + 3 * NCH)
            pe.wait_ge(wtm_in, 32)
            pe.wait_ge(const_in, 48)
            with pe.Fori(0, NT // 2) as tt:
                for s in range(2):
                    t = 2 * tt + s
                    pe.wait_ge(xt_in[s], 16 * tt + 16)
                    for n in range(5):
                        if n < 2:
                            pe.wait_ge(qk_ready, 2 * t + n + 1)
                        if n == 2:
                            pe.wait_ge(v_ready, t + 1)
                        if n == 3:
                            pe.wait_ge(z_ready, t + 1)
                        if n == 4:
                            pe.wait_ge(dt_ready, t + 1)
                        w = 512 if n < 4 else NDT
                        for k in range(KD):
                            mm = pe.matmul(ps[:, n, 0:w], xt[s][:, k, :], wtm[:, k, 512 * n:512 * n + w],
                                           start=(k == 0), stop=(k == KD - 1))
                        mm.then_inc(tm_mm, 1)
                    pe.wait_ge(rope_step, ROPE_STEPS * t + ROPE_STEPS)
                    pe.wait_ge(qkT_ready, 2 * t + 2)
                    for j in range(KD):
                        src = qk[s][:, 2 * j:2 * j + 2, :].rearrange("p a e -> p (a e)")
                        mm = pe.transpose(ps[:, 6 + j // 4, P * (j % 4):P * (j % 4) + P], src, ident[:])
                    mm.then_inc(tr_mm, 1)

        @block.scalar
        def _(act):
            act.sem_inc(raw_ready, 6)
            act.sem_inc(xbc_ready, 1)
            act.sem_inc(qk_ready, 2)
            act.sem_inc(v_ready, 1)
            act.sem_inc(z_ready, 1)
            act.wait_ge(x_in[2], 16)
            act.dma_start(wtm[:, :, 0:2048], w_src[:, :, 0:2048]).then_inc(wtm_in, 16)
            act.dma_start(wtm[:, :, 2048:TM_W], w_src[:, :, 2048 + CONV_CH:]).then_inc(wtm_in, 16)
            act.wait_ge(margins, 2)
            starts = (2, 2 + SEQS[0] + 4, 2 + SEQS[0] + 4 + 512)

            def silu_out(c, cc, s):
                act.wait_ge(conv_step, 10 + 5 * c + 5)
                act.wait_ge(xbc_free, c + 1)
                act.activation(xbc[s][:, 0:SEQS[0]], acc[:, 0:SEQS[0]], ACT.Silu)
                act.activation(xbc[s][:, SEQS[0]:], acc[:, SEQS[0] + 4:], ACT.Silu).then_inc(xbc_ready, 1)

            with act.Fori(0, NCH // 2) as cc:
                for s in range(2):
                    c = 2 * cc + s
                    act.wait_ge(conv_step, 5 * c + 5)
                    for g in range(3):
                        act.wait_ge(fm_mm, 6 + 3 * c + g + 1)
                        act.copy(raw[s][:, starts[g]:starts[g] + 512], ps[:, 3 * s + g, :]).then_inc(raw_ready, 1)
                    silu_out(c, cc, s)
            with act.Fori(0, NT // 2) as tt:
                for s in range(2):
                    t = 2 * tt + s
                    act.wait_ge(tr_mm, t + 1)
                    act.wait_ge(tm_mm, 10 + 5 * t + 1)
                    act.mul(qk[s][:, 0:HEADS, :], ps[:, 0, :].rearrange("p (h e) -> p h e", e=HD), HD ** -0.5).then_inc(qk_ready, 1)
                    act.wait_ge(tm_mm, 10 + 5 * t + 2)
                    act.copy(qk[s][:, HEADS:, :], ps[:, 1, :].rearrange("p (h e) -> p h e", e=HD)).then_inc(qk_ready, 1)
                    act.wait_ge(tm_mm, 10 + 5 * t + 3)
                    act.wait_ge(vq_free, t + 1)
                    act.copy(vt[s][:], ps[:, 2, :]).then_inc(v_ready, 1)
                    act.wait_ge(tm_mm, 10 + 5 * t + 4)
                    act.activation(res["z"][:, bass.ds(t, 1), :], ps[:, 3:4, :], ACT.Silu).then_inc(z_ready, 1)

        @block.vector
        def _(dve):
            dve.sem_inc(conv_step, 10)
            dve.sem_inc(dt_ready, 1)
            dve.sem_inc(qkT_ready, 2)
            for s in range(2):
                dve.memset(raw[s][:, 0:2], 0.0)
                dve.memset(raw[s][:, 2 + SEQS[0]:2 + SEQS[0] + 4], 0.0)
                dve.memset(raw[s][:, RW - 2:RW], 0.0).then_inc(margins, 1)
            dve.wait_ge(margins, 2)
            dve.wait_ge(const_in, 48)
            with dve.Fori(0, NCH // 2) as cc:
                for s in range(2):
                    c = 2 * cc + s
                    dve.wait_ge(raw_ready, 6 + 3 * c + 3)
                    dve.wait_ge(xbc_ready, c + 1)
                    dve.tensor_scalar(acc[:], raw[s][:, 0:CW], convw[:, bass.ds(c, 1), 0], convw[:, bass.ds(c, 1), CONV_K],
                                      ALU.mult, ALU.add).then_inc(conv_step, 1)
                    for k in range(1, CONV_K):
                        dve.wait_ge(conv_step, 10 + 5 * c + k)
                        dve.scalar_tensor_tensor(acc[:], raw[s][:, k:k + CW], convw[:, bass.ds(c, 1), k], acc[:],
                                                 ALU.mult, ALU.add).then_inc(conv_step, 1)
            with dve.Fori(0, NT // 2) as tt:
                for s in range(2):
                    t = 2 * tt + s
                    n0 = ROPE_STEPS * t
                    dve.wait_ge(qk_ready, 2 + 2 * t + 2)
                    t1 = qk[s][:, :, 0:HALF_ROT]
                    t2 = qk[s][:, :, HALF_ROT:ROT]
                    cos = cs[:, bass.ds(t, 1), 0, :].broadcast_to([P, 2 * HEADS, HALF_ROT])
                    sin = cs[:, bass.ds(t, 1), 1, :].broadcast_to([P, 2 * HEADS, HALF_ROT])
                    for n, (a, b) in enumerate(((t1, cos), (t2, sin), (t2, cos), (t1, sin))):
                        dve.tensor_tensor(rope[:, n], a, b, ALU.mult).then_inc(rope_step, 1)
                    dve.wait_ge(rope_step, n0 + 4)
                    dve.tensor_tensor(t1, rope[:, 0], rope[:, 1], ALU.subtract).then_inc(rope_step, 1)
                    dve.tensor_tensor(t2, rope[:, 2], rope[:, 3], ALU.add).then_inc(rope_step, 1)
                    dve.wait_ge(rope_step, n0 + 6)
                    dve.wait_ge(tm_mm, 10 + 5 * t + 5)
                    dve.tensor_copy(res["dt"][:, bass.ds(t, 1), :], ps[:, 4:5, 0:NDT]).then_inc(dt_ready, 1)
                    dve.wait_ge(tr_mm, 2 + t + 1)
                    dve.wait_ge(vq_free, t + 1)
                    for b in range(2):
                        dve.tensor_copy(qkT[s][:, 4 * b:4 * b + 4, :],
                                        ps[:, 6 + b, :].rearrange("p (j t) -> p j t", j=4)).then_inc(qkT_ready, 1)

        @block.gpsimd
        def _(pool):
            pool.sem_inc(xbc_free, 2)
            pool.sem_inc(vq_free, 2)
            pool.dma_start(cs[:], dram["rope"]).then_inc(const_in, 16)
            pool.dma_start(convw[:], dram["conv"]).then_inc(const_in, 16)
            pool.dma_start(ident[:], dram["ident"]).then_inc(const_in, 16)
            with pool.Fori(0, NCH // 2) as cc:
                for s in range(2):
                    c = 2 * cc + s
                    pool.wait_ge(xbc_ready, 1 + c + 1)
                    dst = dram["xbc"][bass.ds(c * P, P), :]
                    pool.dma_start(dst, xbc[s][:]).then_inc(xbc_out, 16)
                    pool.wait_ge(xbc_out, 16 * c + 16)
                    pool.sem_inc(xbc_free, 1)
            with pool.Fori(0, NT // 2) as tt:
                for s in range(2):
                    t = 2 * tt + s
                    pool.wait_ge(v_ready, 1 + t + 1)
                    pool.dma_start(dram["v"][bass.ds(t * P, P), :], vt[s][:]).then_inc(vq_out, 16)
                    pool.wait_ge(qkT_ready, 2 + 2 * t + 2)
                    pool.dma_start(dram["qkT"][:, bass.ds(t * P, P)].rearrange("(k p) t -> p k t", p=P), qkT[s][:]).then_inc(vq_out, 16)
                    pool.wait_ge(vq_out, 32 * t + 32)
                    pool.sem_inc(vq_free, 1)
            pool.wait_ge(dt_ready, 1 + NT)
            pool.wait_ge(z_ready, 1 + NT)


def stage_attend(nc, dram, res):
    ITEMS = NT
    PV0 = 2 * ITEMS
    SPLITS = 4
    first_item = (0, SEQS[0] // P)

    def shape_of(j):
        return (0, SEQS[0], j) if j < first_item[1] else (SEQS[0], SEQS[1], j - first_item[1])

    with ExitStack() as ctx:
        m = Mem(nc, ctx, "att")
        raw = [m.sb(f"raw{s}", [P, 2, TOK]) for s in range(2)]
        q2 = [m.sb(f"q2{s}", [P, TOK], F32R) for s in range(2)]
        k2 = [m.sb(f"k2{s}", [P, TOK], F32R) for s in range(2)]
        klo = [m.sb(f"klo{s}", [HD, TOK], F32R) for s in range(2)]
        v = [m.sb(f"v{s}", [P, NT, HD]) for s in range(2)]
        mask = m.sb("mask", [P, MASK_W])
        ident = m.sb("ident", [P, P])
        neg = [m.sb(f"neg{s}", [P, SEQS[1]]) for s in range(2)]
        negmax = m.sb("negmax", [P, 2])
        probs = [m.sb(f"probs{s}", [P, SEQS[1]]) for s in range(2)]
        pT = [m.sb(f"pT{s}", [P, 2, 4, P]) for s in range(2)]
        den = m.sb("den", [P, 4])
        rden = m.sb("rden", [P, 2])
        sc = [m.ps(f"sc{s}", [P, SEQS[1]]) for s in range(2)]
        trA = m.ps("trA", [P, 4, P])
        trB = m.ps("trB", [P, 4, P])
        o = [m.ps(f"o{s}", [P, 512]) for s in range(2)]

        const_in = m.sem("const_in")
        qk_in = m.sems("qk_in")
        v_in = m.sems("v_in")
        split_done = m.sem("split_done")
        score_mm = m.sem("score_mm")
        masked = m.sem("masked")
        exp_done = m.sem("exp_done")
        tr_mm = m.sem("tr_mm")
        copyA = m.sem("copyA")
        copyB = m.sem("copyB")
        pv_mm = m.sem("pv_mm")
        recip = m.sem("recip")
        normed = m.sem("normed")
        held_sp = res["held_sp"]
        held_pool = res["held_pool"]
        held_dve = res["held_dve"]
        block = ctx.enter_context(nc.Block())

        def heads(eng, body):
            with eng.Fori(0, HEADS // 2 - 1) as hh:
                for s in range(2):
                    body(2 * hh + s, hh, s, False)
            body(HEADS - 2, HEADS // 2 - 1, 0, False)
            body(HEADS - 1, HEADS // 2 - 1, 1, True)

        @block.sync
        def _(sp):
            sp.dma_start(mask[:], dram["mask"]).then_inc(const_in, 16)
            sp.dma_start(ident[:], dram["ident"]).then_inc(const_in, 16)
            with sp.Fori(0, HEADS // 2) as hh:
                for s in range(2):
                    h = 2 * hh + s
                    sp.wait_ge(split_done, SPLITS * h + SPLITS)
                    sp.sem_inc(held_sp, 1)
                    for n in range(2):
                        for half in range(2):
                            sp.dma_start(raw[s][HD * half:HD * half + HD, n, :],
                                         dram["qkT"][bass.ds(n * AW + h * HD, HD), :]).then_inc(qk_in[s], 16)
                    sp.wait_ge(pv_mm, ITEMS * h + ITEMS)
                    sp.sem_inc(held_sp, 1)
                    sp.dma_start(v[s][:], dram["v"][:, bass.ds(h * HD, HD)].rearrange("(t p) e -> p t e", p=P)).then_inc(v_in[s], 16)

        @block.gpsimd
        def _(pool):
            pool.sem_inc(split_done, 2 * SPLITS)

            def split(h, hh, s):
                n0 = SPLITS * h + 2 * SPLITS
                pool.wait_ge(pv_mm, ITEMS * h + ITEMS)
                pool.wait_ge(qk_in[s], 64 * hh + 64)
                pool.wait_ge(split_done, n0)
                pool.sem_inc(held_pool, 1)
                pool.tensor_copy(q2[s][:], raw[s][:, 0, :]).then_inc(split_done, 1)
                pool.tensor_copy(k2[s][:], raw[s][:, 1, :]).then_inc(split_done, 1)
                pool.wait_ge(split_done, n0 + 2)
                pool.tensor_tensor(q2[s][HD:, :], raw[s][HD:, 0, :], q2[s][HD:, :].bitcast(F32), ALU.subtract).then_inc(split_done, 1)
                pool.wait_ge(split_done, n0 + 3)
                pool.tensor_tensor(klo[s][:], raw[s][0:HD, 1, :], k2[s][0:HD, :].bitcast(F32), ALU.subtract).then_inc(split_done, 1)

            split(1, 0, 1)
            with pool.Fori(1, HEADS // 2) as hh:
                for s in range(2):
                    split(2 * hh + s, hh, s)

        @block.tensor
        def _(pe):
            pe.sem_inc(tr_mm, 2)
            pe.sem_inc(pv_mm, PV0)

            def scores(h, hh, s, j):
                n = ITEMS * h + j
                t0, S, i = shape_of(j)
                if j == 0:
                    pe.wait_ge(split_done, SPLITS * (h + 3))
                pe.wait_ge(masked, n + 1)
                for b in range(S // 512):
                    out, qs, ks = sc[j % 2][:, 512 * b:512 * b + 512], slice(t0 + P * i, t0 + P * i + P), slice(t0 + 512 * b, t0 + 512 * b + 512)
                    pe.matmul(out, q2[s][:, qs], k2[s][:, ks], start=True, stop=False)
                    mm = pe.matmul(out, q2[s][0:HD, qs], klo[s][:, ks], start=False, stop=True)
                mm.then_inc(score_mm, 1)

            def transposes(h, j):
                n = ITEMS * h + j
                nb = shape_of(j)[1] // P
                pe.wait_ge(exp_done, 2 + n + 1)
                pe.wait_ge(copyA, n + 1)
                pe.wait_ge(copyB, n + 1)
                for b in range(nb):
                    bank = trA if b < nb // 2 else trB
                    mm = pe.transpose(bank[:, b % (nb // 2), :], probs[j % 2][:, P * b:P * b + P], ident[:])
                mm.then_inc(tr_mm, 1)

            def values(h, hh, s, j):
                n = ITEMS * h + j
                if j == 0:
                    pe.wait_ge(v_in[s], 16 * hh + 16)
                t0, S, i = shape_of(j)
                nb = S // P
                pe.wait_ge(copyA, 1 + n + 1)
                pe.wait_ge(copyB, 1 + n + 1)
                pe.wait_ge(normed, n + 3)
                for b in range(nb):
                    mm = pe.matmul(o[j % 2][:, 0:HD], pT[j % 2][:, b // (nb // 2), b % (nb // 2), :],
                                   v[s][:, t0 // P + b, :], start=(b == 0), stop=(b == nb - 1))
                mm.then_inc(pv_mm, 1)

            def body(h, hh, s, last):
                for j in range(ITEMS):
                    if j + 2 < ITEMS:
                        scores(h, hh, s, j + 2)
                    elif not last:
                        scores(h + 1, hh + s, 1 - s, j + 2 - ITEMS)
                    if j + 1 < ITEMS:
                        transposes(h, j + 1)
                    elif not last:
                        transposes(h + 1, 0)
                    values(h, hh, s, j)

            pe.wait_ge(const_in, 32)
            scores(0, 0, 0, 0)
            scores(0, 0, 0, 1)
            transposes(0, 0)
            heads(pe, body)

        @block.vector
        def _(dve):
            dve.sem_inc(masked, 2)
            dve.sem_inc(copyA, 1)
            dve.sem_inc(normed, 4)

            def mask_scores(h, j):
                n = ITEMS * h + j
                t0, S, i = shape_of(j)
                dve.wait_ge(score_mm, n + 1)
                dve.wait_ge(exp_done, n + 1)
                dve.sem_inc(held_dve, 1)
                at = MASK_0 - P * i
                dve.tensor_tensor_reduce(neg[j % 2][:, 0:S], sc[j % 2][:, 0:S], mask[:, at:at + S], -1.0, 3.0e38,
                                         ALU.add, ALU.min, negmax[:, j % 2:j % 2 + 1]).then_inc(masked, 1)

            def copy_half(h, j):
                n = ITEMS * h + j
                nb = shape_of(j)[1] // P
                dve.wait_ge(tr_mm, 2 + n + 1)
                dve.wait_ge(pv_mm, PV0 - 2 + n + 1)
                dve.tensor_copy(pT[j % 2][:, 0, 0:nb // 2, :], trA[:, 0:nb // 2, :]).then_inc(copyA, 1)

            def normalise(h, j):
                n = ITEMS * h + j
                dve.wait_ge(exp_done, 2 + n + 1)
                dve.wait_ge(normed, 4 + n - 1)
                dve.reciprocal(rden[:, j % 2:j % 2 + 1], den[:, j % 4:j % 4 + 1]).then_inc(recip, 1)
                dve.wait_ge(recip, n + 1)
                dve.wait_ge(pv_mm, PV0 + n + 1)
                out = res["att"][:, j, bass.ds(h * HD, HD)]
                dve.tensor_scalar(out, o[j % 2][:, 0:HD], rden[:, j % 2:j % 2 + 1], None, ALU.mult).then_inc(normed, 1)

            def body(h, hh, s, last):
                for j in range(ITEMS):
                    if j + 2 < ITEMS:
                        mask_scores(h, j + 2)
                    elif not last:
                        mask_scores(h + 1, j + 2 - ITEMS)
                    if j + 1 < ITEMS:
                        copy_half(h, j + 1)
                    elif not last:
                        copy_half(h + 1, 0)
                    normalise(h, j)

            dve.wait_ge(const_in, 32)
            dve.wait_ge(split_done, 2 * SPLITS + 2)
            dve.tensor_tensor(q2[0][HD:, :], raw[0][HD:, 0, :], q2[0][HD:, :].bitcast(F32), ALU.subtract).then_inc(split_done, 1)
            dve.tensor_tensor(klo[0][:], raw[0][0:HD, 1, :], k2[0][0:HD, :].bitcast(F32), ALU.subtract).then_inc(split_done, 1)
            mask_scores(0, 0)
            mask_scores(0, 1)
            copy_half(0, 0)
            heads(dve, body)

        @block.scalar
        def _(act):
            act.sem_inc(exp_done, 2)
            act.sem_inc(copyB, 1)

            def exponent(h, j):
                n = ITEMS * h + j
                S = shape_of(j)[1]
                act.wait_ge(masked, 2 + n + 1)
                act.wait_ge(tr_mm, n + 1)
                act.wait_ge(normed, n + 1)
                act.activation(probs[j % 2][:, 0:S], neg[j % 2][:, 0:S], ACT.Exp, bias=negmax[:, j % 2:j % 2 + 1],
                               scale=-1.0, accum_out=den[:, j % 4:j % 4 + 1]).then_inc(exp_done, 1)

            def copy_half(h, j):
                n = ITEMS * h + j
                nb = shape_of(j)[1] // P
                act.wait_ge(tr_mm, 2 + n + 1)
                act.wait_ge(pv_mm, PV0 - 2 + n + 1)
                act.copy(pT[j % 2][:, 1, 0:nb // 2, :], trB[:, 0:nb // 2, :]).then_inc(copyB, 1)

            def body(h, hh, s, last):
                for j in range(ITEMS):
                    if j + 1 < ITEMS:
                        copy_half(h, j + 1)
                    elif not last:
                        copy_half(h + 1, 0)
                    if j + 2 < ITEMS:
                        exponent(h, j + 2)
                    elif not last:
                        exponent(h + 1, j + 2 - ITEMS)

            act.wait_ge(split_done, 2 * SPLITS)
            act.wait_ge(qk_in[0], 64)
            act.copy(q2[0][:], raw[0][:, 0, :]).then_inc(split_done, 1)
            act.copy(k2[0][:], raw[0][:, 1, :]).then_inc(split_done, 1)
            exponent(0, 0)
            exponent(0, 1)
            copy_half(0, 0)
            heads(act, body)


def stage_ssd(nc, dram, res):
    GH = HEADS // GROUPS
    HP = GH * HD
    LT, LE, GT, GE, ONE = range(5)
    TO_END, TO_START, FROM_START, FROM_END, ALL_F, ALL_B = range(6)
    LOG_TERMS = 9

    with ExitStack() as ctx:
        m = Mem(nc, ctx, "ssd")
        tri = m.sb("tri", [P, 5, P])
        ident = m.sb("ident", [P, P])
        dtb = m.sb("dtb", [P, NDT])
        alog = m.sb("alog", [P, NDT])
        dsk = m.sb("dsk", [P, HEADS])
        dtr = res["dt"]
        w1 = m.sb("w1", [P, NT, NDT])
        w2 = m.sb("w2", [P, NT, NDT])
        w3 = m.sb("w3", [P, NT, NDT])
        w4 = m.sb("w4", [P, NT, NDT])
        dt = m.sb("dt", [P, NT, NDT])
        dtA = m.sb("dtA", [P, NT, NDT])
        ex = m.sb("ex", [P, 6, NT, HEADS])
        wdt = m.sb("wdt", [P, 2, NT, HEADS])
        xb = [m.sb(f"xb{s}", [P, NCH, P]) for s in range(2)]
        rf = [m.sb(f"rf{s}", [P, HEADS, P]) for s in range(2)]
        rb = [m.sb(f"rb{s}", [P, HEADS, P]) for s in range(2)]
        E = [m.sb(f"E{s}", [P, GROUPS, GH, P]) for s in range(2)]
        cb = [m.sb(f"cb{s}", [P, 2, GROUPS, P]) for s in range(2)]
        W = [m.sb(f"W{s}", [P, 2, HEADS, P]) for s in range(2)]
        xtok = [m.sb(f"xtok{s}", [P, HEADS, HD]) for s in range(2)]
        btok = [m.sb(f"btok{s}", [P, GROUPS, P]) for s in range(2)]
        xdt = [m.sb(f"xdt{s}", [P, 3, HEADS, HD]) for s in range(2)]
        xst = [m.sb(f"xst{s}", [P, 2, HEADS, HD]) for s in range(2)]
        Sf = m.sb("Sf", [P, HEADS, HD])
        Sb = [m.sb(f"Sb{s}", [P, HEADS, HD]) for s in range(2)]
        stb = m.sb("stb", [P, NT, HEADS, HD])
        yo = [m.sb(f"yo{s}", [P, HEADS, HD]) for s in range(2)]
        cT = [m.sb(f"cT{s}", [P, GROUPS, P]) for s in range(2)]
        psx = m.ps("psx", [P, 512])
        psb = m.ps("psb", [P, 2, GROUPS, P])
        seg = m.ps("seg", [P, HEADS, P])
        psy = m.ps("psy", [P, HEADS, HD])
        psf = m.ps("psf", [P, HEADS, HD])
        pss = m.ps("pss", [P, HEADS, HD])
        pso = m.ps("pso", [P, HEADS, HD])

        pob = [pso[:], psx[:].rearrange("p (h e) -> p h e", e=HD)]

        const_in = m.sem("const_in")
        pre = m.sem("pre")
        pre_exp = m.sem("pre_exp")
        sums_mm = m.sem("sums_mm")
        tables = m.sem("tables")
        xb_in = m.sems("xb_in")
        tok_mm = m.sem("tok_mm")
        tok_ready = m.sem("tok_ready")
        cb_mm = m.sem("cb_mm")
        cb_ready = m.sem("cb_ready")
        rf_ready = m.sem("rf_ready")
        rb_ready = m.sem("rb_ready")
        seg_mm = m.sem("seg_mm")
        e_ready = m.sem("e_ready")
        w_ready = m.sem("w_ready")
        xdt_ready = m.sem("xdt_ready")
        xst_ready = m.sem("xst_ready")
        y_mm = m.sem("y_mm")
        st_mm = m.sem("st_mm")
        off_mm = m.sem("off_mm")
        stb_ready = m.sem("stb_ready")
        sf_zero = m.sem("sf_zero")
        sf_step = m.sem("sf_step")
        y_step = m.sem("y_step")
        cT_in = m.sems("cT_in")
        offb_mm = m.sem("offb_mm")
        sb_zero = m.sem("sb_zero")
        sb_step = m.sem("sb_step")
        yb_step = m.sem("yb_step")
        yb_add = m.sem("yb_add")
        held_pool = res["held_pool"]
        held_sp = res["held_sp"]
        held_dve = res["held_dve"]
        block = ctx.enter_context(nc.Block())
        FIRST = FIRST_TILE[1]

        def chunks(eng, body, between):
            with eng.Fori(0, FIRST // 2) as tt:
                for s in range(2):
                    body(2 * tt + s, tt, s, 2)
            between()
            with eng.Fori(FIRST // 2, NT // 2 - 1) as tt:
                for s in range(2):
                    body(2 * tt + s, tt, s, 2)
            body(NT - 2, NT // 2 - 1, 0, 1)
            body(NT - 1, NT // 2 - 1, 1, 0)

        def back(eng, body, between):
            with eng.Fori(0, (NT - FIRST) // 2) as ii:
                for s in range(2):
                    body(2 * ii + s, ii, s)
            between()
            with eng.Fori((NT - FIRST) // 2, NT // 2) as ii:
                for s in range(2):
                    body(2 * ii + s, ii, s)

        @block.sync
        def _(sp):
            for dst, name in ((tri, "tri"), (ident, "ident"), (dtb, "dt_bias"), (alog, "a_log"), (dsk, "d_skip")):
                sp.dma_start(dst[:], dram[name]).then_inc(const_in, 16)
            src = dram["xbc"].rearrange("(c p) t -> p c t", p=P)
            with sp.Fori(0, NT // 2) as tt:
                for s in range(2):
                    t = 2 * tt + s
                    sp.wait_ge(off_mm, t + 1)
                    sp.dma_start(xb[s][:], src[:, :, bass.ds(t * P, P)]).then_inc(xb_in[s], 16)
            with sp.Fori(0, NT // 2) as ii:
                for s in range(2):
                    i = 2 * ii + s
                    sp.wait_ge(offb_mm, i + 1)
                    sp.sem_inc(held_sp, 1)
                    at = (NT - 1) * P - i * P
                    sp.dma_start(cT[s][:], src[:, NCH - GROUPS:, bass.ds(at, P)]).then_inc(cT_in[s], 16)

        @block.tensor
        def _(pe):
            for sem, n in ((seg_mm, 2), (y_mm, 2), (st_mm, 2), (off_mm, 2), (offb_mm, 2)):
                pe.sem_inc(sem, n)
            pe.wait_ge(const_in, 80)
            pe.wait_ge(tables, 1)
            sums = ((GT, 0), (LT, HEADS), (LE, 0), (GE, HEADS), (ONE, 0), (ONE, HEADS))
            flat = seg[:].rearrange("p h l -> p (h l)")
            for n, (tr, off) in enumerate(sums):
                at = 512 * (n // 3) + NT * HEADS * (n % 3)
                mm = pe.matmul(flat[:, at:at + NT * HEADS], tri[:, tr, :], dtA[:, :, off:off + HEADS], start=True, stop=True)
            mm.then_inc(sums_mm, 1)
            pe.wait_ge(pre_exp, 4)

            def to_tokens(t, tt, s):
                pe.wait_ge(xb_in[s], 16 * tt + 16)
                pe.wait_ge(tok_ready, 2 * t + 2)
                pe.wait_ge(cb_ready, 2 * t + 2)
                for j in range(SSM_W // P):
                    pe.transpose(psx[:, P * j:P * j + P], xb[s][:, j, :], ident[:])
                for g in range(GROUPS):
                    mm = pe.transpose(psb[:, 0, g, :], xb[s][:, SSM_W // P + g, :], ident[:])
                mm.then_inc(tok_mm, 1)

            def products(t, s):
                pe.wait_ge(tok_ready, 2 + 2 * t + 2)
                for g in range(GROUPS):
                    mm = pe.matmul(psb[:, 1, g, :], xb[s][:, SSM_W // P + g, :], xb[s][:, SSM_W // P + GROUPS + g, :],
                                   start=True, stop=True)
                mm.then_inc(cb_mm, 1)

            def segments(t, s):
                pe.wait_ge(rf_ready, t + 1)
                pe.wait_ge(rb_ready, t + 1)
                pe.wait_ge(e_ready, t + 1)
                for half in range(2):
                    hs = slice(GH * half, GH * half + GH)
                    pe.matmul(seg[:, hs, :], tri[:, GT, :], rf[s][:, hs, :], start=True, stop=False)
                    mm = pe.matmul(seg[:, hs, :], tri[:, LT, :], rb[s][:, hs, :], start=False, stop=True)
                mm.then_inc(seg_mm, 1)

            def body(t, tt, s, ahead):
                if ahead >= 1:
                    to_tokens(t + 1, tt + s, 1 - s)
                    segments(t + 1, 1 - s)
                    products(t + 1, 1 - s)
                pe.wait_ge(sf_step, 2 * t + 2)
                pe.wait_ge(y_step, 3 * t + 1)
                for g in range(GROUPS):
                    gs = slice(GH * g, GH * g + GH)
                    mm = pe.matmul(pso[:, gs, :], xb[s][:, SSM_W // P + GROUPS + g, :], Sf[:, gs, :], start=True, stop=True)
                mm.then_inc(off_mm, 1)
                pe.wait_ge(xst_ready, 4 + 2 * t + 2)
                pe.wait_ge(tok_ready, 2 + 2 * t + 2)
                pe.wait_ge(stb_ready, t + 1)
                for ps_, d in ((psf, 0), (pss, 1)):
                    for g in range(GROUPS):
                        gs = slice(GH * g, GH * g + GH)
                        mm = pe.matmul(ps_[:, gs, :], btok[s][:, g, :], xst[s][:, d, gs, :], start=True, stop=True)
                mm.then_inc(st_mm, 1)
                pe.wait_ge(w_ready, 4 + 2 * t + 2)
                pe.wait_ge(xdt_ready, 6 + 3 * t + 3)
                pe.wait_ge(y_step, 3 * t + 2)
                for h in range(HEADS):
                    for d in range(2):
                        mm = pe.matmul(psy[:, h, :], W[s][:, d, h, :], xdt[s][:, d, h, :], start=(d == 0), stop=(d == 1))
                mm.then_inc(y_mm, 1)

            pe.wait_ge(sf_zero, 1)
            to_tokens(0, 0, 0)
            segments(0, 0)
            products(0, 0)
            chunks(pe, body, lambda: pe.wait_ge(sf_zero, 2))

            def body_back(i, ii, s):
                pe.wait_ge(cT_in[s], 16 * ii + 16)
                pe.wait_ge(sb_step, 2 * i + 2)
                pe.wait_ge(yb_step, i + 1)
                for g in range(GROUPS):
                    gs = slice(GH * g, GH * g + GH)
                    mm = pe.matmul(pob[s][:, gs, :], cT[s][:, g, :], Sb[s][:, gs, :], start=True, stop=True)
                mm.then_inc(offb_mm, 1)

            pe.wait_ge(y_step, 3 + 3 * NT)
            pe.wait_ge(sb_zero, 1)
            back(pe, body_back, lambda: pe.wait_ge(sb_zero, 2))

        @block.scalar
        def _(act):
            for sem, n in ((tok_ready, 2), (e_ready, 1), (stb_ready, 1)):
                act.sem_inc(sem, n)
            act.wait_ge(const_in, 80)
            act.activation(alog[:], alog[:], ACT.Exp).then_inc(pre_exp, 1)
            act.wait_ge(pre, 2)
            act.activation(w3[:], w2[:], ACT.Exp, scale=-1.0).then_inc(pre_exp, 1)
            act.wait_ge(sums_mm, 1)
            flat = seg[:].rearrange("p h l -> p (h l)")
            for n in range(2):
                act.activation(ex[:, 3 * n:3 * n + 3, :, :].rearrange("p n t h -> p (n t h)"),
                               flat[:, 512 * n:512 * n + 3 * NT * HEADS], ACT.Exp).then_inc(pre_exp, 1)

            def tokens(t, s):
                act.wait_ge(tok_mm, t + 1)
                act.wait_ge(xdt_ready, 3 * t + 3)
                act.wait_ge(xst_ready, 2 * t + 2)
                act.wait_ge(st_mm, t + 1)
                act.copy(xtok[s][:].rearrange("p h e -> p (h e)"), psx[:]).then_inc(tok_ready, 1)
                act.copy(btok[s][:], psb[:, 0]).then_inc(tok_ready, 1)

            def exponent(t, s):
                act.wait_ge(seg_mm, 2 + t + 1)
                act.wait_ge(w_ready, 2 * t + 2)
                act.activation(E[s][:].rearrange("p g h l -> p (g h) l"), seg[:], ACT.Exp).then_inc(e_ready, 1)

            def body(t, tt, s, ahead):
                if ahead >= 1:
                    tokens(t + 1, 1 - s)
                    exponent(t + 1, 1 - s)
                act.wait_ge(st_mm, 2 + t + 1)
                act.copy(stb[:, bass.ds(t, 1), :, :].rearrange("p t h e -> p (t h) e"), pss[:]).then_inc(stb_ready, 1)

            tokens(0, 0)
            exponent(0, 0)
            chunks(act, body, lambda: None)

        @block.gpsimd
        def _(pool):
            pool.sem_inc(xst_ready, 4)
            pool.wait_ge(const_in, 80)
            pool.wait_ge(tables, 3)

            def sources(t, s):
                pool.wait_ge(seg_mm, t + 1)
                a = dtA[:, bass.ds(t, 1), 0:HEADS].rearrange("p t h -> p (t h)").unsqueeze(2).broadcast_to([P, HEADS, P])
                pool.tensor_tensor(rf[s][:], a, tri[:, LE:LE + 1, :].broadcast_to([P, HEADS, P]), ALU.mult).then_inc(rf_ready, 1)

            def body(t, tt, s, ahead):
                pool.wait_ge(tok_ready, 2 + 2 * t + 1)
                pool.wait_ge(st_mm, t + 1)
                for d in range(2):
                    a = wdt[:, d, bass.ds(t, 1), :].rearrange("p t h -> p (t h)").unsqueeze(2).broadcast_to([P, HEADS, HD])
                    pool.tensor_tensor(xst[s][:, d], xtok[s][:], a, ALU.mult).then_inc(xst_ready, 1)
                if ahead == 2:
                    sources(t + 2, s)

            sources(0, 0)
            sources(1, 1)
            chunks(pool, body, lambda: None)

            def body_back(i, ii, s):
                t = (NT - 1) - i
                pool.wait_ge(yb_step, 2 + i + 1)
                pool.sem_inc(held_pool, 1)
                out = res["y"][:, bass.ds(t, 1), :].rearrange("p t (h e) -> p (t h) e", e=HD)
                pool.tensor_tensor(out, out, yo[s][:], ALU.add).then_inc(yb_add, 1)

            pool.wait_ge(y_step, 3 + 3 * NT)
            back(pool, body_back, lambda: None)
            pool.wait_ge(yb_add, 2 + NT)

        @block.vector
        def _(dve):
            for sem, n in ((cb_ready, 2), (w_ready, 4), (xdt_ready, 6), (y_step, 3), (sf_step, 2), (sb_step, 2), (yb_step, 2), (yb_add, 2)):
                dve.sem_inc(sem, n)
            dve.memset(Sf[:], 0.0).then_inc(sf_zero, 1)
            dve.memset(Sb[0][:], 0.0).then_inc(sb_zero, 1)
            dve.wait_ge(const_in, 80)
            per_tile = [P, NT, NDT]
            dve.tensor_tensor(w1[:], dtr[:], dtb[:].unsqueeze(1).broadcast_to(per_tile), ALU.add).then_inc(pre, 1)
            dve.wait_ge(pre, 1)
            dve.scalar_tensor_tensor(w2[:], w1[:], -1.0, w1[:], ALU.mult, ALU.max).then_inc(pre, 1)
            dve.wait_ge(pre_exp, 2)
            dve.tensor_scalar(w2[:], w3[:], 2.0, None, ALU.add).then_inc(pre, 1)
            dve.wait_ge(pre, 3)
            dve.reciprocal(w2[:], w2[:]).then_inc(pre, 1)
            dve.wait_ge(pre, 4)
            dve.tensor_tensor(w3[:], w3[:], w2[:], ALU.mult).then_inc(pre, 1)
            dve.wait_ge(pre, 5)
            dve.tensor_tensor(w2[:], w3[:], w3[:], ALU.mult).then_inc(pre, 1)
            dve.wait_ge(pre, 6)
            dve.tensor_scalar(w4[:], w2[:], 1.0 / (2 * LOG_TERMS + 1), None, ALU.mult).then_inc(pre, 1)
            for n in range(LOG_TERMS - 1, 0, -1):
                dve.wait_ge(pre, 6 + LOG_TERMS - n)
                dve.scalar_tensor_tensor(w4[:], w4[:], 1.0 / (2 * n + 1), w2[:], ALU.add, ALU.mult).then_inc(pre, 1)
            dve.wait_ge(pre, 6 + LOG_TERMS)
            dve.scalar_tensor_tensor(w4[:], w4[:], 1.0, w3[:], ALU.add, ALU.mult).then_inc(pre, 1)
            dve.tensor_scalar(w1[:], w1[:], 0.0, None, ALU.max).then_inc(pre, 1)
            dve.wait_ge(pre, 8 + LOG_TERMS)
            dve.scalar_tensor_tensor(dt[:], w4[:], 2.0, w1[:], ALU.mult, ALU.add).then_inc(pre, 1)
            dve.wait_ge(pre, 9 + LOG_TERMS)
            dve.scalar_tensor_tensor(dtA[:], dt[:], -1.0, alog[:].unsqueeze(1).broadcast_to(per_tile), ALU.mult, ALU.mult).then_inc(tables, 1)
            dve.wait_ge(pre_exp, 4)
            for d in range(2):
                dve.tensor_tensor(wdt[:, d], dt[:, :, HEADS * d:HEADS * d + HEADS], ex[:, TO_END + d], ALU.mult).then_inc(tables, 1)
            dve.wait_ge(tables, 3)

            def over(a, shape):
                return a.rearrange("p t h -> p (t h)").unsqueeze(2).broadcast_to(shape)

            def sources(t, s):
                dve.wait_ge(seg_mm, t + 1)
                dve.tensor_tensor(rb[s][:], over(dtA[:, bass.ds(t, 1), HEADS:], [P, HEADS, P]),
                                  tri[:, GE:GE + 1, :].broadcast_to([P, HEADS, P]), ALU.mult).then_inc(rb_ready, 1)

            def mask_cb(t, s):
                dve.wait_ge(cb_mm, t + 1)
                dve.wait_ge(w_ready, 2 * t + 2)
                for d, tr in ((0, LE), (1, GE)):
                    dve.tensor_tensor(cb[s][:, d], psb[:, 1], tri[:, tr:tr + 1, :].broadcast_to([P, GROUPS, P]),
                                      ALU.mult).then_inc(cb_ready, 1)

            def body(t, tt, s, ahead):
                dve.wait_ge(e_ready, 1 + t + 1)
                dve.wait_ge(cb_ready, 2 + 2 * t + 2)
                dve.wait_ge(y_mm, t + 1)
                for d in range(2):
                    dve.tensor_tensor(W[s][:, d].rearrange("p (g r) l -> p g r l", g=GROUPS), E[s][:],
                                      cb[s][:, d].unsqueeze(2).broadcast_to([P, GROUPS, GH, P]), ALU.mult).then_inc(w_ready, 1)
                dve.wait_ge(tok_ready, 2 + 2 * t + 1)
                dve.wait_ge(y_step, 3 * t + 3)
                for d in range(3):
                    a = over(dt[:, bass.ds(t, 1), HEADS * d:HEADS * d + HEADS], [P, HEADS, HD]) if d < 2 else \
                        dsk[:].unsqueeze(2).broadcast_to([P, HEADS, HD])
                    dve.tensor_tensor(xdt[s][:, d], xtok[s][:], a, ALU.mult).then_inc(xdt_ready, 1)
                if ahead == 2:
                    sources(t + 2, s)
                if ahead >= 1:
                    mask_cb(t + 1, 1 - s)
                dve.wait_ge(off_mm, 2 + t + 1)
                dve.tensor_tensor(yo[0][:], pso[:], over(ex[:, FROM_START, bass.ds(t, 1), :], [P, HEADS, HD]), ALU.mult).then_inc(y_step, 1)
                dve.wait_ge(sf_step, 2 + 2 * t)
                dve.tensor_tensor(Sf[:], Sf[:], over(ex[:, ALL_F, bass.ds(t, 1), :], [P, HEADS, HD]), ALU.mult).then_inc(sf_step, 1)
                dve.wait_ge(st_mm, 2 + t + 1)
                dve.wait_ge(sf_step, 2 + 2 * t + 1)
                dve.tensor_tensor(Sf[:], Sf[:], psf[:], ALU.add).then_inc(sf_step, 1)
                dve.wait_ge(y_mm, 2 + t + 1)
                dve.wait_ge(y_step, 3 + 3 * t + 1)
                dve.tensor_tensor(yo[0][:], yo[0][:], psy[:], ALU.add).then_inc(y_step, 1)
                dve.wait_ge(y_step, 3 + 3 * t + 2)
                dve.wait_ge(xdt_ready, 6 + 3 * t + 3)
                out = res["y"][:, bass.ds(t, 1), :].rearrange("p t (h e) -> p (t h) e", e=HD)
                dve.tensor_tensor(out, yo[0][:], xdt[s][:, 2], ALU.add).then_inc(y_step, 1)

            def restart():
                dve.wait_ge(sf_step, 2 + 2 * FIRST)
                dve.memset(Sf[:], 0.0).then_inc(sf_zero, 1)
                dve.wait_ge(sf_zero, 2)

            dve.wait_ge(sf_zero, 1)
            sources(0, 0)
            sources(1, 1)
            mask_cb(0, 0)
            chunks(dve, body, restart)

            def body_back(i, ii, s):
                t = (NT - 1) - i
                dve.wait_ge(sb_step, 2 * i + 2)
                dve.wait_ge(offb_mm, 2 + i)
                dve.sem_inc(held_dve, 1)
                dve.tensor_tensor(Sb[1 - s][:], Sb[s][:], over(ex[:, ALL_B, bass.ds(t, 1), :], [P, HEADS, HD]), ALU.mult).then_inc(sb_step, 1)
                dve.wait_ge(sb_step, 2 * i + 3)
                dve.tensor_tensor(Sb[1 - s][:], Sb[1 - s][:], stb[:, bass.ds(t, 1), :, :].rearrange("p t h e -> p (t h) e"), ALU.add).then_inc(sb_step, 1)
                dve.wait_ge(offb_mm, 2 + i + 1)
                dve.wait_ge(yb_add, i + 1)
                dve.tensor_tensor(yo[s][:], pob[s], over(ex[:, FROM_END, bass.ds(t, 1), :], [P, HEADS, HD]), ALU.mult).then_inc(yb_step, 1)

            def restart_back():
                dve.wait_ge(sb_step, 2 + 2 * (NT - FIRST))
                dve.memset(Sb[0][:], 0.0).then_inc(sb_zero, 1)
                dve.wait_ge(sb_zero, 2)

            dve.wait_ge(stb_ready, 1 + NT)
            dve.wait_ge(sb_zero, 1)
            dve.wait_ge(y_step, 3 + 3 * NT)
            back(dve, body_back, restart_back)
            dve.wait_ge(yb_step, 2 + NT)


def stage_mix(nc, dram, res):
    with ExitStack() as ctx:
        m = Mem(nc, ctx, "mix")
        wout = m.sb("wout", [P, KD, D])
        wr = m.sb("wr", [P, KD, EXPERTS])
        normw = m.sb("normw", [P, SSM_W])
        ln = m.sb("ln", [P, 2, D])
        ident = m.sb("ident", [P, P])
        half = m.sb("half", [P, 1])
        xr = [m.sb(f"xr{s}", [P, D]) for s in range(2)]
        mixin = [m.sb(f"mixin{s}", [P, D]) for s in range(2)]
        sq = m.sb("sq", [P, SSM_W])
        ss = m.sb("ss", [P, 2])
        rs = m.sb("rs", [P, 2])
        mT = [m.sb(f"mT{s}", [P, KD, P]) for s in range(2)]
        r = [m.sb(f"r{s}", [P, D]) for s in range(2)]
        stats = m.sb("stats", [P, 2, 6])
        mv = m.sb("mv", [P, 2])
        rstd = m.sb("rstd", [P, 1])
        h = [m.sb(f"h{s}", [P, D]) for s in range(2)]
        ah = [m.sb(f"ah{s}", [P, D]) for s in range(2)]
        hT = m.sb("hT", [P, KD, P])
        nmx = m.sb("nmx", [P, 1])
        er = m.sb("er", [P, EXPERTS])
        den = m.sb("den", [P, 1])
        rden = m.sb("rden", [P, 1])
        aff = m.sb("aff", [P, NT, EXPERTS])
        trA = m.ps("trA", [P, 4, P])
        trB = m.ps("trB", [P, 4, P])
        hrA = m.ps("hrA", [P, 4, P])
        hrB = m.ps("hrB", [P, 4, P])
        po = m.ps("po", [P, D])
        pr = m.ps("pr", [P, 512])

        const_in = m.sem("const_in")
        wout_in = m.sems("wout_in")
        xr_in = m.sems("xr_in")
        x_free = m.sem("x_free")
        half_set = m.sem("half_set")
        held_dve = res["held_dve"]
        held_pool = res["held_pool"]
        gated = m.sem("gated")
        squared = m.sem("squared")
        rs_ready = m.sem("rs_ready")
        rs_tmp = m.sem("rs_tmp")
        mix_att = m.sem("mix_att")
        mix_ssm = m.sem("mix_ssm")
        tr_mm = m.sem("tr_mm")
        mA = m.sem("mA")
        mB = m.sem("mB")
        out_mm = m.sem("out_mm")
        r_ready = m.sem("r_ready")
        ln_step = m.sem("ln_step")
        rstd_tmp = m.sem("rstd_tmp")
        rstd_ready = m.sem("rstd_ready")
        scaled = m.sem("scaled")
        gained = m.sem("gained")
        h_ready = m.sem("h_ready")
        ah_ready = m.sem("ah_ready")
        h_out = m.sem("h_out")
        h_free = m.sem("h_free")
        ht_mm = m.sem("ht_mm")
        hA = m.sem("hA")
        hB = m.sem("hB")
        rt_mm = m.sem("rt_mm")
        nmx_ready = m.sem("nmx_ready")
        er_ready = m.sem("er_ready")
        aff_step = m.sem("aff_step")
        aff_ready = m.sem("aff_ready")
        at_mm = m.sem("at_mm")
        at_done = m.sem("at_done")
        block = ctx.enter_context(nc.Block())

        def tiles(eng, body):
            with eng.Fori(0, NT // 2 - 1) as tt:
                for s in range(2):
                    body(2 * tt + s, tt, s, 2)
            body(NT - 2, NT // 2 - 1, 0, 1)
            body(NT - 1, NT // 2 - 1, 1, 0)

        @block.sync
        def _(sp):
            sp.dma_start(ident[:], dram["ident"]).then_inc(const_in, 16)
            sp.dma_start(normw[:], dram["norm_w"]).then_inc(const_in, 16)
            sp.dma_start(ln[:], dram["ln"][:, 0:2, :]).then_inc(const_in, 16)
            sp.dma_start(wr[:], dram["w_router"].rearrange("(k p) e -> p k e", p=P)).then_inc(const_in, 16)
            for n in range(2):
                cols = slice(512 * n, 512 * n + 512)
                sp.dma_start(wout[:, :, cols], dram["w_out"].rearrange("(k p) n -> p k n", p=P)[:, :, cols]).then_inc(wout_in[n], 16)
            with sp.Fori(0, NT // 2) as tt:
                for s in range(2):
                    t = 2 * tt + s
                    sp.wait_ge(x_free, t + 1)
                    sp.dma_start(xr[s][:], dram["x"][bass.ds(t * P, P), :]).then_inc(xr_in[s], 16)

        @block.tensor
        def _(pe):
            for sem, n in ((tr_mm, 2), (out_mm, 2), (ht_mm, 2), (rt_mm, 1)):
                pe.sem_inc(sem, n)

            def turn(t, s):
                pe.wait_ge(mix_att, t + 1)
                pe.wait_ge(mix_ssm, t + 1)
                pe.wait_ge(mA, t + 1)
                pe.wait_ge(mB, t + 1)
                for j in range(KD):
                    bank = trA if j < 4 else trB
                    mm = pe.transpose(bank[:, j % 4, :], mixin[s][:, P * j:P * j + P], ident[:])
                mm.then_inc(tr_mm, 1)

            def project(t, s, first=False):
                pe.wait_ge(mA, 1 + t + 1)
                pe.wait_ge(mB, 1 + t + 1)
                pe.wait_ge(r_ready, t + 1)
                for n in range(2):
                    if first:
                        pe.wait_ge(wout_in[n], 16)
                    for k in range(KD):
                        mm = pe.matmul(po[:, 512 * n:512 * n + 512], mT[s][:, k, :], wout[:, k, 512 * n:512 * n + 512],
                                       start=(k == 0), stop=(k == KD - 1))
                mm.then_inc(out_mm, 1)

            def body(t, tt, s, ahead):
                if ahead >= 1:
                    project(t + 1, 1 - s)
                pe.wait_ge(h_ready, t + 1)
                pe.wait_ge(hA, t + 1)
                pe.wait_ge(hB, t + 1)
                for j in range(KD):
                    bank = hrA if j < 4 else hrB
                    mm = pe.transpose(bank[:, j % 4, :], h[s][:, P * j:P * j + P], ident[:])
                mm.then_inc(ht_mm, 1)
                if ahead == 2:
                    turn(t + 2, s)
                pe.wait_ge(hA, 1 + t + 1)
                pe.wait_ge(hB, 1 + t + 1)
                pe.wait_ge(aff_ready, t + 1)
                for k in range(KD):
                    mm = pe.matmul(pr[:, 0:EXPERTS], hT[:, k, :], wr[:, k, :], start=(k == 0), stop=(k == KD - 1))
                mm.then_inc(rt_mm, 1)

            pe.wait_ge(const_in, 64)
            turn(0, 0)
            turn(1, 1)
            project(0, 0, first=True)
            tiles(pe, body)
            pe.wait_ge(aff_ready, 1 + NT)
            for t in range(NT):
                bank = (trA, trB, hrA)[t // 4]
                mm = pe.transpose(bank[0:EXPERTS, t % 4, :], aff[:, t, :], ident[:])
            mm.then_inc(at_mm, 1)

        @block.scalar
        def _(act):
            for sem, n in ((squared, 1), (mB, 1), (hB, 1)):
                act.sem_inc(sem, n)

            def inputs(t, s):
                act.wait_ge(tr_mm, t + 1)
                act.copy(mixin[s][:, 0:AW], res["att"][:, bass.ds(t, 1), :].rearrange("p t n -> p (t n)")).then_inc(mix_att, 1)
                act.wait_ge(gated, t + 1)
                act.wait_ge(squared, t + 1)
                act.activation(sq[:], mixin[s][:, AW:], ACT.Square, accum_out=ss[:, s:s + 1]).then_inc(squared, 1)

            def copies(t, s):
                act.wait_ge(tr_mm, 2 + t + 1)
                act.wait_ge(out_mm, t + 1)
                act.copy(mT[s][:, 4:, :], trB[:]).then_inc(mB, 1)

            def body(t, tt, s, ahead):
                if ahead == 2:
                    inputs(t + 2, s)
                act.wait_ge(h_ready, t + 1)
                act.wait_ge(h_free, t + 1)
                act.mul(ah[s][:], h[s][:], ALPHA).then_inc(ah_ready, 1)
                act.wait_ge(ht_mm, 2 + t + 1)
                act.wait_ge(rt_mm, t + 1)
                act.copy(hT[:, 4:, :], hrB[:]).then_inc(hB, 1)
                if ahead == 2:
                    copies(t + 2, s)
                act.wait_ge(nmx_ready, t + 1)
                act.wait_ge(aff_ready, t + 1)
                act.activation(er[:], pr[:, 0:EXPERTS], ACT.Exp, bias=nmx[:], accum_out=den[:]).then_inc(er_ready, 1)

            for s in range(2):
                inputs(s, s)
            for s in range(2):
                copies(s, s)
            tiles(act, body)

        @block.gpsimd
        def _(pool):
            pool.sem_inc(h_free, 2)
            pool.memset(half[:], -0.5).then_inc(half_set, 1)
            pool.wait_ge(half_set, 1)
            pool.wait_ge(const_in, 64)

            def root(t, s):
                pool.wait_ge(squared, 1 + t + 1)
                pool.sem_inc(held_pool, 1)
                pool.tensor_scalar(rs[:, s:s + 1], ss[:, s:s + 1], 1.0 / SSM_W, RMS_EPS, ALU.mult, ALU.add).then_inc(rs_tmp, 1)
                pool.wait_ge(rs_tmp, t + 1)
                pool.tensor_tensor(rs[:, s:s + 1], rs[:, s:s + 1], half[:], ALU.pow).then_inc(rs_ready, 1)

            def body(t, tt, s, ahead):
                pool.wait_ge(ln_step, 3 * t + 3)
                pool.sem_inc(held_pool, 1)
                pool.tensor_scalar(rstd[:], mv[:, 1:2], 1.0, LN_EPS, ALU.mult, ALU.add).then_inc(rstd_tmp, 1)
                pool.wait_ge(rstd_tmp, t + 1)
                pool.tensor_tensor(rstd[:], rstd[:], half[:], ALU.pow).then_inc(rstd_ready, 1)
                pool.wait_ge(scaled, t + 1)
                pool.tensor_tensor(h[s][:], h[s][:], ln[:, 0, :], ALU.mult).then_inc(gained, 1)
                if ahead == 2:
                    root(t + 2, s)
                pool.wait_ge(h_ready, t + 1)
                pool.sem_inc(held_pool, 1)
                pool.dma_start(dram["h"][bass.ds(t * P, P), :], h[s][:]).then_inc(h_out, 16)
                pool.wait_ge(ah_ready, t + 1)
                pool.sem_inc(held_pool, 1)
                pool.dma_start(dram["acc"][bass.ds(t * P, P), :], ah[s][:]).then_inc(h_out, 16)
                pool.wait_ge(h_out, 32 * t + 32)
                pool.sem_inc(h_free, 1)

            for s in range(2):
                root(s, s)
            tiles(pool, body)

        @block.vector
        def _(dve):
            for sem, n in ((mA, 1), (hA, 1), (r_ready, 1), (aff_ready, 1), (x_free, 2)):
                dve.sem_inc(sem, n)

            def gate(t, s):
                dve.wait_ge(tr_mm, t + 1)
                dve.tensor_tensor(mixin[s][:, AW:], res["y"][:, bass.ds(t, 1), :].rearrange("p t n -> p (t n)"),
                                  res["z"][:, bass.ds(t, 1), :].rearrange("p t n -> p (t n)"), ALU.mult).then_inc(gated, 1)

            def norm(t, s):
                dve.wait_ge(rs_ready, t + 1)
                dve.wait_ge(squared, 1 + t + 1)
                dve.scalar_tensor_tensor(mixin[s][:, AW:], mixin[s][:, AW:], rs[:, s:s + 1], normw[:], ALU.mult, ALU.mult).then_inc(mix_ssm, 1)

            def copies(t, s):
                dve.wait_ge(tr_mm, 2 + t + 1)
                dve.wait_ge(out_mm, t + 1)
                dve.tensor_copy(mT[s][:, 0:4, :], trA[:]).then_inc(mA, 1)

            def residual(t, tt, s):
                dve.wait_ge(out_mm, 2 + t + 1)
                dve.wait_ge(xr_in[s], 16 * tt + 16)
                dve.scalar_tensor_tensor(r[s][:], xr[s][:], ALPHA, po[:], ALU.mult, ALU.add).then_inc(r_ready, 1)

            def body(t, tt, s, ahead):
                dve.wait_ge(r_ready, 1 + t + 1)
                dve.sem_inc(x_free, 1)
                dve.bn_stats(stats[:, 0], r[s][:, 0:512]).then_inc(ln_step, 1)
                dve.bn_stats(stats[:, 1], r[s][:, 512:]).then_inc(ln_step, 1)
                dve.wait_ge(ln_step, 3 * t + 2)
                dve.sem_inc(held_dve, 1)
                dve.bn_aggr(mv[:], stats[:]).then_inc(ln_step, 1)
                if ahead == 2:
                    gate(t + 2, s)
                dve.wait_ge(rstd_ready, t + 1)
                dve.wait_ge(h_free, t + 1)
                dve.wait_ge(ht_mm, t + 1)
                dve.wait_ge(ln_step, 3 * t + 3)
                dve.tensor_scalar(h[s][:], r[s][:], mv[:, 0:1], rstd[:], ALU.subtract, ALU.mult).then_inc(scaled, 1)
                dve.wait_ge(gained, t + 1)
                dve.tensor_tensor(h[s][:], h[s][:], ln[:, 1, :], ALU.add).then_inc(h_ready, 1)
                if ahead == 2:
                    norm(t + 2, s)
                if ahead >= 1:
                    residual(t + 1, tt + s, 1 - s)
                dve.wait_ge(ht_mm, 2 + t + 1)
                dve.wait_ge(rt_mm, t + 1)
                dve.tensor_copy(hT[:, 0:4, :], hrA[:]).then_inc(hA, 1)
                if ahead == 2:
                    copies(t + 2, s)
                dve.wait_ge(rt_mm, 1 + t + 1)
                dve.tensor_reduce(nmx[:], pr[:, 0:EXPERTS], mybir.AxisListType.X, ALU.max, negate=True).then_inc(nmx_ready, 1)
                dve.wait_ge(er_ready, t + 1)
                dve.reciprocal(rden[:], den[:]).then_inc(aff_step, 1)
                dve.wait_ge(aff_step, t + 1)
                dve.tensor_scalar(aff[:, bass.ds(t, 1), :], er[:].unsqueeze(1), rden[:], None, ALU.mult).then_inc(aff_ready, 1)

            dve.wait_ge(const_in, 64)
            for s in range(2):
                gate(s, s)
            for s in range(2):
                norm(s, s)
            for s in range(2):
                copies(s, s)
            residual(0, 0, 0)
            tiles(dve, body)
            dve.wait_ge(at_mm, 1)
            for b, bank in enumerate((trA, trB, hrA)):
                dve.tensor_copy(res["affT"][:, 512 * b:512 * b + 512], bank[0:EXPERTS].rearrange("e j t -> e (j t)")).then_inc(at_done, 1)
            dve.wait_ge(at_done, 3)


def stage_choose(nc, dram, res):
    with ExitStack() as ctx:
        m = Mem(nc, ctx, "top")
        ident = m.sb("ident", [P, P])
        val = m.sb("val", [EXPERTS, CAP])
        idx = m.sb("idx", [EXPERTS, CAP], U32)
        idxf = m.sb("idxf", [EXPERTS, CAP])
        ps = m.ps("ps", [P, 4, EXPERTS])
        const_in = m.sem("const_in")
        step = m.sem("step")
        float_ready = m.sem("float_ready")
        tr_mm = m.sem("tr_mm")
        done = m.sem("done")
        block = ctx.enter_context(nc.Block())
        parts = ((1, 0, CAPS[1]), (0, CAPS[1], CAPS[0]))

        @block.sync
        def _(sp):
            sp.dma_start(ident[:], dram["ident"]).then_inc(const_in, 16)

        @block.vector
        def _(dve):
            n = 0
            for q, c0, cap in parts:
                work = res["affT"][:, sum(SEQS[:q]):sum(SEQS[:q]) + SEQS[q]]
                for r in range(cap // 8):
                    at = slice(c0 + 8 * r, c0 + 8 * r + 8)
                    dve.max(val[:, at], work).then_inc(step, 1)
                    dve.wait_ge(step, n + 1)
                    dve.max_index(idx[:, at], val[:, at], work).then_inc(step, 1)
                    dve.wait_ge(step, n + 2)
                    dve.match_replace(work, val[:, at], work, -1.0).then_inc(step, 1)
                    dve.wait_ge(step, n + 3)
                    n += 3
            dve.tensor_scalar(idxf[:, 0:CAPS[1]], idx[:, 0:CAPS[1]], float(SEQS[0]), None, ALU.add).then_inc(float_ready, 1)
            dve.tensor_copy(idxf[:, CAPS[1]:], idx[:, CAPS[1]:]).then_inc(float_ready, 1)
            dve.wait_ge(tr_mm, 1)
            for i, (q, c0, cap) in enumerate(parts):
                dve.tensor_copy(res["gates"][i][:], ps[0:cap, 2 * i, :]).then_inc(done, 1)
                dve.tensor_copy(res["rows"][i][:], ps[0:cap, 2 * i + 1, :]).then_inc(done, 1)
            dve.wait_ge(done, 4)

        @block.tensor
        def _(pe):
            pe.wait_ge(const_in, 16)
            pe.wait_ge(float_ready, 2)
            for i, (q, c0, cap) in enumerate(parts):
                pe.transpose(ps[0:cap, 2 * i, :], val[:, c0:c0 + cap], ident[0:EXPERTS, 0:EXPERTS])
                mm = pe.transpose(ps[0:cap, 2 * i + 1, :], idxf[:, c0:c0 + cap], ident[0:EXPERTS, 0:EXPERTS])
            mm.then_inc(tr_mm, 1)


def stage_experts(nc, dram, res):
    NS, NP_ = CAPS[1], CAPS[0]
    HALF = FCH // 2
    STEPS = FCH + KD
    GR = 2 * STEPS
    PAIRS = FCH // 2
    with ExitStack() as ctx:
        m = Mem(nc, ctx, "moe")
        raw = [m.sb(f"raw{c}", [P, HALF, P]) for c in range(4)]
        whi = [m.sb(f"whi{c}", [P, HALF, P], F32R) for c in range(4)]
        wlo = [m.sb(f"wlo{c}", [P, HALF, P], F32R) for c in range(4)]
        ident = m.sb("ident", [P, P])
        grow = [m.sb("grow_s", [NS, 1], U32), m.sb("grow_p", [NP_, 1], U32)]
        srow = [m.sb("srow_s", [NS, 1], U32), m.sb("srow_p", [NP_, 1], U32)]
        xg = [m.sb("xg_s", [NS, D]), m.sb("xg_p", [NP_, D])]
        xgT = [m.sb(f"xgT{q}", [P, KD, 2 * CAP], F32R) for q in range(2)]
        part = [m.sb(f"part{s}", [P, 2, CAP]) for s in range(2)]
        guv = [m.sb(f"guv{s}", [P, 2, CAP]) for s in range(2)]
        prod = [m.sb(f"prod{s}", [P, CAP]) for s in range(2)]
        hid = m.sb("hid", [P, FCH, 2 * CAP], F32R)
        dpart = [m.sb(f"dpart{s}", [P, CAP]) for s in range(2)]
        oT = m.sb("oT", [P, KD, CAP])
        og = [m.sb("og_s", [NS, D]), m.sb("og_p", [NP_, D])]
        gu = [m.ps(f"gu{s}", [P, 2, 512]) for s in range(2)]
        dn = [m.ps(f"dn{s}", [P, 512]) for s in range(2)]
        tr = [m.ps(f"tr{b}", [P, 512]) for b in range(2)]

        const_in = m.sem("const_in")
        raw_in = m.sems("raw_in", 4)
        hi_done = m.sem("hi_done")
        lo_done = m.sem("lo_done")
        gran_mm = m.sem("gran_mm")
        part_out = m.sem("part_out")
        summed = m.sem("summed")
        silu = m.sem("silu")
        prod_ready = m.sem("prod_ready")
        hid_hi = m.sem("hid_hi")
        hid_lo = m.sem("hid_lo")
        dpart_out = m.sem("dpart_out")
        dsummed = m.sem("dsummed")
        grow_ready = m.sem("grow_ready")
        xg_in = m.sem("xg_in")
        tok_fill = m.sem("tok_fill")
        tok_hi = m.sem("tok_hi")
        tok_done = m.sem("tok_done")
        row_fill = m.sem("row_fill")
        held_act = res["held_act"]
        row_done = m.sem("row_done")
        srow_ready = m.sem("srow_ready")
        scat_out = m.sem("scat_out")
        scat_free = m.sem("scat_free")
        held_pe = res["held_pe"]
        held_pool = res["held_pool"]
        block = ctx.enter_context(nc.Block())

        def experts(eng, body):
            body(0, 0, True, False)
            with eng.Fori(0, EXPERTS // 2 - 1) as ee:
                for q in range(2):
                    body(2 * ee + 1 + q, 1 - q, False, False)
            body(EXPERTS - 1, 1, False, True)

        @block.sync
        def _(sp):
            sp.dma_start(ident[:], dram["ident"]).then_inc(const_in, 16)
            with sp.Fori(0, EXPERTS) as e:
                with sp.Fori(0, PAIRS) as mm:
                    for c in range(4):
                        sp.wait_ge(lo_done, GR * e + 4 * mm + c + 1)
                        sp.dma_start(raw[c][:, 0:KD, :].rearrange("p k n -> p (k n)"),
                                     dram["w_gu"][bass.ds(2 * FCH * e + 4 * mm + c, 1), :, :].rearrange("u p n -> p (u n)")).then_inc(raw_in[c], 16)
                with sp.Fori(0, KD // 2) as mm:
                    for c in range(4):
                        sp.wait_ge(lo_done, GR * e + 2 * FCH + 4 * mm + c + 1)
                        sp.dma_start(raw[c][:].rearrange("p k n -> p (k n)"),
                                     dram["w_dn"][bass.ds(2 * KD * e + 4 * mm + c, 1), :, :].rearrange("u p n -> p (u n)")).then_inc(raw_in[c], 16)

        @block.gpsimd
        def _(pool):
            pool.sem_inc(scat_free, 1)

            def gather(e):
                for i in range(2):
                    pool.tensor_copy(grow[i][:], res["rows"][i][:, bass.ds(e, 1)]).then_inc(grow_ready, 1)
                pool.wait_ge(grow_ready, 2 * e + 2)
                pool.sem_inc(held_pool, 1)
                for i in range(2):
                    pool.indirect_dma_start(xg[i][:], None, dram["h"], bass.IndirectOffsetOnAxis(ap=grow[i][:], axis=0)).then_inc(xg_in, 16)

            def scatter(e):
                for i in range(2):
                    pool.tensor_copy(srow[i][:], res["rows"][i][:, bass.ds(e, 1)]).then_inc(srow_ready, 1)
                pool.wait_ge(srow_ready, 2 * e + 2)
                pool.wait_ge(row_done, 8 + 4 * e + 4)
                pool.sem_inc(held_pool, 1)
                for i in range(2):
                    pool.indirect_dma_start(dram["acc"], bass.IndirectOffsetOnAxis(ap=srow[i][:], axis=0), og[i][:], None,
                                            compute_op=ALU.add).then_inc(scat_out, 16)
                pool.wait_ge(scat_out, 32 * e + 32)
                pool.sem_inc(scat_free, 1)

            gather(0)
            pool.wait_ge(tok_fill, 4)
            gather(1)
            pool.wait_ge(tok_fill, 8)
            gather(2)
            with pool.Fori(0, EXPERTS - 3) as e:
                scatter(e)
                pool.wait_ge(tok_fill, 4 * e + 12)
                gather(e + 3)
            for e in range(EXPERTS - 3, EXPERTS):
                scatter(e)

        @block.tensor
        def _(pe):
            def fill_tokens(e, b):
                for j in range(2):
                    k = 2 * b + j
                    pe.transpose(tr[b % 2][:, CAP * j:CAP * j + NS], xg[0][:, P * k:P * k + P], ident[:])
                    mm = pe.transpose(tr[b % 2][:, CAP * j + NS:CAP * j + CAP], xg[1][:, P * k:P * k + P], ident[0:NP_, 0:NP_])
                mm.then_inc(tok_fill, 1)

            def fill_rows(b):
                pe.sem_inc(held_pe, 1)
                lo, hi = (0, NS) if b < 2 else (NS, CAP)
                for j in range(4):
                    mm = pe.transpose(tr[b % 2][0:hi - lo, P * j:P * j + P], oT[:, 4 * (b % 2) + j, lo:hi], ident[:])
                mm.then_inc(row_fill, 1)

            def product(out, c, i, x, start, stop):
                pe.matmul(out[:, 0:2 * CAP], whi[c][:, i, :], x, start=start, stop=False)
                return pe.matmul(out[:, 0:CAP], wlo[c][:, i, :], x[:, 0:CAP], start=False, stop=stop)

            def gate_up(e, k, s, q):
                pe.wait_ge(summed, FCH * e + k + 1)
                for a in range(2):
                    pe.wait_ge(lo_done, 4 + GR * e + 2 * k + a + 1)
                    for i in range(KD):
                        mm = product(gu[s][:, a, :], 2 * s + a, i, xgT[q][:, i, :], i == 0, i == KD - 1)
                    mm.then_inc(gran_mm, 1)

            def down(e, j, s):
                pe.wait_ge(dsummed, KD * e + j + 1)
                for a in range(2):
                    pe.wait_ge(hid_lo, FCH * e + HALF * (a + 1))
                    pe.wait_ge(lo_done, 4 + GR * e + 2 * FCH + 2 * j + a + 1)
                    for i in range(HALF):
                        mm = product(dn[s][:], 2 * s + a, i, hid[:, HALF * a + i, :], a == 0 and i == 0, a == 1 and i == HALF - 1)
                    mm.then_inc(gran_mm, 1)

            def body(e, q, first, last):
                pe.wait_ge(tok_done, 4 * e + 4)
                gate_up(e, 0, 0, q)
                if not last:
                    pe.wait_ge(xg_in, 32 * e + 64)
                    pe.wait_ge(row_done, 4 * e + 3)
                    fill_tokens(e + 1, 0)
                    pe.wait_ge(row_done, 4 * e + 4)
                    fill_tokens(e + 1, 1)
                gate_up(e, 1, 1, q)
                if not last:
                    pe.wait_ge(tok_done, 4 * e + 5)
                    fill_tokens(e + 1, 2)
                    pe.wait_ge(tok_done, 4 * e + 6)
                    fill_tokens(e + 1, 3)
                gate_up(e, 2, 0, q)
                if not first:
                    pe.wait_ge(dsummed, 2 + KD * e)
                    if last:
                        pe.wait_ge(row_done, 4 * e + 4)
                    else:
                        pe.wait_ge(tok_done, 4 * e + 8)
                    fill_rows(0)
                    fill_rows(1)
                gate_up(e, 3, 1, q)
                if not first:
                    pe.wait_ge(row_done, 4 * e + 5)
                    fill_rows(2)
                    pe.wait_ge(row_done, 4 * e + 6)
                    fill_rows(3)
                with pe.Fori(2, PAIRS) as mm:
                    for s in range(2):
                        gate_up(e, 2 * mm + s, s, q)
                with pe.Fori(0, KD // 2) as mm:
                    for s in range(2):
                        down(e, 2 * mm + s, s)

            pe.wait_ge(const_in, 16)
            pe.wait_ge(xg_in, 32)
            for b in range(4):
                if b >= 2:
                    pe.wait_ge(tok_done, b - 1)
                fill_tokens(0, b)
            experts(pe, body)
            pe.wait_ge(dsummed, 2 + KD * EXPERTS)
            for b in range(4):
                pe.wait_ge(row_done, 4 * EXPERTS + 3 + b)
                fill_rows(b)

        def splitters(eng, body_part, tokens, rows, first_parts):

            def body(e, q, first, last):
                for k in range(4):
                    body_part(e, k, 0 if k < 2 else 1, k % 2, (e, k + 2, k // 2 + 1, KD))
                    if k < 2 and not last:
                        tokens(e + 1, 1 - q, 2 * k)
                        tokens(e + 1, 1 - q, 2 * k + 1)
                    if k >= 2 and not first:
                        rows(e - 1, 2 * k - 4)
                        rows(e - 1, 2 * k - 3)
                with eng.Fori(2, PAIRS - 1) as mm:
                    for s in range(2):
                        body_part(e, 2 * mm + s, mm, s, (e, 2 * mm + s + 2, mm + 1, KD))
                for s in range(2):
                    body_part(e, FCH - 2 + s, PAIRS - 1, s, (e, FCH + s, PAIRS, HALF))
                with eng.Fori(0, KD // 2 - 1) as mm:
                    for s in range(2):
                        body_part(e, FCH + 2 * mm + s, PAIRS + mm, s, (e, FCH + 2 * mm + s + 2, PAIRS + mm + 1, HALF), 2 * mm + s)
                for s in range(2):
                    j = KD - 2 + s
                    body_part(e, FCH + j, PAIRS + KD // 2 - 1, s, None if last else (e + 1, s, 0, KD), j)

            for b in range(4):
                tokens(0, 0, b)
            for s in range(2):
                for a in range(2):
                    first_parts(s, a)
            experts(eng, body)
            for b in range(4):
                rows(EXPERTS - 1, b)

        @block.scalar
        def _(act):
            act.sem_inc(row_done, 8)

            def split(e, k, mm, s, a, tiles):
                c = 2 * s + a
                act.wait_ge(raw_in[c], 16 * (GR // 4 * e + mm + 1))
                act.copy(whi[c][:, 0:tiles, :], raw[c][:, 0:tiles, :]).then_inc(hi_done, 1)

            def part_(e, k, mm, s, nxt, j=None):
                n = GR * e + 2 * k
                act.wait_ge(gran_mm, n + 2)
                if j is None:
                    f = FCH * e + k
                    act.wait_ge(summed, f + 1)
                    act.copy(part[s][:], gu[s][:, :, CAP:2 * CAP]).then_inc(part_out, 1)
                else:
                    act.wait_ge(dsummed, KD * e + j + 1)
                    act.copy(dpart[s][:], dn[s][:, CAP:2 * CAP]).then_inc(dpart_out, 1)
                late = isinstance(k, int) and FCH - 2 <= k < FCH
                if nxt and not late:
                    split(*nxt[:3], s, 0, nxt[3])
                if j is None:
                    act.wait_ge(summed, 2 + f + 1)
                    act.activation(guv[s][:, 0, :], guv[s][:, 0, :], ACT.Silu).then_inc(silu, 1)
                if nxt and not late:
                    split(*nxt[:3], s, 1, nxt[3])
                if j is None:
                    act.wait_ge(prod_ready, f + 1)
                    act.copy(hid[:, bass.ds(k, 1), 0:CAP], prod[s][:].unsqueeze(1)).then_inc(hid_hi, 1)
                if nxt and late:
                    for a in range(2):
                        split(*nxt[:3], s, a, nxt[3])

            def tokens(e, q, b):
                act.wait_ge(tok_fill, 4 * e + b + 1)
                act.copy(xgT[q][:, 2 * b:2 * b + 2, 0:CAP], tr[b % 2][:, 0:2 * CAP].rearrange("p (j c) -> p j c", j=2)).then_inc(tok_hi, 1)

            def rows(e, b):
                i = b // 2
                if b == 0:
                    act.wait_ge(scat_free, e + 1)
                act.wait_ge(row_fill, 4 * e + b + 1)
                act.sem_inc(held_act, 1)
                act.mul(og[i][:, 512 * (b % 2):512 * (b % 2) + 512], tr[b % 2][0:CAPS[1 - i], :],
                        res["gates"][i][:, bass.ds(e, 1)]).then_inc(row_done, 1)

            splitters(act, part_, tokens, rows, lambda s, a: split(0, s, 0, s, a, KD))

        @block.vector
        def _(dve):
            for sem, n in ((lo_done, 4), (summed, 2), (dsummed, 2)):
                dve.sem_inc(sem, n)

            def split(e, k, mm, s, a, tiles):
                c = 2 * s + a
                dve.wait_ge(hi_done, GR * e + 2 * k + a + 1)
                dve.tensor_tensor(wlo[c][:, 0:tiles, :], raw[c][:, 0:tiles, :], whi[c][:, 0:tiles, :].bitcast(F32),
                                  ALU.subtract).then_inc(lo_done, 1)

            def part_(e, k, mm, s, nxt, j=None):
                if j is None:
                    f = FCH * e + k
                    dve.wait_ge(part_out, f + 1)
                    dve.tensor_tensor(guv[s][:], gu[s][:, :, 0:CAP], part[s][:], ALU.add).then_inc(summed, 1)
                else:
                    if not isinstance(e, int) or e > 0:
                        dve.wait_ge(row_fill, 4 * e)
                    dve.wait_ge(dpart_out, KD * e + j + 1)
                    out = oT[:, bass.ds(j, 1), :].rearrange("p j c -> p (j c)")
                    dve.tensor_tensor(out, dn[s][:, 0:CAP], dpart[s][:], ALU.add).then_inc(dsummed, 1)
                late = isinstance(k, int) and FCH - 2 <= k < FCH
                if nxt and not late:
                    split(*nxt[:3], s, 0, nxt[3])
                if j is None:
                    dve.wait_ge(silu, f + 1)
                    dve.tensor_tensor(prod[s][:], guv[s][:, 0, :], guv[s][:, 1, :], ALU.mult).then_inc(prod_ready, 1)
                if nxt and not late:
                    split(*nxt[:3], s, 1, nxt[3])
                if j is None:
                    dve.wait_ge(hid_hi, f + 1)
                    ks = bass.ds(k, 1)
                    dve.tensor_tensor(hid[:, ks, CAP:2 * CAP], prod[s][:].unsqueeze(1), hid[:, ks, 0:CAP].bitcast(F32),
                                      ALU.subtract).then_inc(hid_lo, 1)
                if nxt and late:
                    for a in range(2):
                        split(*nxt[:3], s, a, nxt[3])

            def tokens(e, q, b):
                dve.wait_ge(tok_hi, 4 * e + b + 1)
                dve.tensor_tensor(xgT[q][:, 2 * b:2 * b + 2, CAP:2 * CAP], tr[b % 2][:, 0:2 * CAP].rearrange("p (j c) -> p j c", j=2),
                                  xgT[q][:, 2 * b:2 * b + 2, 0:CAP].bitcast(F32), ALU.subtract).then_inc(tok_done, 1)

            splitters(dve, part_, tokens, lambda e, b: None, lambda s, a: split(0, s, 0, s, a, KD))


def stage_finish(nc, dram, res):
    with ExitStack() as ctx:
        m = Mem(nc, ctx, "fin")
        ln = m.sb("ln", [P, 2, D])
        half = m.sb("half", [P, 1])
        r = m.sb("r", [P, NT, D])
        stats = [m.sb(f"stats{s}", [P, 2, 6]) for s in range(2)]
        mv = [m.sb(f"mv{s}", [P, 2]) for s in range(2)]
        rstd = [m.sb(f"rstd{s}", [P, 1]) for s in range(2)]
        const_in = m.sem("const_in")
        half_set = m.sem("half_set")
        held_dve = res["held_dve"]
        held_pool = res["held_pool"]
        r_in = m.sems("r_in")
        ln_step = m.sem("ln_step")
        rstd_tmp = m.sem("rstd_tmp")
        rstd_ready = m.sem("rstd_ready")
        scaled = m.sem("scaled")
        gained = m.sem("gained")
        o_ready = m.sem("o_ready")
        o_out = m.sem("o_out")
        block = ctx.enter_context(nc.Block())

        def row(t, cols=slice(0, D)):
            return r[:, bass.ds(t, 1), cols].rearrange("p t n -> p (t n)")

        @block.sync
        def _(sp):
            for s in range(2):
                sp.dma_start(row(s), dram["acc"][P * s:P * s + P, :]).then_inc(r_in[s], 16)
            sp.dma_start(ln[:], dram["ln"][:, 2:4, :]).then_inc(const_in, 16)
            with sp.Fori(1, NT // 2) as tt:
                for s in range(2):
                    t = 2 * tt + s
                    sp.wait_ge(r_in[s], 16 * tt)
                    sp.dma_start(row(t), dram["acc"][bass.ds(t * P, P), :]).then_inc(r_in[s], 16)

        @block.scalar
        def _(act):
            with act.Fori(0, NT) as t:
                act.wait_ge(o_ready, t + 1)
                act.dma_start(dram["out"][bass.ds(t * P, P), :], row(t)).then_inc(o_out, 16)
            act.wait_ge(o_out, 16 * NT)

        @block.gpsimd
        def _(pool):
            pool.memset(half[:], -0.5).then_inc(half_set, 1)
            pool.wait_ge(half_set, 1)

            def root(t, s):
                pool.wait_ge(ln_step, 3 * t + 3)
                pool.sem_inc(held_pool, 1)
                pool.tensor_scalar(rstd[s][:], mv[s][:, 1:2], 1.0, LN_EPS, ALU.mult, ALU.add).then_inc(rstd_tmp, 1)
                pool.wait_ge(rstd_tmp, t + 1)
                pool.tensor_tensor(rstd[s][:], rstd[s][:], half[:], ALU.pow).then_inc(rstd_ready, 1)

            def gain(t):
                pool.wait_ge(scaled, t + 1)
                pool.tensor_tensor(row(t), row(t), ln[:, 0, :], ALU.mult).then_inc(gained, 1)

            root(0, 0)
            pool.wait_ge(const_in, 16)
            with pool.Fori(0, NT // 2 - 1) as tt:
                for s in range(2):
                    t = 2 * tt + s
                    root(t + 1, 1 - s)
                    gain(t)
            root(NT - 1, 1)
            gain(NT - 2)
            gain(NT - 1)

        @block.vector
        def _(dve):
            def measure(t, tt, s):
                dve.wait_ge(r_in[s], 16 * tt + 16)
                dve.bn_stats(stats[s][:, 0], row(t, slice(0, 512))).then_inc(ln_step, 1)
                dve.bn_stats(stats[s][:, 1], row(t, slice(512, D))).then_inc(ln_step, 1)
                dve.wait_ge(ln_step, 3 * t + 2)
                dve.sem_inc(held_dve, 1)
                dve.bn_aggr(mv[s][:], stats[s][:]).then_inc(ln_step, 1)

            def scale(t, s):
                dve.wait_ge(rstd_ready, t + 1)
                dve.wait_ge(ln_step, 3 * t + 3)
                dve.tensor_scalar(row(t), row(t), mv[s][:, 0:1], rstd[s][:], ALU.subtract, ALU.mult).then_inc(scaled, 1)

            def shift(t):
                dve.wait_ge(gained, t + 1)
                dve.tensor_tensor(row(t), row(t), ln[:, 1, :], ALU.add).then_inc(o_ready, 1)

            measure(0, 0, 0)
            measure(1, 0, 1)
            scale(0, 0)
            with dve.Fori(0, NT // 2 - 1) as tt:
                for s in range(2):
                    t = 2 * tt + s
                    measure(t + 2, tt + 1, s)
                    scale(t + 1, 1 - s)
                    shift(t)
            scale(NT - 1, 1)
            shift(NT - 2)
            shift(NT - 1)


def residents_held(nc, ctx):
    return {f"held_{e}": ctx.enter_context(nc.semaphore(f"held_{e}")) for e in ("sp", "act", "dve", "pool", "pe")}


def residents_first(nc, ctx):
    m = Mem(nc, ctx, "res")
    return {
        "z": m.sb("z", [P, NT, 512]),
        "dt": m.sb("dt", [P, NT, NDT]),
    }


def residents_router(nc, ctx):
    m = Mem(nc, ctx, "rtr")
    return {
        "gates": [m.sb("gates_s", [CAPS[1], EXPERTS]), m.sb("gates_p", [CAPS[0], EXPERTS])],
        "rows": [m.sb("rows_s", [CAPS[1], EXPERTS], U32), m.sb("rows_p", [CAPS[0], EXPERTS], U32)],
    }


def residents_later(nc, ctx):
    m = Mem(nc, ctx, "res")
    return {
        "affT": m.sb("affT", [EXPERTS, TOK]),
        "att": m.sb("att", [P, NT, AW]),
        "y": m.sb("y", [P, NT, SSM_W]),
    }


def layouts(x_prompt, x_sample, w_in, conv_w, conv_b, dt_bias, a_log, d_skip, ssm_norm_w, w_out,
            ln1_g, ln1_b, w_router, w_gate, w_up, w_down, ln2_g, ln2_b):
    a = {}
    x = np.concatenate([np.asarray(x_prompt)[0], np.asarray(x_sample)[0]], axis=0)
    a["x"] = np.ascontiguousarray(x)
    a["xT"] = np.ascontiguousarray(x.T)
    a["w_in"] = np.asarray(w_in)[0]
    taps = np.concatenate([np.asarray(conv_w)[0], np.asarray(conv_b)[0][None]], axis=0)
    a["conv"] = np.ascontiguousarray(taps.T.reshape(NCH, P, CONV_K + 1).transpose(1, 0, 2))
    rows = lambda v: np.ascontiguousarray(np.broadcast_to(np.asarray(v).reshape(1, -1), (P, np.asarray(v).size)))
    a["dt_bias"] = rows(dt_bias)
    a["a_log"] = rows(a_log)
    a["d_skip"] = rows(d_skip)
    a["norm_w"] = rows(ssm_norm_w)
    a["ln"] = np.ascontiguousarray(np.stack([rows(ln1_g), rows(ln1_b), rows(ln2_g), rows(ln2_b)], axis=1))
    a["w_out"] = np.asarray(w_out)[0]
    a["w_router"] = np.asarray(w_router)[0]
    gu = np.stack([np.asarray(w_gate)[0], np.asarray(w_up)[0]])
    gu = gu.reshape(2, EXPERTS, KD, P, FCH, P).transpose(1, 4, 0, 3, 2, 5)
    a["w_gu"] = np.ascontiguousarray(gu).reshape(EXPERTS * FCH * 2, P, KD * P)
    dn = np.asarray(w_down)[0].reshape(EXPERTS, 2, FCH // 2, P, KD, P).transpose(0, 4, 1, 3, 2, 5)
    a["w_dn"] = np.ascontiguousarray(dn).reshape(EXPERTS * KD * 2, P, FCH // 2 * P)
    pos = np.concatenate([np.arange(s) for s in SEQS]).astype(np.float32)
    inv = np.float32(500000.0) ** (-np.arange(HALF_ROT, dtype=np.float32) * np.float32(2.0) / np.float32(ROT))
    ang = (pos[:, None] * inv.astype(np.float32)[None, :]).astype(np.float32)
    cs = np.stack([np.cos(ang), np.sin(ang)], axis=1).astype(np.float32)
    a["rope"] = np.ascontiguousarray(cs.reshape(NT, P, 2, HALF_ROT).transpose(1, 0, 2, 3))
    delta = np.abs(np.arange(MASK_W)[None, :] - MASK_0 - np.arange(P)[:, None])
    times = sum(((delta % dil == 0) & (delta <= window // 2)).astype(np.float64) for window, dil in PATTERNS)
    a["mask"] = np.where(times > 0, np.log(np.maximum(times, 1)), NEG).astype(np.float32)
    i = np.arange(P)
    lt, le = i[:, None] < i[None, :], i[:, None] <= i[None, :]
    a["tri"] = np.ascontiguousarray(np.stack([lt, le, lt.T, le.T, lt | lt.T | le], axis=1).astype(np.float32))
    a["ident"] = np.eye(P, dtype=np.float32)
    return a


def build(nc, dram):
    with ExitStack() as ctx:
        held = residents_held(nc, ctx)
        router = dict(residents_router(nc, ctx), **held)
        with ExitStack() as mixer:
            res = dict(residents_first(nc, mixer), **held)
            stage_project(nc, dram, res)
            res.update(residents_later(nc, mixer), **router)
            stage_attend(nc, dram, res)
            stage_ssd(nc, dram, res)
            stage_mix(nc, dram, res)
            stage_choose(nc, dram, res)
        stage_experts(nc, dram, router)
        stage_finish(nc, dram, res)


def kernel(**inputs):
    import concourse.bacc as bacc
    from concourse.bass_utils import run_bass_kernel_spmd

    nc = bacc.Bacc("TRN2", target_bir_lowering=False, num_devices=1)
    arrays = layouts(**inputs)
    dram = {name: nc.dram_tensor(f"in_{name}", a.shape, mybir.dt.from_np(a.dtype), kind="ExternalInput").ap()
            for name, a in arrays.items()}
    scratch = {"v": [TOK, AW], "qkT": [2 * AW, TOK], "xbc": [CONV_CH, TOK], "h": [TOK, D], "acc": [TOK, D]}
    for name, shape in scratch.items():
        dram[name] = nc.dram_tensor(f"tmp_{name}", shape, F32, kind="Internal").ap()
    dram["out"] = nc.dram_tensor("out", [TOK, D], F32, kind="ExternalOutput").ap()
    build(nc, dram)
    r = run_bass_kernel_spmd(nc, [{f"in_{k}": v for k, v in arrays.items()}], core_ids=[0])
    out = np.asarray(r.results[0]["out"])
    return out[None, :SEQS[0]], out[None, SEQS[0]:]
```
